# Optimizing a Trainium2 kernel written in Bass

```python
import math
import jax
import jax.numpy as jnp
from jax import lax
import numpy as np

D_MODEL = 1024
BATCH = 1
SEQ = 512
DEPTH = 2
DEC_BATCH = 8
DEC_SEQ = 1
PAST_LEN = 1024
PAGE_SIZE = 128

HEAD_DIM = 64
H_RET = 8
H_SB = 8
RET_WIDTH = H_RET * HEAD_DIM
SB_WIDTH = H_SB * HEAD_DIM
IN0_WIDTH = 4 * RET_WIDTH + 4 * SB_WIDTH
RET_CHUNK = 128
ROPE_BASE = 10000.0
Q_BLOCK = 128
H_NSA = 16
G_NSA = 2
HPG = H_NSA // G_NSA
NSA_WIDTH = H_NSA * HEAD_DIM
KV_WIDTH = G_NSA * HEAD_DIM
IN1_SIZES = (NSA_WIDTH, KV_WIDTH, KV_WIDTH, KV_WIDTH, KV_WIDTH, KV_WIDTH, KV_WIDTH, NSA_WIDTH, 3 * H_NSA)
IN1_WIDTH = NSA_WIDTH * 2 + KV_WIDTH * 6 + 3 * H_NSA
CMP_BLOCK = 32
SEL_BLOCK = 64
TOP_N = 16
WINDOW = 512
FORCE_BONUS = 1000.0
NEG_INF = -1e30
EPS = 1e-6

kernel_name = 'hybrid_retention_stickbreak_nsa_step'

def _rmsnorm(x, g):
    xf = x.astype(jnp.float32)
    y = xf * lax.rsqrt(jnp.mean(xf * xf, axis=-1, keepdims=True) + EPS)
    return (y * g.astype(jnp.float32)).astype(x.dtype)

def _head_groupnorm(o, g):
    mu = jnp.mean(o, axis=-1, keepdims=True)
    oc = o - mu
    return oc * lax.rsqrt(jnp.mean(oc * oc, axis=-1, keepdims=True) + EPS) * g.astype(jnp.float32)

def _rope(x, pos):
    half = x.shape[-1] // 2
    inv = ROPE_BASE ** (-jnp.arange(half, dtype=jnp.float32) / half)
    ang = pos.astype(jnp.float32)[:, None] * inv[None, :]
    cos = jnp.cos(ang)[None, :, None, :]
    sin = jnp.sin(ang)[None, :, None, :]
    xf = x.astype(jnp.float32)
    x1, x2 = xf[..., :half], xf[..., half:]
    return jnp.concatenate([x1 * cos - x2 * sin, x1 * sin + x2 * cos], axis=-1).astype(x.dtype)

def _split_cols(z, sizes):
    cuts = [int(c) for c in np.cumsum(sizes)[:-1]]
    return jnp.split(z, cuts, axis=-1)

def _block_size(l):
    return Q_BLOCK if l % Q_BLOCK == 0 else l

def _gather_pages(pool, page_table):
    g = pool[page_table]
    return g.reshape(page_table.shape[0], page_table.shape[1] * pool.shape[1], pool.shape[2], pool.shape[3])

def _retention(q, k, v, s0):
    b, l, h, d = q.shape
    f32 = jnp.float32
    c = RET_CHUNK if l % RET_CHUNK == 0 else l
    n = l // c
    lg = jnp.log1p(-jnp.exp2(-5.0 - jnp.arange(h, dtype=f32)))
    idx = jnp.arange(c, dtype=f32)
    diff = idx[:, None] - idx[None, :]
    inner = jnp.where(diff >= 0, jnp.exp(lg[:, None, None] * jnp.maximum(diff, 0.0)), 0.0)
    q_dec = jnp.exp(lg[:, None] * (idx + 1.0))[None, :, :, None]
    k_dec = jnp.exp(lg[:, None] * (c - 1.0 - idx))[None, :, :, None]
    c_dec = jnp.exp(lg * c)[None, :, None, None]

    def chunks(t):
        return t.astype(f32).reshape(b, n, c, h, d).transpose(1, 0, 3, 2, 4)

    def step(s, inp):
        qi, ki, vi = inp
        att = jnp.einsum('bhnd,bhmd->bhnm', qi, ki) * inner
        o = jnp.einsum('bhnm,bhme->bhne', att, vi) + jnp.einsum('bhnd,bhde->bhne', qi, s) * q_dec
        s = s * c_dec + jnp.einsum('bhmd,bhme->bhde', ki * k_dec, vi)
        return s, o

    s, o = lax.scan(step, s0.astype(f32), (chunks(q), chunks(k) * d ** -0.5, chunks(v)))
    return o.transpose(1, 0, 3, 2, 4).reshape(b, l, h, d), s

def _sb_attention(q, k, v, q_pos, k_pos):
    b, lq, h, d = q.shape
    qb = _block_size(lq)
    nb = lq // qb
    qs = q.reshape(b, nb, qb, h, d).swapaxes(0, 1)
    ps = q_pos.reshape(nb, qb)

    def blk(args):
        qi, pi = args
        z = jnp.einsum('bqhd,bkhd->bhqk', qi, k).astype(jnp.float32) * d ** -0.5
        mask = k_pos[None, :] < pi[:, None]
        lm = jnp.where(mask, jax.nn.log_sigmoid(-z), 0.0)
        la = jax.nn.log_sigmoid(z) + lax.cumsum(lm, axis=3, reverse=True) - lm
        a = jnp.where(mask, jnp.exp(la), 0.0)
        return jnp.einsum('bhqk,bkhd->bqhd', a.astype(v.dtype), v)

    o = lax.map(blk, (qs, ps))
    return o.swapaxes(0, 1).reshape(b, lq, h, d)

def _compress(t, pe, w):
    b, lk, g, d = t.shape
    nb = lk // CMP_BLOCK
    tb = t[:, :nb * CMP_BLOCK].reshape(b, nb, CMP_BLOCK, g, d) + pe[None, None, :, None, :]
    return jnp.einsum('bnlgd,lde->bnge', tb, w)

def _nsa_block(qg, gates, q_pos, cmp_k, cmp_v, ksb, vsb, kw, vw, kw_pos):
    b, lq, g, hp, d = qg.shape
    scale = d ** -0.5
    nb = cmp_k.shape[1]
    nsb = ksb.shape[2]
    s = jnp.einsum('bqghd,bngd->bghqn', qg, cmp_k).astype(jnp.float32) * scale
    cmask = (jnp.arange(nb) * CMP_BLOCK + CMP_BLOCK - 1)[None, :] <= q_pos[:, None]
    p = jax.nn.softmax(jnp.where(cmask, s, NEG_INF), axis=-1) * cmask
    o_cmp = jnp.einsum('bghqn,bngd->bqghd', p.astype(cmp_v.dtype), cmp_v)
    ratio = SEL_BLOCK // CMP_BLOCK
    imp = jnp.pad(p.sum(axis=2), ((0, 0), (0, 0), (0, 0), (0, nsb * ratio - nb)))
    imp = imp.reshape(b, g, lq, nsb, ratio).sum(axis=-1)
    cur = q_pos // SEL_BLOCK
    blk = jnp.arange(nsb)[None, :]
    forced = (blk == 0) | (blk == cur[:, None]) | (blk == cur[:, None] - 1)
    valid = blk <= cur[:, None]
    score = jnp.where(valid, imp + FORCE_BONUS * forced, NEG_INF)
    n_sel = min(TOP_N, nsb)
    _, idx = lax.top_k(score, n_sel)
    bi = jnp.arange(b)[:, None, None, None]
    gi = jnp.arange(g)[None, :, None, None]
    ksel = ksb[bi, gi, idx].reshape(b, g, lq, n_sel * SEL_BLOCK, d)
    vsel = vsb[bi, gi, idx].reshape(b, g, lq, n_sel * SEL_BLOCK, d)
    kpos = (idx[..., None] * SEL_BLOCK + jnp.arange(SEL_BLOCK)).reshape(b, g, lq, n_sel * SEL_BLOCK)
    smask = (kpos <= q_pos[None, None, :, None])[:, :, None]
    ss = jnp.einsum('bqghd,bgqkd->bghqk', qg, ksel).astype(jnp.float32) * scale
    ps = jax.nn.softmax(jnp.where(smask, ss, NEG_INF), axis=-1)
    o_sel = jnp.einsum('bghqk,bgqkd->bqghd', ps.astype(vsel.dtype), vsel)
    sw = jnp.einsum('bqghd,bkgd->bghqk', qg, kw).astype(jnp.float32) * scale
    wmask = (kw_pos[None, :] <= q_pos[:, None]) & (kw_pos[None, :] > q_pos[:, None] - WINDOW) & (kw_pos[None, :] >= 0)
    pw = jax.nn.softmax(jnp.where(wmask, sw, NEG_INF), axis=-1)
    o_win = jnp.einsum('bghqk,bkgd->bqghd', pw.astype(vw.dtype), vw)
    return gates[..., 0:1] * o_cmp + gates[..., 1:2] * o_sel + gates[..., 2:3] * o_win

def _layer0(x, pos, s0, sb_past, norm_g, w_in, ret_gn_g, sb_qn_g, sb_kn_g, w_out):
    b, l, _ = x.shape
    z = _rmsnorm(x, norm_g) @ w_in
    rq, rk, rv, rg, sq, sk, sv, sg = jnp.split(z, 8, axis=-1)
    rq = _rope(rq.reshape(b, l, H_RET, HEAD_DIM), pos)
    rk = _rope(rk.reshape(b, l, H_RET, HEAD_DIM), pos)
    o_ret, s_new = _retention(rq, rk, rv.reshape(b, l, H_RET, HEAD_DIM), s0)
    o_ret = _head_groupnorm(o_ret, ret_gn_g).astype(x.dtype).reshape(b, l, RET_WIDTH)
    sq = _rmsnorm(sq.reshape(b, l, H_SB, HEAD_DIM), sb_qn_g)
    sk = _rmsnorm(sk.reshape(b, l, H_SB, HEAD_DIM), sb_kn_g)
    sv = sv.reshape(b, l, H_SB, HEAD_DIM)
    if sb_past is None:
        k_all, v_all = sk, sv
    else:
        k_all = jnp.concatenate([sb_past[0].astype(sk.dtype), sk], axis=1)
        v_all = jnp.concatenate([sb_past[1].astype(sv.dtype), sv], axis=1)
    k_pos = jnp.arange(k_all.shape[1], dtype=jnp.int32)
    o_sb = _sb_attention(sq, k_all, v_all, pos, k_pos).reshape(b, l, SB_WIDTH)
    mix = jnp.concatenate([o_ret * jax.nn.silu(rg), o_sb * jax.nn.silu(sg)], axis=-1)
    return x + mix @ w_out, s_new.astype(s0.dtype), sk, sv

def _layer1(x, pos, past, norm_g, w_in, qn_g, cmp_kn_g, sel_kn_g, win_kn_g, cmp_pe, w_cmp_k, w_cmp_v, w_out):
    b, l, _ = x.shape
    z = _rmsnorm(x, norm_g) @ w_in
    q, kc, vc, ks, vs, kw, vw, gate, bgate = _split_cols(z, IN1_SIZES)
    q = _rmsnorm(q.reshape(b, l, H_NSA, HEAD_DIM), qn_g).reshape(b, l, G_NSA, HPG, HEAD_DIM)
    kc = kc.reshape(b, l, G_NSA, HEAD_DIM)
    vc = vc.reshape(b, l, G_NSA, HEAD_DIM)
    ks = _rmsnorm(ks.reshape(b, l, G_NSA, HEAD_DIM), sel_kn_g)
    vs = vs.reshape(b, l, G_NSA, HEAD_DIM)
    kw = _rmsnorm(kw.reshape(b, l, G_NSA, HEAD_DIM), win_kn_g)
    vw = vw.reshape(b, l, G_NSA, HEAD_DIM)
    gates = jax.nn.sigmoid(bgate.astype(jnp.float32)).reshape(b, l, G_NSA, HPG, 3).astype(x.dtype)
    if past is None:
        kc_all, vc_all, ks_all, vs_all = kc, vc, ks, vs
    else:
        pkc, pvc, pks, pvs, wk_buf, wv_buf = past
        kc_all = jnp.concatenate([pkc.astype(kc.dtype), kc], axis=1)
        vc_all = jnp.concatenate([pvc.astype(vc.dtype), vc], axis=1)
        ks_all = jnp.concatenate([pks.astype(ks.dtype), ks], axis=1)
        vs_all = jnp.concatenate([pvs.astype(vs.dtype), vs], axis=1)
    lk = kc_all.shape[1]
    cmp_k = _rmsnorm(_compress(kc_all, cmp_pe, w_cmp_k), cmp_kn_g)
    cmp_v = _compress(vc_all, cmp_pe, w_cmp_v)
    nsb = -(-lk // SEL_BLOCK)

    def to_blocks(t):
        t = jnp.pad(t, ((0, 0), (0, nsb * SEL_BLOCK - lk), (0, 0), (0, 0)))
        return t.reshape(b, nsb, SEL_BLOCK, G_NSA, HEAD_DIM).transpose(0, 3, 1, 2, 4)

    ksb, vsb = to_blocks(ks_all), to_blocks(vs_all)
    if past is None:
        qb = _block_size(l)
        nqb = l // qb
        kw_pad = jnp.pad(kw, ((0, 0), (WINDOW, 0), (0, 0), (0, 0)))
        vw_pad = jnp.pad(vw, ((0, 0), (WINDOW, 0), (0, 0), (0, 0)))

        def body(args):
            qi, gi, st = args
            kwi = lax.dynamic_slice_in_dim(kw_pad, st, WINDOW + qb, axis=1)
            vwi = lax.dynamic_slice_in_dim(vw_pad, st, WINDOW + qb, axis=1)
            kwp = st - WINDOW + jnp.arange(WINDOW + qb, dtype=jnp.int32)
            return _nsa_block(qi, gi, st + jnp.arange(qb, dtype=jnp.int32), cmp_k, cmp_v, ksb, vsb, kwi, vwi, kwp)

        def qblocks(t):
            return t.reshape((b, nqb, qb) + t.shape[2:]).swapaxes(0, 1)

        o = lax.map(body, (qblocks(q), qblocks(gates), jnp.arange(nqb, dtype=jnp.int32) * qb))
        o = o.swapaxes(0, 1).reshape(b, l, NSA_WIDTH)
        keep = min(WINDOW, l)
        win_k_new, win_v_new = kw[:, l - keep:], vw[:, l - keep:]
    else:
        wbuf = wk_buf.shape[1]
        wk_all = jnp.concatenate([wk_buf.astype(kw.dtype), kw], axis=1)
        wv_all = jnp.concatenate([wv_buf.astype(vw.dtype), vw], axis=1)
        wpos = PAST_LEN - wbuf + jnp.arange(wk_all.shape[1], dtype=jnp.int32)
        o = _nsa_block(q, gates, pos, cmp_k, cmp_v, ksb, vsb, wk_all, wv_all, wpos).reshape(b, l, NSA_WIDTH)
        win_k_new, win_v_new = wk_all[:, l:], wv_all[:, l:]
    y = x + (o * jax.nn.silu(gate)) @ w_out
    return y, kc, vc, ks, vs, win_k_new, win_v_new

def setup_inputs(seed: int = 0) -> dict:
    key = jax.random.key(seed)
    ks = jax.random.split(key, 40)
    f32 = jnp.float32
    n_pages = PAST_LEN // PAGE_SIZE
    n_used = DEC_BATCH * n_pages
    n_phys = n_used + n_used // 4
    w_buf = min(WINDOW, PAST_LEN)

    def nrm(k, shape, s=1.0):
        return s * jax.random.normal(k, shape, f32)

    def gain(k, shape):
        return 1.0 + 0.02 * jax.random.normal(k, shape, f32)

    page_table = jax.random.permutation(ks[0], n_phys)[:n_used].reshape(DEC_BATCH, n_pages).astype(jnp.int32)
    return {
        'x_prompt': nrm(ks[1], (BATCH, SEQ, D_MODEL)),
        'x_sample': nrm(ks[2], (DEC_BATCH, DEC_SEQ, D_MODEL)),
        'state_ret': nrm(ks[3], (DEC_BATCH, H_RET, HEAD_DIM, HEAD_DIM), 0.1),
        'cache_sb_k': nrm(ks[4], (n_phys, PAGE_SIZE, H_SB, HEAD_DIM)),
        'cache_sb_v': nrm(ks[5], (n_phys, PAGE_SIZE, H_SB, HEAD_DIM)),
        'cache_cmp_k': nrm(ks[6], (n_phys, PAGE_SIZE, G_NSA, HEAD_DIM)),
        'cache_cmp_v': nrm(ks[7], (n_phys, PAGE_SIZE, G_NSA, HEAD_DIM)),
        'cache_sel_k': nrm(ks[8], (n_phys, PAGE_SIZE, G_NSA, HEAD_DIM)),
        'cache_sel_v': nrm(ks[9], (n_phys, PAGE_SIZE, G_NSA, HEAD_DIM)),
        'cache_win_k': nrm(ks[10], (DEC_BATCH, w_buf, G_NSA, HEAD_DIM)),
        'cache_win_v': nrm(ks[11], (DEC_BATCH, w_buf, G_NSA, HEAD_DIM)),
        'page_table': page_table,
        'norm0_g': gain(ks[12], (D_MODEL,)),
        'w_in0': nrm(ks[13], (D_MODEL, IN0_WIDTH), D_MODEL ** -0.5),
        'ret_gn_g': gain(ks[14], (H_RET, HEAD_DIM)),
        'sb_qn_g': gain(ks[15], (HEAD_DIM,)),
        'sb_kn_g': gain(ks[16], (HEAD_DIM,)),
        'w_out0': nrm(ks[17], (RET_WIDTH + SB_WIDTH, D_MODEL), (RET_WIDTH + SB_WIDTH) ** -0.5),
        'norm1_g': gain(ks[18], (D_MODEL,)),
        'w_in1': nrm(ks[19], (D_MODEL, IN1_WIDTH), D_MODEL ** -0.5),
        'nsa_qn_g': gain(ks[20], (HEAD_DIM,)),
        'cmp_kn_g': gain(ks[21], (HEAD_DIM,)),
        'sel_kn_g': gain(ks[22], (HEAD_DIM,)),
        'win_kn_g': gain(ks[23], (HEAD_DIM,)),
        'cmp_pe': nrm(ks[24], (CMP_BLOCK, HEAD_DIM), 0.1),
        'w_cmp_k': nrm(ks[25], (CMP_BLOCK, HEAD_DIM, HEAD_DIM), (CMP_BLOCK * HEAD_DIM) ** -0.5),
        'w_cmp_v': nrm(ks[26], (CMP_BLOCK, HEAD_DIM, HEAD_DIM), (CMP_BLOCK * HEAD_DIM) ** -0.5),
        'w_out1': nrm(ks[27], (NSA_WIDTH, D_MODEL), NSA_WIDTH ** -0.5),
    }

def reference(x_prompt, x_sample, state_ret, cache_sb_k, cache_sb_v, cache_cmp_k, cache_cmp_v,
              cache_sel_k, cache_sel_v, cache_win_k, cache_win_v, page_table,
              norm0_g, w_in0, ret_gn_g, sb_qn_g, sb_kn_g, w_out0,
              norm1_g, w_in1, nsa_qn_g, cmp_kn_g, sel_kn_g, win_kn_g, cmp_pe, w_cmp_k, w_cmp_v, w_out1):
    yp, ys = x_prompt, x_sample
    pos_p = jnp.arange(x_prompt.shape[1], dtype=jnp.int32)
    pos_s = PAST_LEN + jnp.arange(x_sample.shape[1], dtype=jnp.int32)
    for layer in range(DEPTH):
        if layer % 2 == 0:
            s0 = jnp.zeros((x_prompt.shape[0], H_RET, HEAD_DIM, HEAD_DIM), state_ret.dtype)
            yp, ret_p, sbk_p, sbv_p = _layer0(yp, pos_p, s0, None, norm0_g, w_in0, ret_gn_g, sb_qn_g, sb_kn_g, w_out0)
            sb_past = (_gather_pages(cache_sb_k, page_table), _gather_pages(cache_sb_v, page_table))
            ys, ret_s, sbk_s, sbv_s = _layer0(ys, pos_s, state_ret, sb_past, norm0_g, w_in0, ret_gn_g, sb_qn_g, sb_kn_g, w_out0)
        else:
            yp, ckp, cvp, skp, svp, wkp, wvp = _layer1(yp, pos_p, None, norm1_g, w_in1, nsa_qn_g, cmp_kn_g, sel_kn_g,
                                                     win_kn_g, cmp_pe, w_cmp_k, w_cmp_v, w_out1)
            nsa_past = (_gather_pages(cache_cmp_k, page_table), _gather_pages(cache_cmp_v, page_table),
                        _gather_pages(cache_sel_k, page_table), _gather_pages(cache_sel_v, page_table),
                        cache_win_k, cache_win_v)
            ys, cks, cvs, sks, svs, wks, wvs = _layer1(ys, pos_s, nsa_past, norm1_g, w_in1, nsa_qn_g, cmp_kn_g, sel_kn_g,
                                                     win_kn_g, cmp_pe, w_cmp_k, w_cmp_v, w_out1)
    return (yp, ys, ret_p, ret_s, sbk_p, sbv_p, sbk_s, sbv_s, ckp, cvp, skp, svp, wkp, wvp, cks, cvs, sks, svs, wks, wvs)


_drawn_inputs = setup_inputs


def setup_inputs(seed=0):
    import zlib

    import numpy as np

    out = dict(_drawn_inputs(seed))
    spreads = {}
    factors = {'cache_sel_k': 5.066,
     'cache_sel_v': 4.14,
     'ret_gn_g': 7.554,
     'sb_qn_g': 23.526,
     'norm1_g': 2.764,
     'nsa_qn_g': 8.0,
     'cmp_kn_g': 8.0,
     'sel_kn_g': 3.417,
     'win_kn_g': 3.019}
    for name, (base, spread) in spreads.items():
        noise = np.random.default_rng([zlib.crc32(name.encode()), seed]).standard_normal(out[name].shape)
        drawn = base * np.exp(spread * noise) if base else spread * noise
        out[name] = jnp.asarray(drawn.astype(out[name].dtype))
    for name, factor in factors.items():
        out[name] = (out[name] * factor).astype(out[name].dtype)
    return out
```

```python
import math
from contextlib import ExitStack, contextmanager

import numpy as np

import concourse.bass as bass
from concourse import mybir

F32 = mybir.dt.float32
I32 = mybir.dt.int32
ALU = mybir.AluOpType
ACT = mybir.ActivationFunctionType
AX = mybir.AxisListType

P = 128
D = 1024
KT = D // P
SEQ = 512
NT = SEQ // P
NB = 8
PAST = 1024
PAGE = 128
NPG = PAST // PAGE
DH = 64
H = 8
HW = H * DH
NHP = H // 2
CH = 512
W0 = 8 * HW
W1 = 2864
HN = 16
G = 2
HPG = HN // G
CB = 32
NCB = PAST // CB
NPB = SEQ // CB
NSB = PAST // 64
EPS = 1e-6
NEG = -1e30
SCALE = DH ** -0.5
SQ, SK, SV, SG, RQ, RK, RV, RG = range(8)
SECTION = [(i + 4) % 8 for i in range(8)]

AUX = [("ident", P), ("tri_neg", P), ("ones_neg", P), ("strict", P), ("strict_neg", P),
       ("causal_neg", P), ("swap", P), ("ret_decay", H * P), ("q_decay", H), ("k_decay", H), ("chunk_decay", NHP),
       ("cosine", (NT + 1) * DH), ("sine", (NT + 1) * DH), ("gamma", NHP), ("half_ones", 2),
       ("mean_ones", P), ("own_head", HW), ("to_row", NB * NB),
       ("gain_in0", KT), ("gain_in1", KT), ("gain_ret", HW), ("gain_sq", DH), ("gain_sk", DH),
       ("gain_q", DH), ("gain_sel", DH), ("gain_win", DH), ("gain_cmp", 1), ("pe", CB),
       ("own_group", G), ("group_sum", NB * G), ("cmp_own", NB * NCB), ("spread", P),
       ("forced", NSB), ("block_no", NSB), ("cmp_neg", NT * NPB), ("cmp_one", NT * NPB)]
AT = {}
_n = 0
for _name, _w in AUX:
    AT[_name] = (_n, _n + _w)
    _n += _w
NAUX = _n


def constants():
    f = np.float32
    c = np.zeros((P, NAUX), f)

    def put(name, a):
        a = np.asarray(a, f)
        lo, hi = AT[name]
        c[:a.shape[0], lo:hi] = a.reshape(a.shape[0], -1)

    i = np.arange(P)
    row, col = i[:, None], i[None, :]
    put("ident", np.eye(P))
    put("tri_neg", -(row >= col).astype(f))
    put("ones_neg", -np.ones((P, P)))
    put("strict", row < col)
    put("strict_neg", np.where(row < col, 0, NEG))
    put("swap", (row + DH) % P == col)
    put("causal_neg", np.where(col <= row, 0, NEG))
    lg = np.log1p(-np.exp2(-5.0 - np.arange(H)))
    dec = np.exp(-lg[None, :] * (i[:, None] + 1)) * SCALE
    put("ret_decay", dec[:, :, None] * (row <= col)[:, None, :])
    put("q_decay", np.exp(lg[None, :] * (i[:, None] + 1)))
    put("k_decay", np.exp(lg[None, :] * (P - 1 - i[:, None])) * SCALE)
    head = 2 * np.arange(NHP)[None, :] + (i[:, None] // DH)
    put("chunk_decay", np.exp(lg[head] * P))
    put("gamma", np.exp(lg[head]))
    half = DH // 2
    inv = (10000.0 ** (-np.arange(half, dtype=f) / half)).astype(f)
    pos = np.concatenate([np.arange(SEQ), np.full(P, PAST)]).reshape(NT + 1, P).T.astype(f)
    ang = pos[:, :, None] * inv
    put("cosine", np.concatenate([np.cos(ang), np.cos(ang)], -1))
    put("sine", np.concatenate([-np.sin(ang), np.sin(ang)], -1))
    put("half_ones", (row // DH == np.arange(2)[None, :]))
    put("mean_ones", (row // DH == col // DH) / DH)
    put("own_head", (i[:, None] % 32 == np.arange(HW)[None, :] // DH))
    put("to_row", np.broadcast_to(np.eye(NB)[None], (P, NB, NB)))
    put("own_group", ((i[:, None] % HN) // HPG == np.arange(G)[None, :]))
    bg = np.arange(NB * G)
    put("group_sum", ((i[:, None] // HPG) == bg[None, :]))
    put("spread", (bg[:, None] == i[None, :] // HPG))
    put("cmp_own", np.where(i[:, None] // HN == np.arange(NB * NCB)[None, :] // NCB, 0, NEG))
    blk = np.arange(NSB)
    put("forced", np.broadcast_to(1000.0 * ((blk == 0) | (blk == NSB - 1)), (NB * G, NSB)))
    put("block_no", np.broadcast_to(blk + 1.0, (NB * G, NSB)))
    t = np.arange(SEQ).reshape(NT, P).T[:, :, None]
    ok = np.arange(NPB) * CB + CB - 1 <= t
    put("cmp_neg", np.where(ok, 0, NEG))
    put("cmp_one", ok)
    return c


class Steps:

    def __init__(self, eng, sem):
        self.eng, self.sem, self.n, self.base = eng, sem, 0, 0

    def done(self, ins):
        ins.then_inc(self.sem, 1)
        self.n += 1
        self.eng.wait_ge(self.sem, self.base + self.n)

    @contextmanager
    def loop(self, count, steps):
        start = self.n
        with self.eng.Fori(0, count) as i:
            self.base, self.n = i * steps + start, 0
            yield i
            assert self.n == steps, (self.n, steps)
        self.base, self.n = 0, start + count * steps


class Marks:

    def __init__(self, sem, names):
        self.sem, self.names, self.given = sem, names, 0

    def next(self, name):
        assert self.names[self.given] == name, name
        self.given += 1
        return self.sem, 1

    def at(self, name):
        return self.sem, self.names.index(name) + 1


def build(nc, ins, outs):
    with ExitStack() as ctx:
        def sb(name, shape, dt=F32):
            return ctx.enter_context(nc.sbuf_tensor(name, shape, dt))

        def sem(name):
            return ctx.enter_context(nc.semaphore(name))

        def dram(name, shape):
            return nc.dram_tensor(name, shape, F32, kind="Internal").ap()

        ps = ctx.enter_context(nc.psum_tensor("ps", [P, 8, CH], F32))

        z = sb("z", [P, NT + 1, W0])
        wring = sb("wring", [P, 2, KT, CH])
        xres = sb("xres", [P, NT + 1, D])
        aux = sb("consts", [P, NAUX])
        NX, NQ, NPAGES = KT * (SEQ + NB), NB * HW, 4 * HW
        arena = sb("arena", [P, NX + NQ + NPAGES])
        xnT = arena[:, 0:NX].rearrange("p (k n) -> p k n", k=KT)
        qbc = arena[:, NX:NX + NQ].rearrange("p (b c) -> p b c", b=NB)
        pages = arena[:, NX + NQ:].rearrange("p (s c) -> p s c", s=4)
        work = sb("work", [P, 3072])
        S_ret = sb("S_ret", [P, NHP, DH])
        kqT = sb("kqT", [P, 2 * NHP * NB])
        stats = sb("stats", [P, 96])
        table = sb("table", [1, NB * NPG], I32)

        def cst(name, rows=P):
            lo, hi = AT[name]
            return aux[0:rows, lo:hi]

        def flat(a):
            return a.rearrange("p a b -> p (a b)")

        xflat = flat(xres[:])

        d_sq = dram("d_sq", (NB, HW))
        d_rv = dram("d_rv", (NB, HW))
        d_ro = dram("d_ro", (2, NB, NHP, DH))

        s_aux, s_x, s_table = sem("aux_loaded"), sem("x_loaded"), sem("table_loaded")
        w_loaded = [sem("w_loaded0"), sem("w_loaded1")]
        page_loaded = [sem(f"page_loaded{i}") for i in range(4)]
        page_free = sem("page_free")
        act_step, dve_step, pool_step = sem("act_step"), sem("dve_step"), sem("pool_step")
        xn_ready, xt_summed, xnT_ready = sem("xn_ready"), sem("xt_summed"), sem("xnT_ready")
        mm_done, bank_free = sem("mm_done"), sem("bank_free")
        ssq_ready, rstd_ready = sem("ssq_ready"), sem("rstd_ready")
        sq_sent, sq_spread = sem("sq_sent"), sem("sq_spread")
        sections_ready = sem("sections_ready")
        ret_staged, ret_turned, ret_T, ret_att, ret_attm, ret_kd, ret_o, ret_kv, ret_S, ret_done = (
            sem("ret_" + x) for x in ("staged", "turned", "T", "att", "attm", "kd", "o", "kv", "S", "done"))
        gn_sum, gn_rstd = sem("gn_sum"), sem("gn_rstd")
        sb_staged, sb_turned, sb_T, sb_z, sb_ln, sb_sp, sb_la, sb_masked, sb_a, sb_o, sb_mixed = (
            sem("sb_" + x) for x in ("staged", "turned", "T", "z", "ln", "sp", "la", "masked", "a", "o", "mixed"))
        ds_scores, ds_ln, ds_sp, ds_la, ds_lasum, ds_a, ds_stage, ds_o, ds_om, ds_row, ds_mixed = (
            sem("ds_" + x) for x in ("scores", "ln", "sp", "la", "lasum", "a", "stage", "o", "om", "row", "mixed"))
        rs_in, rs_turned, rs_kqT, rs_S, rs_t, rs_sum, rs_row, rs_sent, rs_back, rs_done = (
            sem("rs_" + x) for x in ("in", "turned", "kqT", "S", "t", "sum", "row", "sent", "back", "done"))
        rv_sent = sem("rv_sent")
        zeroed, zeroed_stats, rstd_x = sem("zeroed"), sem("zeroed_stats"), sem("rstd_x")
        mix_turned, mix_T, xr_loaded = sem("mix_turned"), sem("mix_T"), sem("xr_loaded")
        stored = sem("stored")

        rows = [P] * NT + [NB]
        NCHUNK0 = W0 // CH
        NC1 = -(-W1 // CH)

        Q1, KC, VC, KS, VS, KW, VW, GATE, BG = 0, 1024, 1152, 1280, 1408, 1536, 1664, 1792, 2816
        P_OFF, PT_OFF = 2864, 3376
        N_CMP = NB * NCB + NPB
        kcT = arena[:, 0:CB * N_CMP].rearrange("p (l n) -> p l n", l=CB)
        ckT, rk1, cvT = work[:, 0:N_CMP], work[:, 272:544], work[:, 816:1088]
        cv_s = work[:, 1088:1344]
        cv_pair = work[:, 1344:1600]
        cvT_pair = work[:, 544:672]
        q_bh, kn_bh, QT = work[:, 1664:1728], work[:, 1728:1984], work[:, 1984:2112]
        q_st, q_dup = work[:, 2112:2240], work[:, 2240:2368]
        kn_bg = work[0:NB * G, 2368:2624]
        small = work[:, 2624:2880]
        KZ = 2 * SEQ + NPB
        Kz = arena[:, 0:4 * KZ].rearrange("p (g u c) -> p g u c", g=G, u=2)
        q_tok, qTs = arena[:, 4160:4672], arena[:, 4672:5184]
        p_cmp = arena[:, 5184:5696].rearrange("p (t u n) -> p t u n", t=NT, u=2)
        p_cmpT = arena[:, 5696:6208]
        Qpad = arena[:, 5952:6976]
        KTs = arena[:, 0:1536].rearrange("p (q c) -> p q c", q=3)
        Pexp = arena[:, 1536:3072]
        PT1 = arena[:, 3072:4608].rearrange("p (j c) -> p j c", j=12)
        p_imp = arena[:, 4608:4864]
        p_impT = arena[:, 4864:5120].rearrange("p (j c) -> p j c", j=2)
        oT1 = arena[:, 6976:7232].rearrange("p (w c) -> p w c", w=2)
        o3 = arena[:, 7232:7616]
        o_row = arena[0:NB, 7616:8640]
        slot1 = pages[:, 1:4, :]
        wcmp = [wring[:, u].rearrange("p k c -> p (k c)").rearrange("p (l m) -> p l m", l=CB) for u in range(2)]
        d_q, d_kv, d_g, d_o = (dram("d_q", (NB, D)), dram("d_kv", (NB, G, 4, DH)), dram("d_g", (NB, 3 * HN)), dram("d_o", (NB, D)))
        k_ssq, k_rstd = sem("k_ssq"), sem("k_rstd")
        heads_ready = sem("heads_ready")
        wz, wcmp_loaded = sem("wz"), [sem("wcmp_k_loaded"), sem("wcmp_v_loaded")]
        cm_loaded = [sem("cm_loaded0"), sem("cm_loaded1")]
        cm_turned, cm_T, cmp_turned, cmp_T, cm_proj, cm_sq, cm_mean, cm_rstd, ckT_ready, cvT_ready = (
            sem("cm_" + x) for x in ("turned", "T", "p_turned", "p_T", "proj", "sq", "mean", "rstd", "ckT", "cvT"))
        cv_turned, cv_ready, kz_turned, kz_T, kz_swapped, kz_ready = (
            sem(x) for x in ("cv_turned", "cv_ready", "kz_turned", "kz_T", "kz_swapped", "kz_ready"))
        nq_staged, nq_turned, nq_T, nc_s, nc_max, nc_exp, nc_p, nc_turned, nc_T = (
            sem(x) for x in ("nq_staged", "nq_turned", "nq_T", "nc_s", "nc_max", "nc_exp", "nc_p", "nc_turned", "nc_T"))
        n_s, n_max, n_p, n_t, n_av, n_o = (sem("n_" + x) for x in ("s", "max", "p", "t", "av", "o"))
        n_pt = [sem("n_pt_sel"), sem("n_pt_win")]
        r_sent, r_back = sem("r_sent"), sem("r_back")
        marks_dve = Marks(sem("sample_dve"), ["r_dup", "r_kn", "i_zero", "r_pad", "i_max", "i_p", "i_neg", "sk_max", "sv_oT", "sv_sum", "sv_done"])
        marks_pe = Marks(sem("sample_pe"), ["r_spread", "r_turned", "i_s", "i_sum", "i_o", "sk_pturned", "sv_back"])
        marks_act = Marks(sem("sample_act"), ["r_QT", "i_exp", "i_T", "sk_exp", "sk_PT"])
        sk_loaded = [sem(f"sk_loaded{q}") for q in range(3)]
        sk_turned, sk_T, sk_scored, sk_q = (sem("sk_" + x) for x in ("turned", "T", "scored", "q"))
        sv_loaded = [sem(f"sv_loaded{q}") for q in range(3)]
        sv_used, sv_sent, sv_row = sem("sv_used"), sem("sv_sent"), sem("sv_row")

        def sec(t, s, r=None):
            return z[0:(r or rows[t]), t, s * HW:(s + 1) * HW]

        def quarters(a, e):
            return [(c // P * 32, c, min(c + P, e)) for c in range(a, e, P)]

        def heads(a):
            return a.rearrange("p (h d) -> p h d", d=DH)

        def bc(a, shape):
            return a.broadcast_to(shape)

        def page_group(eng, name, col, dst, sem_):
            src = ins[name].rearrange("n p g d -> n p (g d)")
            for m in range(4):
                page = eng.value_load(table[0:1, bass.ds(col + m, 1)], min_val=0, max_val=src.shape[0] - 1)
                eng.dma_start(dst[:, m * P:(m + 1) * P].rearrange("p (a c) -> p a c", a=1),
                              src[bass.ds(page, 1)].rearrange("n p c -> p n c")).then_inc(sem_, 16)

        qk_st = xflat[:, 256:256 + 1024]
        qBD = xflat[:, 1280:2304].rearrange("p (a b n) -> p a b n", a=NHP, b=2)
        kT_r = xflat[:, 2304:2816]
        attm = xflat[:, 2816:3840]
        kd = xflat[:, 3840:4352]
        o_tmp = xflat[:, 4352:4864]
        tmp = work[:, 0:512]
        tmp2 = work[:, 512:1024]
        zs = work[:, 1024:1536]
        spz = work[:, 1536:2048]
        tail = work[:, 2048:2560]
        lnz = work[:, 2560:3072]
        a_st = work[:, 1536:2048].rearrange("p (j c) -> p j c", c=32)
        om = arena[:, 0:NB * HW]
        A_rs, B_rs = arena[:, NX:NX + 2048], arena[:, NX + 2048:NX + NQ]

        def by_pair(a):
            return a.rearrange("p (b a e) -> p b a e", b=NB, a=NHP)

        with nc.Block() as block:

            @block.sync
            def _(sp):
                sp.dma_start(aux[:], ins["aux"]).then_inc(s_aux, 16)
                x_tiles = ins["x_prompt"].rearrange("b (t p) d -> p (b t) d", p=P)
                x_rows = ins["x_sample"].rearrange("b s d -> (b s) d")
                sp.dma_start(xres[:, 0:NT, :], x_tiles).then_inc(s_x, 16)
                sp.dma_start(xres[0:NB, NT, :], x_rows).then_inc(s_x, 16)

                w_in0 = ins["w_in0"].rearrange("(k p) n -> p k n", p=P)
                for n in range(4):
                    if n >= 2:
                        sp.wait_ge(mm_done, 5 * (n - 1))
                    c = SECTION[n] * CH
                    sp.dma_start(wring[:, n % 2], w_in0[:, :, c:c + CH]).then_inc(w_loaded[n % 2], 16)
                with sp.Fori(0, 2) as i:
                    for u in range(2):
                        sp.wait_ge(mm_done, 10 * i + 5 * (3 + u))
                        sp.dma_start(wring[:, u], w_in0[:, :, bass.ds(i * 2 * CH + u * CH, CH)]).then_inc(w_loaded[u], 16)
                sp.wait_ge(bank_free, 5 + 5 * 7)
                sp.dma_start(d_rv, sec(NT, RV)).then_inc(rv_sent, 16)
                sp.wait_ge(rv_sent, 16)
                sp.wait_ge(ds_scores, 1)
                for u in range(2):
                    half = slice(u * DH, (u + 1) * DH)
                    sp.dma_start(by_pair(A_rs)[half], ins["state_ret"].rearrange("b (a u) d e -> u d b a e", u=2)[u]).then_inc(rs_in, 16)
                    for b in range(NB):
                        row = d_rv.rearrange("b (a u e) -> b u a e", u=2, e=DH)[b, u]
                        sp.dma_start(by_pair(B_rs)[half, b], row.partition_broadcast(DH)).then_inc(rs_in, 16)
                w_out0 = ins["w_out0"].rearrange("(k p) n -> p k n", p=P)
                for u in range(2):
                    sp.wait_ge(mm_done, 5 * (7 + u))
                    sp.dma_start(wring[:, u], w_out0[:, :, u * CH:(u + 1) * CH]).then_inc(w_loaded[u], 16)

                n_store = [0]

                def store(out, src):
                    sp.dma_start(out, src).then_inc(stored, 16)
                    n_store[0] += 16

                sp.wait_ge(sections_ready, 2)
                store(outs["o4"].rearrange("b (t p) h d -> p (b t) (h d)", p=P), z[:, 0:NT, SK * HW:(SK + 1) * HW])
                store(outs["o5"].rearrange("b (t p) h d -> p (b t) (h d)", p=P), z[:, 0:NT, SV * HW:(SV + 1) * HW])
                store(outs["o6"].rearrange("b s h d -> (b s) (h d)"), sec(NT, SK))
                store(outs["o7"].rearrange("b s h d -> (b s) (h d)"), sec(NT, SV))
                sp.wait_ge(ret_S, NT + 1)
                for u in range(2):
                    store(outs["o2"].rearrange("b (a u) d e -> u d (b a) e", u=2)[u], S_ret[u * DH:(u + 1) * DH])
                sp.wait_ge(rs_S, 1)
                for u in range(2):
                    store(outs["o3"].rearrange("b (a u) d e -> u d b a e", u=2)[u], by_pair(A_rs)[u * DH:(u + 1) * DH])
                sp.wait_ge(rs_row, 1)
                sp.dma_start(d_ro.rearrange("u b a e -> u (b a e)"), B_rs[0:2]).then_inc(rs_sent, 16)
                sp.wait_ge(rs_sent, 16)
                for u in range(2):
                    sp.dma_start(B_rs[0:NB, 0:HW].rearrange("b (a u e) -> b a u e", u=2, e=DH)[:, :, u], d_ro[u]).then_inc(rs_back, 16)
                sp.wait_ge(sb_mixed, H + 2)
                sp.dma_start(xres[:, 0:NT, :], x_tiles).then_inc(xr_loaded, 16)
                sp.dma_start(xres[0:NB, NT, :], x_rows).then_inc(xr_loaded, 16)
                w_in1 = ins["w_in1"].rearrange("(k p) n -> p k n", p=P)
                for c in range(NC1):
                    n, w = 10 + c, min(CH, W1 - c * CH)
                    sp.wait_ge(mm_done, 5 * (n - 1))
                    sp.dma_start(wring[:, n % 2, :, 0:w], w_in1[:, :, c * CH:c * CH + w]).then_inc(w_loaded[n % 2], 16)
                for k, name in ((18, "cache_win_k"), (19, "cache_win_v")):
                    store(outs[f"o{k}"].rearrange("b s g d -> b (s g d)")[:, 0:511 * G * DH],
                          ins[name].rearrange("b s g d -> b (s g d)")[:, G * DH:512 * G * DH])
                sp.wait_ge(s_table, 16)

                for w, name in enumerate(("cache_cmp_k", "cache_cmp_v")):
                    with sp.Fori(0, NB) as b:
                        sp.wait_ge(cm_turned, b * 2 + (16 * w + 1))
                        page_group(sp, name, b * NPG, slot1[:, 0], cm_loaded[0])
                sp.wait_ge(heads_ready, 2)
                for k, col in ((8, KC), (9, VC), (10, KS), (11, VS), (12, KW), (13, VW)):
                    store(outs[f"o{k}"].rearrange("b (t p) g d -> p (b t) (g d)", p=P), z[:, 0:NT, col:col + P])
                for k, col in ((14, KC), (15, VC), (16, KS), (17, VS)):
                    store(outs[f"o{k}"].rearrange("b s g d -> (b s) (g d)"), z[0:NB, NT, col:col + P])
                for k, col in ((18, KW), (19, VW)):
                    store(outs[f"o{k}"].rearrange("b s g d -> b (s g d)")[:, 511 * G * DH:], z[0:NB, NT, col:col + P])
                sp.dma_start(d_q, z[0:NB, NT, Q1:Q1 + D]).then_inc(r_sent, 16)
                sp.dma_start(d_g, z[0:NB, NT, BG:BG + 3 * HN]).then_inc(r_sent, 16)
                for g in range(G):
                    sp.dma_start(d_kv[:, g], z[0:NB, NT, KS:GATE].rearrange("b (k g e) -> b k g e", k=4, g=G)[:, :, g]).then_inc(r_sent, 16)
                sp.wait_ge(r_sent, 64)
                sp.dma_start(q_bh, d_q.rearrange("b (h e) -> (b h) e", e=DH)).then_inc(r_back, 16)
                sp.dma_start(stats[:, 0:3], d_g.rearrange("b (h x) -> (b h) x", x=3)).then_inc(r_back, 16)
                sp.dma_start(kn_bg, d_kv.rearrange("b g k e -> (b g) (k e)")).then_inc(r_back, 16)
                w_out1 = ins["w_out1"].rearrange("(k p) n -> p k n", p=P)
                for u in range(2):
                    sp.wait_ge(cm_proj, u + 1)
                    sp.dma_start(wring[:, u], w_out1[:, :, u * CH:(u + 1) * CH]).then_inc(w_loaded[u], 16)
                for name, loaded, used in (("cache_sel_k", sk_loaded, sk_turned), ("cache_sel_v", sv_loaded, sv_used)):
                    with sp.Fori(0, NB) as b:
                        sp.wait_ge(used, b * 3 + 1)
                        page_group(sp, name, b * NPG, slot1[:, 0], loaded[0])
                sp.wait_ge(*marks_dve.at("sv_sum"))
                sp.dma_start(d_o.rearrange("b (h e) -> (b h) e", e=DH), q_bh).then_inc(sv_sent, 16)
                sp.wait_ge(sv_sent, 16)
                sp.dma_start(o_row, d_o).then_inc(sv_row, 16)
                sp.wait_ge(bank_free, 5 + 90)
                store(outs["o0"].rearrange("b (t p) d -> p (b t) d", p=P), xres[:, 0:NT, :])
                store(outs["o1"].rearrange("b s d -> (b s) d"), xres[0:NB, NT, :])
                sp.wait_ge(stored, n_store[0])

            @block.gpsimd
            def _(pool):
                pool.dma_start(table[:], ins["page_table"].rearrange("(o b) n -> o (b n)", o=1)).then_inc(s_table, 16)
                pool.wait_ge(s_table, 16)
                pool.wait_ge(s_aux, 16)
                pool.sem_inc(page_free, 4)

                def load_pages(cache, before):
                    src = ins[cache].rearrange("n p h d -> n p (h d)")
                    with pool.Fori(0, NB * NPG // 4) as r:
                        for u in range(4):
                            pool.wait_ge(page_free, r * 4 + (before + u + 1))
                            page = pool.value_load(table[0:1, bass.ds(r * 4 + u, 1)], min_val=0, max_val=src.shape[0] - 1)
                            pool.dma_start(pages[:, u:u + 1, :], src[bass.ds(page, 1)].rearrange("n p c -> p n c")
                                           ).then_inc(page_loaded[u], 16)

                load_pages("cache_sb_k", 0)
                with pool.Fori(0, NT) as t:
                    pool.wait_ge(ret_staged, t + 1)
                    nc.gpsimd.tensor_tensor(heads(kd), heads(qk_st[:, HW:2 * HW]),
                                            bc(cst("k_decay").unsqueeze(2), [P, H, DH]), ALU.mult).then_inc(ret_kd, 1)
                    pool.wait_ge(ret_kv, t + 1)
                load_pages("cache_sb_v", NB * NPG)
                pool.wait_ge(mm_done, 5 * (10 + NC1))
                nc.gpsimd.memset(wring[:], 0.0).then_inc(wz, 1)
                pool.wait_ge(wz, 1)
                for v, wname in enumerate(("w_cmp_k", "w_cmp_v")):
                    for g in range(G):
                        pool.dma_start(wcmp[v][g * DH:(g + 1) * DH, :, g * DH:(g + 1) * DH],
                                       ins[wname].rearrange("l d e -> d l e")).then_inc(wcmp_loaded[v], 16)
                for win, loaded, used in (("cache_win_k", sk_loaded, sk_turned), ("cache_win_v", sv_loaded, sv_used)):
                    with pool.Fori(0, NB) as b:
                        pool.wait_ge(used, b * 3 + 3)
                        pool.dma_start(slot1[:, 2].rearrange("p (t c) -> p t c", t=4),
                                       ins[win][bass.ds(b, 1)].rearrange("b (t p) g d -> p (b t) (g d)", p=P)).then_inc(loaded[2], 16)

            kT_s = xflat[:, 1024:1536]

            def q_s(h2):
                return xflat[:, 1536 + h2 * 512:2048 + h2 * 512]

            def sp_s(h2, s):
                off = 2560 + h2 * 1280 + [0, 512, 896, 1152][s]
                return xflat[:, off:off + (NT - s) * P]

            def a_s(h2, s):
                off = RQ * HW + h2 * HW
                return z[:, s, off:off + (NT - s) * P]

            def xk(w):
                return arena[:, 4672 + w * 512:5184 + w * 512]

            win_neg = arena[0:NB * G, 7200:7712]
            tmp3 = work[:, 2048:2560]
            o3b = small[:, 64:192]

            def nmax(u):
                return small[:, 16 + u % 8:17 + u % 8]

            def dens(u):
                t, h2, br = units[u]
                c = 32 + 6 * (t % 2) + 2 + 2 * br + h2
                return small[:, c:c + 1]

            units = [(t, h2, br) for t in range(NT) for h2 in range(2) for br in range(2)]
            blocks = [(h2, s) for h2 in range(2) for s in (3, 2, 1, 0)]
            NBK = len(blocks)

            @block.tensor
            def _(pe):
                ident = cst("ident")

                def turn(source, done_sem, ready_sem, free_sem, before):
                    for t in range(NT + 1):
                        n, r = before + t, rows[t]
                        pe.wait_ge(ready_sem, n + 1) if ready_sem is not None else None
                        if t >= 2:
                            pe.wait_ge(free_sem, n - 1)
                        for k in range(KT):
                            b = 4 + 2 * (t % 2) + k // 4
                            mm = pe.transpose(ps[:, b, (k % 4) * P:(k % 4) * P + r], source(t, k), ident[0:r, 0:r])
                        mm.then_inc(done_sem, 1)

                def project(n, slot, width=CH):
                    for t in range(NT):
                        pe.wait_ge(bank_free, n * 5 + (t + 1))
                        for k in range(KT):
                            mm = pe.matmul(ps[:, t, 0:width], xnT[:, k, t * P:(t + 1) * P], wring[:, slot, k, 0:width],
                                           start=(k == 0), stop=(k == KT - 1))
                        mm.then_inc(mm_done, 1)
                    pe.wait_ge(bank_free, n * 5 + (NT + 1))
                    for k in range(KT):
                        for row, a, e in quarters(0, width):
                            mm = pe.matmul(ps[row:row + NB, NT, 0:e - a], xnT[:, k, SEQ:SEQ + NB], wring[:, slot, k, a:e],
                                           start=(k == 0), stop=(k == KT - 1))
                    mm.then_inc(mm_done, 1)

                pe.wait_ge(s_aux, 16)
                turn(lambda t, k: work[0:rows[t], (t % 2) * D + k * P:(t % 2) * D + (k + 1) * P],
                     xt_summed, xn_ready, xnT_ready, 0)
                pe.wait_ge(xnT_ready, 5)
                with pe.Fori(0, NCHUNK0 // 2) as i:
                    for u in range(2):
                        pe.wait_ge(w_loaded[u], i * 16 + 16)
                        project(i * 2 + u, u)

                pe.wait_ge(bank_free, 5 + 5 * NCHUNK0)
                pe.wait_ge(zeroed, 1)
                with pe.Fori(0, NT) as t:
                    v_t = z[:, bass.ds(t, 1), RV * HW:(RV + 1) * HW].rearrange("p a c -> p (a c)")
                    pe.wait_ge(ret_staged, t + 1)
                    for j in range(2 * NHP):
                        mm = pe.transpose(ps[:, j // 4, (j % 4) * P:(j % 4 + 1) * P], qk_st[:, j * P:(j + 1) * P], ident)
                    mm.then_inc(ret_turned, 1)
                    pe.wait_ge(ret_T, t * 3 + 3)
                    for a in range(NHP):
                        mm = pe.matmul(ps[:, 2 + a // 2, (a % 2) * 256:(a % 2) * 256 + 256], kT_r[:, a * P:(a + 1) * P],
                                       qBD[:, a].rearrange("p b n -> p (b n)"), start=True, stop=True)
                    mm.then_inc(ret_att, 1)
                    pe.wait_ge(ret_S, t + 1)
                    pe.wait_ge(ret_attm, t * 2 + 2)
                    for h in range(H):
                        o = ps[:, 4, h * DH:(h + 1) * DH]
                        pe.matmul(o, qBD[:, h // 2, h % 2, :], S_ret[:, h // 2, :], start=True, stop=False)
                        mm = pe.matmul(o, attm[:, h * P:(h + 1) * P], v_t[:, h * DH:(h + 1) * DH], start=False, stop=True)
                    mm.then_inc(ret_o, 1)
                    pe.wait_ge(ret_kd, t + 1)
                    for a in range(NHP):
                        mm = pe.matmul(ps[:, 5, a * P:(a + 1) * P], kd[:, a * P:(a + 1) * P], v_t[:, a * P:(a + 1) * P],
                                       start=True, stop=True)
                    mm.then_inc(ret_kv, 1)

                for j in range(2 * NHP):
                    src = z[0:NB, NT, RQ * HW + j * P:RQ * HW + (j + 1) * P]
                    mm = pe.transpose(ps[:, 6, j * NB:(j + 1) * NB], src, ident[0:NB, 0:NB])
                mm.then_inc(rs_turned, 1)
                pe.wait_ge(ds_sp, 1)
                pe.matmul(ps[:, 7, :], cst("tri_neg"), spz, start=True, stop=False)
                pe.matmul(ps[:, 7, :], cst("ones_neg"), tail, start=False, stop=True).then_inc(ds_la, 1)
                pe.wait_ge(rs_t, 1)
                for j in range(4):
                    mm = pe.matmul(ps[0:2, j, :], cst("half_ones"), B_rs[:, j * 512:(j + 1) * 512], start=True, stop=True)
                mm.then_inc(rs_sum, 1)
                pe.wait_ge(rs_row, 1)
                pe.wait_ge(ds_lasum, 1)
                pe.wait_ge(ret_done, NT)

                pe.wait_ge(zeroed, 2)
                with pe.Fori(0, NHP) as i:
                    pe.wait_ge(sb_staged, i + 1)
                    for w in range(2):
                        for t in range(NT):
                            mm = pe.transpose(ps[:, w, t * P:(t + 1) * P], xflat[:, (2 * t + w) * P:(2 * t + w + 1) * P], ident)
                    mm.then_inc(sb_turned, 1)
                    pe.wait_ge(sb_T, i * 3 + 3)

                    def scores(j):
                        h2, s = blocks[j]
                        pe.wait_ge(sb_sp, i * NBK + (j + 1))
                        pe.matmul(ps[:, 2 + j % 2, 0:(NT - s) * P], kT_s[:, s * P:(s + 1) * P], q_s(h2)[:, s * P:SEQ],
                                  start=True, stop=True).then_inc(sb_z, 1)

                    def values(h2):
                        pe.wait_ge(sb_a, i * NBK + (4 * h2 + 6))
                        pe.wait_ge(sb_mixed, i * 2 + (h2 + 1))
                        for t in range(NT):
                            for s in range(t + 1):
                                mm = pe.matmul(ps[:, 6, (NT * h2 + t) * DH:(NT * h2 + t + 1) * DH], a_s(h2, s)[:, (t - s) * P:(t - s + 1) * P],
                                               z[:, s, bass.ds(i * P + (SV * HW + h2 * DH), DH)], start=(s == 0), stop=(s == t))
                        mm.then_inc(sb_o, 1)

                    def sample_page(j):
                        if j % NPG == 0:
                            pe.wait_ge(ds_stage, i + 1)
                            pe.wait_ge(ds_om, i * 2 + (j // NPG + 1))
                        pe.wait_ge(page_loaded[j % 4], i * 64 + 16 * (NB * NPG // 4 + j // 4 + 1))
                        row = j % 4 * 32
                        pe.matmul(ps[row:row + 32, 7, :], a_st[:, j, :], pages[:, j % 4, :],
                                  start=(j % NPG < 4), stop=(j % NPG >= 4)).then_inc(page_free, 1)

                    scores(0)
                    scores(1)
                    for j, (h2, s) in enumerate(blocks):
                        N = (NT - s) * P
                        bank = 4 + j % 2
                        pe.wait_ge(sb_sp, i * NBK + (j + 3))
                        pe.wait_ge(sb_a, i * NBK + (j + 1))
                        pe.matmul(ps[:, bank, 0:N], cst("tri_neg"), sp_s(h2, s), start=True, stop=False)
                        for j2 in range(s + 1, NT):
                            pe.matmul(ps[:, bank, (j2 - s) * P:N], cst("ones_neg"), sp_s(h2, j2), start=False, stop=False)
                        pe.matmul(ps[:, bank, 0:N], kT_s[:, s * P:(s + 1) * P], q_s(h2)[:, s * P:SEQ],
                                  start=False, stop=True).then_inc(sb_la, 1)
                        if j + 2 < NBK:
                            scores(j + 2)
                        if j == 4:
                            values(0)
                        sample_page(2 * j)
                        sample_page(2 * j + 1)
                    values(1)
                pe.wait_ge(ds_om, NB + 1)
                for b in range(NB):
                    mm = pe.matmul(ps[0:NB, 1, :], cst("to_row")[:, b * NB:(b + 1) * NB], om[:, b * HW:(b + 1) * HW],
                                   start=(b == 0), stop=(b == NB - 1))
                mm.then_inc(ds_row, 1)

                pe.wait_ge(ds_mixed, 1)
                pe.wait_ge(rs_done, 1)
                pe.wait_ge(sb_mixed, H + 2)
                turn(lambda t, k: z[0:rows[t], t, ((RG if k < 4 else SG) * HW + (k % 4) * P):((RG if k < 4 else SG) * HW + (k % 4 + 1) * P)],
                     mix_turned, None, mix_T, 0)
                pe.wait_ge(mix_T, 5)
                for u in range(2):
                    pe.wait_ge(w_loaded[u], 16 * 5)
                    project(NCHUNK0 + u, u)

                turn(lambda t, k: work[0:rows[t], (t % 2) * D + k * P:(t % 2) * D + (k + 1) * P],
                     xt_summed, xn_ready, xnT_ready, 5)
                pe.wait_ge(xnT_ready, 10)
                with pe.Fori(0, 2) as i:
                    for u in range(2):
                        pe.wait_ge(w_loaded[u], i * 16 + 16 * 6)
                        project(i * 2 + (10 + u), u)
                for u in range(2):
                    pe.wait_ge(w_loaded[u], 16 * 8)
                    project(14 + u, u, (CH, W1 - 5 * CH)[u])

                pe.sem_inc(cm_turned, 2)
                for w in range(2):
                    with pe.Fori(0, NB) as b:
                        for q in range(2):
                            pe.wait_ge(cm_loaded[q], b * 64 + 64 * (8 * w + 1))
                            pe.wait_ge(cm_T, b * 2 + (16 * w + q + 1))
                            for m in range(4):
                                mm = pe.transpose(ps[:, 5 + q, m * P:(m + 1) * P], slot1[:, q, m * P:(m + 1) * P], ident)
                            mm.then_inc(cm_turned, 1)
                    if w == 0:
                        pe.wait_ge(bank_free, 5 + 80)
                    else:
                        pe.wait_ge(cmp_T, 1)
                    for t in range(NT):
                        col = (KC, VC)[w]
                        mm = pe.transpose(ps[:, 4, t * P:(t + 1) * P], z[:, t, col:col + P], ident)
                    mm.then_inc(cmp_turned, 1)
                    pe.wait_ge(cm_T, 2 + 16 * (w + 1))
                    pe.wait_ge(cmp_T, w + 1)
                    pe.wait_ge(wcmp_loaded[w], 32)
                    for l in range(CB):
                        mm = pe.matmul(ps[:, 7 if w == 0 else 3, 0:N_CMP], wcmp[w][:, l, :], kcT[:, l, :], start=(l == 0), stop=(l == CB - 1))
                    mm.then_inc(cm_proj, 1)
                    if w == 0:
                        pe.wait_ge(cm_sq, 1)
                        pe.matmul(ps[:, 2, 0:N_CMP], cst("mean_ones"), rk1, start=True, stop=True).then_inc(cm_mean, 1)
                pe.wait_ge(cvT_ready, 2)
                for j in range(2):
                    pe.transpose(ps[:, 4, j * P:(j + 1) * P], cvT[:, j * P:(j + 1) * P], ident)
                pe.transpose(ps[:, 4, 2 * P:3 * P], cvT_pair, ident).then_inc(cv_turned, 1)

                pe.wait_ge(heads_ready, 2)
                pe.wait_ge(ckT_ready, 1)
                for w in range(2):
                    for t in range(NT):
                        col = (KS, KW)[w]
                        mm = pe.transpose(ps[:, w, t * P:(t + 1) * P], z[:, t, col:col + P], ident)
                mm.then_inc(kz_turned, 1)
                pe.wait_ge(kz_T, 2)
                for w in range(2):
                    pe.matmul(ps[:, 5 + w, :], cst("swap"), xk(w), start=True, stop=True)
                pe.matmul(ps[:, 7, 0:NPB], cst("swap"), ckT[:, NB * NCB:N_CMP], start=True, stop=True).then_inc(kz_swapped, 1)

                pe.wait_ge(kz_ready, 1)
                pe.wait_ge(cv_ready, 1)
                with pe.Fori(0, HN // 2) as i:
                    g = i // 4
                    pe.wait_ge(nq_staged, i + 1)
                    for t in range(NT):
                        mm = pe.transpose(ps[:, 4, t * P:(t + 1) * P], q_tok[:, t * P:(t + 1) * P], ident)
                    mm.then_inc(nq_turned, 1)
                    pe.wait_ge(nq_T, i + 1)
                    for t in range(NT):
                        for h2 in range(2):
                            mm = pe.matmul(ps[:, 5, (2 * t + h2) * NPB:(2 * t + h2 + 1) * NPB], qTs[:, t * P:(t + 1) * P],
                                           Kz[:, bass.ds(g, 1), h2, 2 * SEQ:KZ], start=True, stop=True)
                    mm.then_inc(nc_s, 1)

                    def s1(u):
                        t, h2, br = units[u]
                        N = (t + 1) * P
                        pe.wait_ge(n_p, i * 16 + (u + 1))
                        pe.matmul(ps[:, u % 4, 0:N], qTs[:, t * P:(t + 1) * P], Kz[:, bass.ds(g, 1), h2, br * SEQ:br * SEQ + N],
                                  start=True, stop=True).then_inc(n_s, 1)

                    def turn_p(u):
                        t, h2, br = units[u]
                        pe.wait_ge(n_p, i * 16 + (u + 5))
                        pe.wait_ge(n_pt[br], i * 8 + (u // 2 + 1))
                        for s in range(t + 1):
                            mm = pe.transpose(ps[:, 4 + br, s * P:(s + 1) * P], z[:, u % 4, P_OFF + s * P:P_OFF + (s + 1) * P], ident)
                        mm.then_inc(n_t, 1)

                    def av(u):
                        t, h2, br = units[u]
                        pe.wait_ge(n_pt[br], i * 8 + (u // 2 + 2))
                        if u % 4 == 0:
                            pe.wait_ge(n_o, i * 4 + (t + 1))
                            pe.matmul(ps[:, 6 + t % 2, 0:P], p_cmpT[:, t * P:(t + 1) * P],
                                      cv_pair.rearrange("p (g c) -> p g c", g=G)[:, bass.ds(g, 1), :], start=True, stop=True)
                        for s in range(t + 1):
                            col = (VS, VW)[br]
                            mm = pe.matmul(ps[:, 6 + t % 2, P + br * P + h2 * DH:P + br * P + (h2 + 1) * DH],
                                           z[:, u % 4, PT_OFF + s * P:PT_OFF + (s + 1) * P],
                                           z[:, s, bass.ds(g * DH + col, DH)], start=(s == 0), stop=(s == t))
                        mm.then_inc(n_av, 1)

                    s1(0)
                    s1(1)
                    pe.wait_ge(nc_p, i + 1)
                    for t in range(NT):
                        mm = pe.transpose(ps[:, 4, t * P:(t + 1) * P], p_cmp[:, t].rearrange("p u n -> p (u n)"), ident)
                    mm.then_inc(nc_turned, 1)
                    pe.wait_ge(nc_T, i + 1)
                    for u in range(16):
                        if u + 2 < 16:
                            s1(u + 2)
                        turn_p(u)
                        if u:
                            av(u - 1)
                    av(15)

                pe.wait_ge(r_back, 48)
                pe.matmul(ps[:, 0, 0:4 * DH], cst("spread", NB * G), kn_bg, start=True, stop=True).then_inc(*marks_pe.next("r_spread"))
                pe.wait_ge(*marks_dve.at("r_dup"))
                pe.transpose(ps[:, 1, 0:P], q_dup, ident).then_inc(*marks_pe.next("r_turned"))
                pe.wait_ge(*marks_act.at("r_QT"))
                pe.matmul(ps[:, 2, 0:NB * NCB], QT, ckT[:, 0:NB * NCB], start=True, stop=True).then_inc(*marks_pe.next("i_s"))
                pe.wait_ge(*marks_dve.at("i_p"))
                for j in range(2):
                    pe.transpose(ps[:, 3, j * P:(j + 1) * P], p_imp[:, j * P:(j + 1) * P], ident)
                pe.matmul(ps[0:NB * G, 5, 0:NB * NCB], cst("group_sum"), p_imp, start=True, stop=True).then_inc(*marks_pe.next("i_sum"))
                pe.wait_ge(*marks_act.at("i_T"))
                for j in range(2):
                    mm = pe.matmul(ps[:, 7, 0:P], p_impT[:, j], cv_s[:, j * P:(j + 1) * P], start=(j == 0), stop=(j == 1))
                mm.then_inc(*marks_pe.next("i_o"))
                pe.wait_ge(*marks_dve.at("i_neg"))
                pe.wait_ge(*marks_dve.at("i_zero"))
                pe.wait_ge(*marks_dve.at("r_kn"))
                neg = small[0:NB * G, 64:80]
                for j in range(2):
                    pe.matmul(ps[:, j, :], cst("spread", NB * G),
                              bc(neg[:, 8 * j:8 * j + 8].unsqueeze(2), [NB * G, 8, DH]), start=True, stop=False, skip_group_check=True)
                pe.matmul(ps[:, 2, :], cst("spread", NB * G), win_neg, start=True, stop=False, skip_group_check=True)
                pe.sem_inc(sk_turned, 3)
                pe.sem_inc(sk_scored, 3)
                with pe.Fori(0, NB) as b:
                    def turn_k(q):
                        pe.wait_ge(sk_loaded[q], (b * 64 + 64) if q < 2 else (b * 16 + 16))
                        pe.wait_ge(sk_T, b * 3 + (q + 1))
                        for m in range(4):
                            mm = pe.transpose(ps[:, 4 + q, m * P:(m + 1) * P], slot1[:, q, m * P:(m + 1) * P], ident)
                        mm.then_inc(sk_turned, 1)
                    turn_k(0)
                    turn_k(1)
                    turn_k(2)
                    pe.wait_ge(sk_q, b + 1)
                    for q in range(3):
                        pe.wait_ge(sk_T, b * 3 + (q + 4))
                        pe.matmul(ps[:, q, :], q_st, KTs[:, q], start=False, stop=False, skip_group_check=True).then_inc(sk_scored, 1)
                pe.sem_inc(sv_used, 3)
                pe.wait_ge(*marks_act.at("sk_exp"))
                for j in range(12):
                    mm = pe.transpose(ps[:, 4 + j // 4, (j % 4) * P:(j % 4 + 1) * P], Pexp[:, j * P:(j + 1) * P], ident)
                mm.then_inc(*marks_pe.next("sk_pturned"))
                pe.wait_ge(*marks_act.at("sk_PT"))
                with pe.Fori(0, NB) as b:
                    for q in range(3):
                        pe.wait_ge(sv_loaded[q], (b * 64 + 64) if q < 2 else (b * 16 + 16))
                        for m in range(4):
                            j = 4 * q + m
                            mm = pe.matmul(ps[:, 0 if q < 2 else 1, bass.ds(b * HN, HN)], slot1[:, q, m * P:(m + 1) * P],
                                           PT1[:, j, bass.ds(b * HN, HN)], start=(j in (0, 8)), stop=(j in (7, 11)))
                        mm.then_inc(sv_used, 1)
                pe.wait_ge(*marks_dve.at("sv_oT"))
                for w in range(2):
                    mm = pe.transpose(ps[:, 2, w * P:(w + 1) * P], oT1[:, w], ident)
                mm.then_inc(*marks_pe.next("sv_back"))

                pe.wait_ge(n_o, 2 + 4 * (HN // 2))
                pe.wait_ge(*marks_dve.at("sv_done"))
                turn(lambda t, k: z[0:rows[t], t, GATE + k * P:GATE + (k + 1) * P], mix_turned, None, mix_T, 5)
                pe.wait_ge(mix_T, 10)
                for u in range(2):
                    pe.wait_ge(w_loaded[u], 16 * 9)
                    project(16 + u, u)

            @block.scalar
            def _(act):
                st = Steps(act, act_step)

                def rsqrt(a, n, sem_, value):
                    st.done(nc.scalar.activation(a, a, ACT.Ln, bias=EPS, scale=1.0 / n))
                    nc.scalar.activation(a, a, ACT.Exp, scale=-0.5).then_inc(sem_, 1)
                    act.wait_ge(sem_, value)

                def norm_x(layer):
                    for t in range(NT + 1):
                        r = rows[t]
                        st.done(nc.scalar.activation(work[0:r, 2 * D:3 * D], xres[0:r, t, :], ACT.Square,
                                                     accum_out=stats[0:r, 80 + t:81 + t]))
                    rsqrt(stats[:, 80:85], D, rstd_x, layer + 1)
                    for t in range(NT + 1):
                        r, n = rows[t], 5 * layer + t
                        if t >= 2:
                            act.wait_ge(xt_summed, n - 1)
                        nc.scalar.activation(work[0:r, (t % 2) * D:(t % 2 + 1) * D], xres[0:r, t, :], ACT.Copy,
                                             scale=stats[0:r, 80 + t:81 + t]).then_inc(xn_ready, 1)

                LOG_EXP = "natural_log_exp_and_others"
                nc.scalar.preload_act_table_set(LOG_EXP)
                act.wait_ge(s_x, 32)
                act.wait_ge(zeroed_stats, 1)
                norm_x(0)
                act.sem_inc(bank_free, 5)
                for n in range(NCHUNK0):
                    if n == 0:
                        act.wait_ge(xn_ready, 5)
                        act.wait_ge(xnT_ready, 5)
                    for t in range(NT + 1):
                        act.wait_ge(mm_done, 5 * n + t + 1)
                        for row, a, e in (quarters(0, CH) if t == NT else [(0, 0, CH)]):
                            ins_ = nc.scalar.activation(sec(t, n)[:, a:e], ps[row:row + rows[t], t, 0:e - a],
                                                        ACT.Silu if n in (SG, RG) else ACT.Copy)
                        ins_.then_inc(bank_free, 1)
                    if n in (SQ, SK):
                        act.wait_ge(ssq_ready, n + 1)
                        rsqrt(stats[:, 0:40], DH, rstd_ready, n + 1)
                        if n == SQ:
                            act.wait_ge(sections_ready, 1)
                            act.dma_start(d_sq, sec(NT, SQ)).then_inc(sq_sent, 16)
                            act.wait_ge(sq_sent, 16)
                            act.dma_start(arena[:, NX:NX + NQ], d_sq.rearrange("(o b) c -> o (b c)", o=1)[0].partition_broadcast(P)).then_inc(sq_spread, 16)

                def softplus_tail(src, dst, sem_):
                    st.done(nc.scalar.activation(dst, src, ACT.Abs))
                    st.done(nc.scalar.activation(dst, dst, ACT.Exp, scale=-1.0))
                    nc.scalar.activation(dst, dst, ACT.Ln, bias=1.0).then_inc(sem_, 1)

                nc.scalar.preload_act_table_set(LOG_EXP)
                act.wait_ge(ds_scores, 1)
                softplus_tail(zs, lnz, ds_ln)

                act.wait_ge(sections_ready, 4)
                act.wait_ge(bank_free, 5 + 5 * NCHUNK0)
                with st.loop(NT, 1) as t:
                    nc.scalar.activation(qk_st.rearrange("p (a c) -> p a c", a=1), z[:, bass.ds(t, 1), RQ * HW:(RK + 1) * HW],
                                         ACT.Copy).then_inc(ret_staged, 1)
                    act.wait_ge(ret_turned, t + 1)
                    for u in range(2):
                        half = slice(u * DH, (u + 1) * DH)
                        nc.scalar.activation(qBD[half, :, u, :], ps[half, 0, :].rearrange("p (a n) -> p a n", a=NHP), ACT.Copy).then_inc(ret_T, 1)
                    nc.scalar.activation(kT_r, ps[:, 1, :], ACT.Copy).then_inc(ret_T, 1)
                    act.wait_ge(gn_sum, t + 1)
                    st.done(nc.scalar.activation(stats[:, 40:48], stats[:, 40:48], ACT.Ln, bias=EPS, scale=1.0 / DH))
                    nc.scalar.activation(stats[:, 40:48], stats[:, 40:48], ACT.Exp, scale=-0.5).then_inc(gn_rstd, 1)
                    act.wait_ge(ret_o, t + 1)
                    act.wait_ge(ret_kd, t + 1)
                act.wait_ge(rs_sum, 1)
                nc.scalar.activation(B_rs[0:2].rearrange("p (a c) -> p a c", a=4), ps[0:2, 0:4, :], ACT.Copy).then_inc(rs_row, 1)
                act.wait_ge(ds_lasum, 1)
                nc.scalar.activation(zs, zs, ACT.Exp).then_inc(ds_a, 1)

                act.wait_ge(ds_a, 1)
                act.wait_ge(zeroed, 2)
                act.sem_inc(sb_a, 2)
                with st.loop(NHP, 2 * NBK) as i:
                    act.wait_ge(page_free, i * 2 * NPG + (4 + NB * NPG))
                    nc.scalar.activation(a_st[:, :, 0:H], zs[:, bass.ds(i * 2 * NPG * H, 2 * NPG * H)].rearrange("p (j h) -> p j h", h=H),
                                         ACT.Copy).then_inc(ds_stage, 1)
                    nc.scalar.activation(xflat[:, 0:1024].rearrange("p (t w c) -> p t w c", t=NT, w=2),
                                         z[:, 0:NT, 0:2 * HW].rearrange("p t (w c) -> p t w c", w=2)[:, :, :, bass.ds(i * P, P)],
                                         ACT.Copy).then_inc(sb_staged, 1)
                    act.wait_ge(sb_turned, i + 1)
                    for u in range(2):
                        half = slice(u * DH, (u + 1) * DH)
                        nc.scalar.activation(q_s(u)[half], ps[half, 0, :], ACT.Copy, scale=SCALE).then_inc(sb_T, 1)
                    nc.scalar.activation(kT_s, ps[:, 1, :], ACT.Copy).then_inc(sb_T, 1)

                    def tail_of(j):
                        h2, s = blocks[j]
                        act.wait_ge(sb_z, i * NBK + (j + 1))
                        act.wait_ge(sb_sp, i * NBK + (j + 1))
                        softplus_tail(ps[:, 2 + j % 2, 0:(NT - s) * P], (tmp, tmp2)[j % 2][:, 0:(NT - s) * P], sb_ln)

                    tail_of(0)
                    for j, (h2, s) in enumerate(blocks):
                        if j + 1 < NBK:
                            tail_of(j + 1)
                        act.wait_ge(sb_masked, i * NBK + (j + 1))
                        act.wait_ge(sb_mixed, i * 2 + (h2 + 1))
                        nc.scalar.activation(a_s(h2, s), ps[:, 4 + j % 2, 0:(NT - s) * P], ACT.Exp).then_inc(sb_a, 1)

                act.wait_ge(gn_sum, NT + 1)
                rsqrt(stats[0:NB, 40:48], DH, gn_rstd, NT + 1)
                act.wait_ge(w_loaded[0], 16 * 5)
                for t in range(NT + 1):
                    act.wait_ge(mix_turned, t + 1)
                    b, r = 4 + 2 * (t % 2), rows[t]
                    nc.scalar.activation(xnT[:, :, t * P:t * P + r],
                                         ps[:, b:b + 2, :].rearrange("p b (k n) -> p (b k) n", k=4)[:, :, 0:r], ACT.Copy).then_inc(mix_T, 1)

                nc.scalar.preload_act_table_set(LOG_EXP)
                act.wait_ge(bank_free, 5 + 50)
                norm_x(1)
                for c in range(NC1):
                    n = 10 + c
                    w = min(CH, W1 - c * CH)
                    lo, hi = min(max(GATE - c * CH, 0), w), min(max(BG - c * CH, 0), w)
                    parts = [(0, lo, ACT.Copy), (lo, hi, ACT.Silu), (hi, w, ACT.Sigmoid)]
                    parts = [x for x in parts if x[1] > x[0]]
                    for k, (a, e, f) in enumerate(parts):
                        for t in range(NT + 1):
                            act.wait_ge(mm_done, 5 * n + t + 1)
                            if t < NT:
                                ins_ = nc.scalar.activation(z[:, t, c * CH + a:c * CH + e], ps[:, t, a:e], f)
                            else:
                                for row, a2, e2 in quarters(a, e):
                                    ins_ = nc.scalar.activation(z[0:NB, NT, c * CH + a2:c * CH + e2], ps[row:row + NB, NT, 0:e2 - a2], f)
                            if k == len(parts) - 1:
                                ins_.then_inc(bank_free, 1)
                    if c in (1, 3):
                        act.wait_ge(k_ssq, (c + 1) // 2)
                        rsqrt(stats[:, 0:80], DH, k_rstd, (c + 1) // 2)
                nc.scalar.preload_act_table_set(LOG_EXP)
                act.wait_ge(s_table, 16)
                with act.Fori(0, NB) as b:
                    act.wait_ge(cm_turned, b * 2 + 2)
                    page_group(act, "cache_cmp_k", b * NPG + 4, slot1[:, 1], cm_loaded[1])
                for b in range(1):
                    act.wait_ge(cm_turned, 18)
                    page_group(act, "cache_cmp_v", 4, slot1[:, 1], cm_loaded[1])
                act.wait_ge(cm_mean, 1)
                st.done(nc.scalar.activation(rk1, ps[:, 2, 0:N_CMP], ACT.Ln, bias=EPS))
                nc.scalar.activation(rk1, rk1, ACT.Exp, scale=-0.5).then_inc(cm_rstd, 1)
                with act.Fori(1, NB) as b:
                    act.wait_ge(cm_turned, b * 2 + 18)
                    page_group(act, "cache_cmp_v", b * NPG + 4, slot1[:, 1], cm_loaded[1])
                act.wait_ge(cm_proj, 2)
                nc.scalar.activation(cvT[:, 0:N_CMP], ps[:, 3, 0:N_CMP], ACT.Copy).then_inc(cvT_ready, 1)
                act.wait_ge(kz_turned, 1)
                for w in range(2):
                    nc.scalar.activation(xk(w), ps[:, w, :], ACT.Copy).then_inc(kz_T, 1)

                act.wait_ge(kz_ready, 1)
                act.sem_inc(n_p, 4)
                act.sem_inc(n_pt[1], 1)
                with st.loop(HN // 2, 0) as i:
                    nc.scalar.activation(q_tok.rearrange("p (t c) -> p t c", t=NT), z[:, 0:NT, bass.ds(i * P, P)], ACT.Copy).then_inc(nq_staged, 1)
                    act.wait_ge(nq_turned, i + 1)
                    nc.scalar.activation(qTs, ps[:, 4, :], ACT.Copy, scale=SCALE).then_inc(nq_T, 1)
                    act.wait_ge(nc_max, i + 1)
                    nc.scalar.activation(p_cmp[:, :, :, 0:NPB], p_cmp[:, :, :, 0:NPB], ACT.Exp).then_inc(nc_exp, 1)
                    act.wait_ge(nc_turned, i + 1)
                    nc.scalar.activation(p_cmpT, ps[:, 4, :], ACT.Copy).then_inc(nc_T, 1)

                    def exp(u):
                        t, h2, br = units[u]
                        N = (t + 1) * P
                        act.wait_ge(n_max, i * 16 + (u + 1))
                        act.wait_ge(n_t, i * 16 + (u + 1))
                        if u % 4 == 0:
                            act.wait_ge(n_o, i * 4 + (t + 1))
                        nc.scalar.activation(z[:, u % 4, P_OFF:P_OFF + N], ps[:, u % 4, 0:N], ACT.Exp, bias=nmax(u),
                                             accum_out=dens(u)).then_inc(n_p, 1)

                    exp(0)
                    for u in range(16):
                        t, h2, br = units[u]
                        if u + 1 < 16:
                            exp(u + 1)
                        if br == 1:
                            act.wait_ge(n_t, i * 16 + (u + 5))
                            act.wait_ge(n_av, i * 16 + (u + 1))
                            N = (t + 1) * P
                            nc.scalar.activation(z[:, u % 4, PT_OFF:PT_OFF + N], ps[:, 5, 0:N], ACT.Copy).then_inc(n_pt[1], 1)

                act.wait_ge(*marks_pe.at("r_turned"))
                nc.scalar.activation(QT, ps[:, 1, 0:P], ACT.Copy).then_inc(*marks_act.next("r_QT"))
                act.wait_ge(*marks_dve.at("i_max"))
                nc.scalar.activation(p_imp, p_imp, ACT.Exp, bias=stats[:, 4:5], accum_out=stats[:, 5:6]).then_inc(*marks_act.next("i_exp"))
                act.wait_ge(*marks_pe.at("i_sum"))
                nc.scalar.activation(arena[:, 4864:5120], ps[:, 3, 0:2 * P], ACT.Copy).then_inc(*marks_act.next("i_T"))
                act.wait_ge(*marks_dve.at("r_pad"))
                with act.Fori(0, NB) as b:
                    act.wait_ge(sk_turned, b * 3 + 2)
                    page_group(act, "cache_sel_k", b * NPG + 4, slot1[:, 1], sk_loaded[1])
                    act.wait_ge(sk_scored, b * 3 + 3)
                    nc.scalar.activation(q_st, Qpad[:, bass.ds(b * P, P)], ACT.Copy).then_inc(sk_q, 1)
                act.wait_ge(*marks_dve.at("sk_max"))
                sel, win = ps[:, 0:2, :].rearrange("p a c -> p (a c)"), ps[:, 2, :]
                st.done(nc.scalar.activation(Pexp[:, 0:1024], sel, ACT.Exp, bias=stats[:, 8:9], accum_out=stats[:, 12:13]))
                st.done(nc.scalar.activation(Pexp[:, 1024:1536], win, ACT.Exp, bias=stats[:, 9:10], accum_out=stats[:, 13:14]))
                nc.scalar.activation(stats[:, 14:16], stats[:, 6:8], ACT.Exp).then_inc(*marks_act.next("sk_exp"))
                act.wait_ge(*marks_pe.at("sk_pturned"))
                nc.scalar.activation(PT1.rearrange("p (q m) c -> p q (m c)", q=3), ps[:, 4:7, :], ACT.Copy).then_inc(*marks_act.next("sk_PT"))
                with act.Fori(0, NB) as b:
                    act.wait_ge(sv_used, b * 3 + 2)
                    page_group(act, "cache_sel_v", b * NPG + 4, slot1[:, 1], sv_loaded[1])
                for t in range(NT + 1):
                    act.wait_ge(mix_turned, 5 + t + 1)
                    b, r = 4 + 2 * (t % 2), rows[t]
                    nc.scalar.activation(xnT[:, :, t * P:t * P + r],
                                         ps[:, b:b + 2, :].rearrange("p b (k n) -> p (b k) n", k=4)[:, :, 0:r], ACT.Copy).then_inc(mix_T, 1)

            @block.vector
            def _(dve):
                st = Steps(dve, dve_step)
                TT, TS, STT, RED = (nc.vector.tensor_tensor, nc.vector.tensor_scalar,
                                    nc.vector.scalar_tensor_tensor, nc.vector.tensor_reduce)
                nc.vector.memset(stats[:], 1.0).then_inc(zeroed_stats, 1)
                dve.wait_ge(zeroed_stats, 1)
                dve.wait_ge(s_aux, 16)

                def turned_x(layer):
                    gain = cst(f"gain_in{layer}")
                    for t in range(NT + 1):
                        r, n = rows[t], 5 * layer + t
                        dve.wait_ge(xt_summed, n + 1)
                        b = 4 + 2 * (t % 2)
                        TT(xnT[:, :, t * P:t * P + r], ps[:, b:b + 2, :].rearrange("p b (k n) -> p (b k) n", k=4)[:, :, 0:r],
                           bc(gain.unsqueeze(2), [P, KT, r]), ALU.mult).then_inc(xnT_ready, 1)

                turned_x(0)
                st.done(nc.vector.memset(S_ret[:], 0.0))
                dve.sem_inc(ret_S, 1)
                dve.wait_ge(xn_ready, 5)
                st.done(nc.vector.memset(qBD[0:DH, :, 1, :], 0.0))
                nc.vector.memset(qBD[DH:P, :, 0, :], 0.0).then_inc(zeroed, 1)
                dve.wait_ge(xt_summed, 5)

                def head_norm(n, gain):
                    dve.wait_ge(bank_free, 5 + 5 * (n + 1))
                    for t in range(NT + 1):
                        r = rows[t]
                        st.done(TT(tmp[0:r], sec(t, n), sec(t, n), ALU.mult))
                        red = RED(stats[0:r, 8 * t:8 * t + 8], heads(tmp[0:r]), AX.X, ALU.add)
                        if t < NT:
                            st.done(red)
                        else:
                            red.then_inc(ssq_ready, 1)
                    dve.wait_ge(rstd_ready, n + 1)
                    for t in reversed(range(NT + 1)):
                        r = rows[t]
                        st.done(TT(heads(sec(t, n)), heads(sec(t, n)), bc(stats[0:r, 8 * t:8 * t + 8].unsqueeze(2), [r, H, DH]), ALU.mult))
                        mul = TT(heads(sec(t, n)), heads(sec(t, n)), bc(cst(gain, r).unsqueeze(1), [r, H, DH]), ALU.mult)
                        if t:
                            st.done(mul)
                        else:
                            mul.then_inc(sections_ready, 1)
                            dve.wait_ge(sections_ready, n + 1)

                head_norm(SQ, "gain_sq")
                head_norm(SK, "gain_sk")

                dve.wait_ge(sq_spread, 16)
                with st.loop(NB * NPG // 4, 4) as r:
                    for u in range(4):
                        dve.wait_ge(page_loaded[u], r * 16 + 16)
                        TT(tmp.rearrange("p (a c) -> p a c", a=1), pages[:, u:u + 1, :], qbc[:, bass.ds(r // 2, 1), :], ALU.mult).then_inc(page_free, 1)
                        dve.wait_ge(page_free, r * 4 + (4 + u + 1))
                        st.done(RED(zs[:, bass.ds(r * 4 * H + u * H, H)], heads(tmp), AX.X, ALU.add))
                TS(zs, zs, SCALE, None, ALU.mult).then_inc(ds_scores, 1)
                dve.wait_ge(ds_scores, 1)

                def rotate(n, value):
                    dve.wait_ge(bank_free, 5 + 5 * (n + 1))
                    hf = DH // 2
                    for t in range(NT + 1):
                        r = rows[t]
                        x = heads(sec(t, n))
                        cos = bc(cst("cosine", r)[:, t * DH:(t + 1) * DH].unsqueeze(1), [r, H, DH])
                        sin = cst("sine", r)[:, t * DH:(t + 1) * DH]
                        st.done(TT(heads(tmp[0:r]), x, cos, ALU.mult))
                        st.done(TT(heads(tmp2[0:r])[:, :, 0:hf], x[:, :, hf:DH], bc(sin[:, 0:hf].unsqueeze(1), [r, H, hf]), ALU.mult))
                        st.done(TT(heads(tmp2[0:r])[:, :, hf:DH], x[:, :, 0:hf], bc(sin[:, hf:DH].unsqueeze(1), [r, H, hf]), ALU.mult))
                        add = TT(sec(t, n), tmp[0:r], tmp2[0:r], ALU.add)
                        if t < NT:
                            st.done(add)
                        else:
                            add.then_inc(sections_ready, 1)
                            dve.wait_ge(sections_ready, value)

                rotate(RQ, 3)
                rotate(RK, 4)
                dve.wait_ge(ds_ln, 1)
                st.done(STT(spz, zs, 0.0, lnz, ALU.max, ALU.add))
                pg = lambda a, j: a.rearrange("p (b j h) -> p b j h", b=NB, j=NPG)[:, :, j, :]
                st.done(nc.vector.memset(pg(tail, NPG - 1), 0.0))
                for j in reversed(range(NPG - 1)):
                    add = TT(pg(tail, j), pg(tail, j + 1), pg(spz, j + 1), ALU.add)
                    if j:
                        st.done(add)
                    else:
                        add.then_inc(ds_sp, 1)

                def group_norm(o, r, gate, n, sem_, wait=None):
                    mean, var = stats[0:r, 48:56], stats[0:r, 40:48]
                    st.done(RED(mean, heads(o), AX.X, ALU.add))
                    st.done(TS(mean, mean, 1.0 / DH, None, ALU.mult))
                    st.done(TT(heads(o), heads(o), bc(mean.unsqueeze(2), [r, H, DH]), ALU.subtract))
                    st.done(TT(tmp[0:r], o, o, ALU.mult))
                    RED(var, heads(tmp[0:r]), AX.X, ALU.add).then_inc(gn_sum, 1)
                    dve.wait_ge(gn_rstd, n)
                    st.done(TT(heads(o), heads(o), bc(var.unsqueeze(2), [r, H, DH]), ALU.mult))
                    st.done(TT(o, o, cst("gain_ret", r), ALU.mult))
                    TT(gate, gate, o.rearrange("p (a c) -> p a c", a=1), ALU.mult).then_inc(sem_, 1)

                dve.wait_ge(bank_free, 5 + 5 * NCHUNK0)
                with st.loop(NT, 9) as t:
                    dve.wait_ge(ret_att, t + 1)
                    for j in range(2):
                        TT(attm[:, j * 512:(j + 1) * 512], ps[:, 2 + j, :], cst("ret_decay")[:, j * 512:(j + 1) * 512], ALU.mult).then_inc(ret_attm, 1)
                    dve.wait_ge(ret_o, t + 1)
                    st.done(TT(heads(o_tmp), heads(ps[:, 4, :]), bc(cst("q_decay").unsqueeze(2), [P, H, DH]), ALU.mult))
                    st.done(TT(S_ret[:], S_ret[:], bc(cst("chunk_decay").unsqueeze(2), [P, NHP, DH]), ALU.mult))
                    dve.wait_ge(ret_kv, t + 1)
                    kv = ps[:, 5, :].rearrange("p (a c) -> p a c", a=NHP)
                    st.done(TT(S_ret[0:DH], S_ret[0:DH], kv[0:DH, :, 0:DH], ALU.add))
                    TT(S_ret[DH:P], S_ret[DH:P], kv[DH:P, :, DH:P], ALU.add).then_inc(ret_S, 1)
                    dve.wait_ge(ret_S, t + 2)
                    group_norm(o_tmp, P, z[:, bass.ds(t, 1), RG * HW:(RG + 1) * HW], t + 1, ret_done)
                    dve.wait_ge(ret_done, t + 1)

                dve.wait_ge(rs_turned, 1)
                st.done(nc.vector.tensor_copy(kqT[:], ps[:, 6, 0:2 * NHP * NB]))
                kq = kqT[:].rearrange("p (w a b) -> p w b a", w=2, b=NB)
                dve.wait_ge(rs_in, 16 * 18)
                st.done(TT(by_pair(B_rs), by_pair(B_rs), bc(kq[:, 1].unsqueeze(3), [P, NB, NHP, DH]), ALU.mult))
                st.done(TT(by_pair(A_rs), by_pair(A_rs), bc(cst("gamma").unsqueeze(1).unsqueeze(3), [P, NB, NHP, DH]), ALU.mult))
                STT(A_rs, B_rs, SCALE, A_rs, ALU.mult, ALU.add).then_inc(rs_S, 1)
                dve.wait_ge(rs_S, 1)
                TT(by_pair(B_rs), by_pair(A_rs), bc(kq[:, 0].unsqueeze(3), [P, NB, NHP, DH]), ALU.mult).then_inc(rs_t, 1)
                dve.wait_ge(ds_la, 1)
                TT(zs, zs, ps[:, 7, :], ALU.add).then_inc(ds_lasum, 1)

                st.done(nc.vector.memset(a_st, 0.0))
                st.done(nc.vector.memset(q_s(0)[DH:P], 0.0))
                nc.vector.memset(q_s(1)[0:DH], 0.0).then_inc(zeroed, 1)
                dve.sem_inc(sb_sp, 2)
                dve.sem_inc(sb_mixed, 2)
                dve.sem_inc(ds_om, 1)
                with st.loop(NHP, NBK) as i:
                    def softplus(j):
                        h2, s = blocks[j]
                        N = (NT - s) * P
                        dve.wait_ge(sb_ln, i * NBK + (j + 1))
                        st.done(STT(sp_s(h2, s), ps[:, 2 + j % 2, 0:N], 0.0, (tmp, tmp2)[j % 2][:, 0:N], ALU.max, ALU.add))
                        TT(sp_s(h2, s)[:, 0:P], sp_s(h2, s)[:, 0:P], cst("strict"), ALU.mult).then_inc(sb_sp, 1)

                    def mix(h2):
                        dve.wait_ge(sb_o, i * 2 + (h2 + 1))
                        gate = z[:, 0:NT, bass.ds(i * P + (SG * HW + h2 * DH), DH)]
                        TT(gate, gate, ps[:, 6, h2 * NT * DH:(h2 + 1) * NT * DH].rearrange("p (t d) -> p t d", d=DH), ALU.mult).then_inc(sb_mixed, 1)

                    def own_columns(b2):
                        dve.wait_ge(page_free, i * 2 * NPG + (4 + NB * NPG + NPG * (b2 + 1)))
                        TT(om[:, bass.ds(i * 2 * HW + b2 * HW, HW)], ps[:, 7, :], cst("own_head"), ALU.mult).then_inc(ds_om, 1)

                    softplus(0)
                    for j, (h2, s) in enumerate(blocks):
                        if j + 1 < NBK:
                            softplus(j + 1)
                        if j == 4:
                            own_columns(0)
                        dve.wait_ge(sb_la, i * NBK + (j + 1))
                        TT(ps[:, 4 + j % 2, 0:P], ps[:, 4 + j % 2, 0:P], cst("strict_neg"), ALU.add).then_inc(sb_masked, 1)
                        if j == 5:
                            mix(0)
                    mix(1)
                    own_columns(1)

                dve.wait_ge(rs_back, 32)
                group_norm(B_rs[0:NB, 0:HW], NB, sec(NT, RG).rearrange("p (a c) -> p a c", a=1), NT + 1, rs_done)
                dve.wait_ge(ds_row, 1)
                TT(sec(NT, SG), sec(NT, SG), ps[0:NB, 1, :], ALU.mult).then_inc(ds_mixed, 1)

                def add_residual(n, u):
                    for t in range(NT + 1):
                        dve.wait_ge(mm_done, 5 * n + t + 1)
                        for row, a, e in (quarters(0, CH) if t == NT else [(0, 0, CH)]):
                            x = xres[0:rows[t], t, u * CH + a:u * CH + e]
                            add = TT(x, x, ps[row:row + rows[t], t, 0:e - a], ALU.add)
                        add.then_inc(bank_free, 1)

                dve.wait_ge(xr_loaded, 32)
                for u in range(2):
                    add_residual(NCHUNK0 + u, u)


                turned_x(1)

                def squares(a, t, col, n):
                    r = rows[t]
                    x = z[0:r, t, a:a + n * DH]
                    st.done(TT(tmp3[0:r, 0:n * DH], x, x, ALU.mult))
                    return RED(stats[0:r, col:col + n], heads(tmp3[0:r, 0:n * DH]), AX.X, ALU.add)

                def scaled(a, t, col, n, gain):
                    r = rows[t]
                    x = heads(z[0:r, t, a:a + n * DH])
                    st.done(TT(x, x, bc(stats[0:r, col:col + n].unsqueeze(2), [r, n, DH]), ALU.mult))
                    return TT(x, x, bc(cst(gain, r).unsqueeze(1), [r, n, DH]), ALU.mult)

                st.done(nc.vector.memset(stats[:], 1.0))
                for c in range(2):
                    dve.wait_ge(bank_free, 5 + 5 * (11 + c))
                    for t in range(NT + 1):
                        red = squares(c * CH, t, 16 * t + 8 * c, 8)
                        if c == 1 and t == NT:
                            red.then_inc(k_ssq, 1)
                        else:
                            st.done(red)
                dve.wait_ge(k_rstd, 1)
                for t in range(NT + 1):
                    mul = scaled(Q1, t, 16 * t, HN, "gain_q")
                    mul.then_inc(heads_ready, 1) if t == NT else st.done(mul)
                dve.wait_ge(heads_ready, 1)
                dve.wait_ge(bank_free, 5 + 5 * 14)
                for t in range(NT + 1):
                    st.done(squares(KS, t, 16 * t, 2))
                    red = squares(KW, t, 16 * t + 2, 2)
                    red.then_inc(k_ssq, 1) if t == NT else st.done(red)
                dve.wait_ge(k_rstd, 2)
                for t in range(NT + 1):
                    st.done(scaled(KS, t, 16 * t, 2, "gain_sel"))
                    mul = scaled(KW, t, 16 * t + 2, 2, "gain_win")
                    st.done(mul)
                dve.wait_ge(bank_free, 5 + 80)
                dve.sem_inc(heads_ready, 1)

                dve.sem_inc(cm_T, 2)
                for w in range(2):
                    if w == 1:
                        dve.wait_ge(cm_proj, 1)
                    with dve.Fori(0, NB) as b:
                        for q in range(2):
                            dve.wait_ge(cm_turned, b * 2 + (16 * w + q + 3))
                            TT(kcT[:, :, bass.ds(b * NCB + q * NPB, NPB)].rearrange("p l n -> p n l"),
                               ps[:, 5 + q, :].rearrange("p (n l) -> p n l", l=CB),
                               bc(cst("pe").unsqueeze(1), [P, NPB, CB]), ALU.add).then_inc(cm_T, 1)
                    dve.wait_ge(cmp_turned, w + 1)
                    TT(kcT[:, :, NB * NCB:N_CMP].rearrange("p l n -> p n l"), ps[:, 4, :].rearrange("p (n l) -> p n l", l=CB),
                       bc(cst("pe").unsqueeze(1), [P, NPB, CB]), ALU.add).then_inc(cmp_T, 1)
                    if w == 0:
                        dve.wait_ge(cm_proj, 1)
                        st.done(nc.vector.tensor_copy(ckT, ps[:, 7, 0:N_CMP]))
                        TT(rk1, ckT, ckT, ALU.mult).then_inc(cm_sq, 1)
                        dve.wait_ge(cm_rstd, 1)
                        STT(ckT, ckT, cst("gain_cmp"), rk1, ALU.mult, ALU.mult).then_inc(ckT_ready, 1)
                dve.wait_ge(cvT_ready, 1)
                pair = cvT_pair.rearrange("p (u n) -> p u n", u=2)
                st.done(nc.vector.memset(cvT_pair, 0.0))
                nc.vector.tensor_copy(pair[:, :, 0:NPB], bc(cvT[:, NB * NCB:N_CMP].unsqueeze(1), [P, 2, NPB])).then_inc(cvT_ready, 1)
                st.done(nc.vector.memset(cv_pair, 0.0))
                dve.wait_ge(cv_turned, 1)
                st.done(nc.vector.tensor_copy(cv_s, ps[:, 4, 0:2 * P]))
                for u in range(2):
                    half = slice(u * DH, (u + 1) * DH)
                    cp = nc.vector.tensor_copy(cv_pair[half].rearrange("p (g u e) -> p g u e", g=G, u=2)[:, :, u, :],
                                               ps[half, 4, 2 * P:3 * P].rearrange("p (g e) -> p g e", g=G))
                    st.done(cp) if u == 0 else cp.then_inc(cv_ready, 1)

                dve.wait_ge(cm_proj, 2)
                st.done(nc.vector.memset(arena[:, 0:4 * KZ], 0.0))
                dve.wait_ge(kz_swapped, 1)
                for u in range(2):
                    half = slice(u * DH, (u + 1) * DH)
                    for w in range(2):
                        st.done(nc.vector.tensor_copy(Kz[half, u, u, w * SEQ:(w + 1) * SEQ], xk(w)[half]))
                        st.done(nc.vector.tensor_copy(Kz[half, 1 - u, u, w * SEQ:(w + 1) * SEQ], ps[half, 5 + w, :]))
                    st.done(nc.vector.tensor_copy(Kz[half, u, u, 2 * SEQ:KZ], ckT[half, NB * NCB:N_CMP]))
                    cp = nc.vector.tensor_copy(Kz[half, 1 - u, u, 2 * SEQ:KZ], ps[half, 7, 0:NPB])
                    st.done(cp)
                st.done(nc.vector.memset(small[:, 32:44], 1.0))
                nc.vector.memset(arena[:, 5184:5696], 0.0).then_inc(kz_ready, 1)
                dve.wait_ge(kz_ready, 1)

                dve.sem_inc(n_pt[0], 1)
                dve.sem_inc(n_o, 2)
                dve.sem_inc(n_t, 4)
                dve.sem_inc(n_av, 4)
                with st.loop(HN // 2, 5 + 16 + 4 * 4) as i:
                    pc = p_cmp[:, :, :, 0:NPB]
                    cs = small[:, 0:8].rearrange("p (t u) -> p t u", t=NT)
                    dve.wait_ge(nc_s, i + 1)
                    st.done(TT(pc, ps[:, 5, 0:P].rearrange("p (t u n) -> p t u n", t=NT, u=2),
                               bc(cst("cmp_neg").rearrange("p (t n) -> p t n", t=NT).unsqueeze(2), [P, NT, 2, NPB]), ALU.add))
                    st.done(RED(cs, pc, AX.X, ALU.max))
                    TT(pc, pc, bc(cs.unsqueeze(3), [P, NT, 2, NPB]), ALU.subtract).then_inc(nc_max, 1)
                    dve.wait_ge(nc_exp, i + 1)
                    st.done(RED(cs, pc, AX.X, ALU.add))
                    st.done(nc.vector.reciprocal(cs, cs))
                    st.done(TT(pc, pc, bc(cs.unsqueeze(3), [P, NT, 2, NPB]), ALU.mult))
                    TT(pc, pc, bc(cst("cmp_one").rearrange("p (t n) -> p t n", t=NT).unsqueeze(2), [P, NT, 2, NPB]), ALU.mult).then_inc(nc_p, 1)

                    def row_max(u):
                        t, h2, br = units[u]
                        N = (t + 1) * P
                        dve.wait_ge(n_s, i * 16 + (u + 1))
                        st.done(TT(ps[:, u % 4, t * P:N], ps[:, u % 4, t * P:N], cst("causal_neg"), ALU.add))
                        RED(nmax(u), ps[:, u % 4, 0:N], AX.X, ALU.max, negate=True).then_inc(n_max, 1)

                    def combine(t):
                        dve.wait_ge(n_av, i * 16 + (4 * t + 8))
                        d, c = small[:, 32 + 6 * (t % 2):38 + 6 * (t % 2)], small[:, 48:54]
                        gates = z[:, t, bass.ds(i * 6 + BG, 6)].rearrange("p (u x) -> p x u", x=3)
                        st.done(nc.vector.reciprocal(c, d))
                        st.done(TT(c.rearrange("p (x u) -> p x u", u=2), c.rearrange("p (x u) -> p x u", u=2), gates, ALU.mult))
                        TT(o3.rearrange("p (x d) -> p x d", x=6), ps[:, 6 + t % 2, 0:3 * P].rearrange("p (x d) -> p x d", x=6),
                           bc(c.unsqueeze(2), [P, 6, DH]), ALU.mult).then_inc(n_o, 1)
                        dve.wait_ge(n_o, i * 4 + (t + 3))
                        st.done(RED(o3b, o3.rearrange("p (x c) -> p c x", x=3), AX.X, ALU.add))
                        gate = z[:, t:t + 1, bass.ds(i * P + GATE, P)]
                        st.done(TT(gate, gate, o3b.rearrange("p (a c) -> p a c", a=1), ALU.mult))

                    row_max(0)
                    for u in range(16):
                        t, h2, br = units[u]
                        if u + 1 < 16:
                            row_max(u + 1)
                        if br == 0:
                            dve.wait_ge(n_t, i * 16 + (u + 5))
                            dve.wait_ge(n_av, i * 16 + (u + 1))
                            N = (t + 1) * P
                            nc.vector.tensor_copy(z[:, u % 4, PT_OFF:PT_OFF + N], ps[:, 4, 0:N]).then_inc(n_pt[0], 1)
                        if u % 4 == 1 and u > 4:
                            combine(u // 4 - 1)
                    combine(3)

                dve.wait_ge(r_back, 48)
                st.done(nc.vector.memset(Qpad, 0.0))
                dve.wait_ge(*marks_pe.at("r_spread"))
                st.done(nc.vector.tensor_copy(kn_bh, ps[:, 0, 0:4 * DH]))
                st.done(TS(q_bh, q_bh, SCALE, None, ALU.mult))
                for g in range(G):
                    ts = TS(q_dup[:, g * DH:(g + 1) * DH], q_bh, cst("own_group")[:, g:g + 1], None, ALU.mult)
                    st.done(ts) if g == 0 else ts.then_inc(*marks_dve.next("r_dup"))
                for w in range(2):
                    st.done(TT(small[:, 96:160], q_bh, kn_bh[:, 2 * w * DH:(2 * w + 1) * DH], ALU.mult))
                    red = RED(stats[:, 6 + w:7 + w], small[:, 96:160], AX.X, ALU.add)
                    st.done(red) if w == 0 else red.then_inc(*marks_dve.next("r_kn"))
                st.done(nc.vector.memset(win_neg, 0.0))
                nc.vector.memset(win_neg[:, 0:1], NEG).then_inc(*marks_dve.next("i_zero"))
                dve.wait_ge(*marks_act.at("r_QT"))
                for b in range(NB):
                    cp = nc.vector.tensor_copy(Qpad[:, b * P + b * HN:b * P + (b + 1) * HN], QT[:, b * HN:(b + 1) * HN])
                    st.done(cp) if b < NB - 1 else cp.then_inc(*marks_dve.next("r_pad"))
                dve.wait_ge(*marks_pe.at("i_s"))
                st.done(TT(p_imp, ps[:, 2, 0:NB * NCB], cst("cmp_own"), ALU.add))
                RED(stats[:, 4:5], p_imp, AX.X, ALU.max, negate=True).then_inc(*marks_dve.next("i_max"))
                dve.wait_ge(*marks_act.at("i_exp"))
                st.done(nc.vector.reciprocal(stats[:, 5:6], stats[:, 5:6]))
                TS(p_imp, p_imp, stats[:, 5:6], None, ALU.mult).then_inc(*marks_dve.next("i_p"))
                dve.wait_ge(*marks_pe.at("i_sum"))
                imp, least, hit, last = small[0:NB * G, 0:16], small[0:NB * G, 16:17], small[0:NB * G, 32:48], small[0:NB * G, 17:18]
                neg = small[0:NB * G, 64:80]
                st.done(RED(imp, ps[0:NB * G, 5, 0:NB * NCB].rearrange("p (b k r) -> p k b r", b=NB, r=2), AX.XY, ALU.add))
                st.done(TT(imp, imp, cst("forced", NB * G), ALU.add))
                st.done(RED(least, imp, AX.X, ALU.min))
                st.done(TS(hit, imp, least, None, ALU.is_equal))
                st.done(TT(hit, hit, cst("block_no", NB * G), ALU.mult))
                st.done(RED(last, hit, AX.X, ALU.max))
                TS(neg, cst("block_no", NB * G), last, NEG, ALU.is_equal, ALU.mult).then_inc(*marks_dve.next("i_neg"))
                dve.wait_ge(*marks_pe.at("i_o"))
                dve.sem_inc(sk_T, 3)
                with dve.Fori(0, NB) as b:
                    for q in range(3):
                        dve.wait_ge(sk_turned, b * 3 + (q + 4))
                        dve.wait_ge(sk_scored, b * 3 + (q + 1))
                        nc.vector.tensor_copy(KTs[:, q], ps[:, 4 + q, :]).then_inc(sk_T, 1)
                dve.wait_ge(sk_scored, 3 + 3 * NB)
                sel, win = ps[:, 0:2, :].rearrange("p a c -> p (a c)"), ps[:, 2, :]
                st.done(RED(stats[:, 8:9], sel, AX.X, ALU.max))
                st.done(RED(stats[:, 9:10], win, AX.X, ALU.max))
                st.done(TT(stats[:, 8:10], stats[:, 8:10], stats[:, 6:8], ALU.max))
                st.done(TS(stats[:, 8:10], stats[:, 8:10], -1.0, None, ALU.mult))
                TT(stats[:, 6:8], stats[:, 6:8], stats[:, 8:10], ALU.add).then_inc(*marks_dve.next("sk_max"))
                dve.wait_ge(*marks_act.at("sk_exp"))
                st.done(TT(stats[:, 12:14], stats[:, 12:14], stats[:, 14:16], ALU.add))
                st.done(nc.vector.reciprocal(stats[:, 12:14], stats[:, 12:14]))
                st.done(TT(stats[:, 1:3], stats[:, 1:3], stats[:, 12:14], ALU.mult))
                dve.wait_ge(sv_used, 3 + 3 * NB)
                nc.vector.tensor_copy(oT1, ps[:, 0:2, 0:P]).then_inc(*marks_dve.next("sv_oT"))
                own = bc(cst("own_group").unsqueeze(2), [P, G, DH])
                st.done(TT(o3[:, 0:P].rearrange("p (g e) -> p g e", g=G), ps[:, 7, 0:P].rearrange("p (g e) -> p g e", g=G), own, ALU.mult))
                dve.wait_ge(*marks_pe.at("sv_back"))
                for w in range(2):
                    st.done(TT(o3[:, (w + 1) * P:(w + 2) * P].rearrange("p (g e) -> p g e", g=G),
                               ps[:, 2, w * P:(w + 1) * P].rearrange("p (g e) -> p g e", g=G), own, ALU.mult))
                r3 = small[:, 0:3 * DH].rearrange("p (x e) -> p x e", x=3)
                st.done(RED(r3, o3.rearrange("p (x g e) -> p x e g", x=3, g=G), AX.X, ALU.add))
                for w in range(2):
                    st.done(STT(r3[:, w + 1, :], kn_bh[:, (2 * w + 1) * DH:(2 * w + 2) * DH], stats[:, 14 + w:15 + w], r3[:, w + 1, :], ALU.mult, ALU.add))
                st.done(TS(q_bh, r3[:, 0, :], stats[:, 0:1], None, ALU.mult))
                for w in range(2):
                    add = STT(q_bh, r3[:, w + 1, :], stats[:, w + 1:w + 2], q_bh, ALU.mult, ALU.add)
                    st.done(add) if w == 0 else add.then_inc(*marks_dve.next("sv_sum"))
                dve.wait_ge(sv_row, 16)
                gate = z[0:NB, NT, GATE:BG]
                TT(gate, gate, o_row, ALU.mult).then_inc(*marks_dve.next("sv_done"))
                for u in range(2):
                    add_residual(16 + u, u)


SHAPES = {
    "x_prompt": (1, SEQ, D), "x_sample": (NB, 1, D), "state_ret": (NB, H, DH, DH),
    "cache_sb_k": (80, PAGE, H, DH), "cache_sb_v": (80, PAGE, H, DH), "page_table": (NB, NPG),
    "w_in0": (D, W0), "w_out0": (D, D), "w_in1": (D, W1), "w_out1": (D, D),
}
DIRECT = ["x_prompt", "x_sample", "state_ret", "cache_sb_k", "cache_sb_v", "cache_cmp_k", "cache_cmp_v",
          "cache_sel_k", "cache_sel_v", "cache_win_k", "cache_win_v", "page_table", "w_in0", "w_out0",
          "w_in1", "w_cmp_k", "w_cmp_v", "w_out1"]
KV = (1, SEQ, G, DH)
KVS = (NB, 1, G, DH)
WB = (NB, 512, G, DH)
OUTS = [(1, SEQ, D), (NB, 1, D), (1, H, DH, DH), (NB, H, DH, DH), (1, SEQ, H, DH), (1, SEQ, H, DH),
        (NB, 1, H, DH), (NB, 1, H, DH), KV, KV, KV, KV, KV, KV, KVS, KVS, KVS, KVS, WB, WB]


def parameters(aux, inputs):
    def put(name, a):
        lo, hi = AT[name]
        aux[:, lo:hi] = a

    for layer in (0, 1):
        put(f"gain_in{layer}", inputs[f"norm{layer}_g"].reshape(KT, P).T)
    put("gain_ret", inputs["ret_gn_g"].reshape(1, HW))
    for name, key in (("gain_sq", "sb_qn_g"), ("gain_sk", "sb_kn_g"), ("gain_q", "nsa_qn_g"),
                      ("gain_sel", "sel_kn_g"), ("gain_win", "win_kn_g")):
        put(name, inputs[key].reshape(1, DH))
    put("gain_cmp", np.concatenate([inputs["cmp_kn_g"]] * G).reshape(P, 1))
    put("pe", np.concatenate([inputs["cmp_pe"].T] * G))
    return aux


def kernel(**inputs):
    import concourse.bacc as bacc
    from concourse.bass_utils import run_bass_kernel_spmd

    inputs = {k: np.asarray(v) for k, v in inputs.items()}
    arrays = {name: np.ascontiguousarray(inputs[name]) for name in DIRECT}
    arrays["aux"] = parameters(constants(), inputs)
    nc = bacc.Bacc("TRN2", target_bir_lowering=False, num_devices=1)
    ins = {k: nc.dram_tensor(k, a.shape, mybir.dt.from_np(a.dtype), kind="ExternalInput").ap() for k, a in arrays.items()}
    outs = {f"o{i}": nc.dram_tensor(f"o{i}", s, F32, kind="ExternalOutput").ap() for i, s in enumerate(OUTS)}
    build(nc, ins, outs)
    r = run_bass_kernel_spmd(nc, [arrays], core_ids=[0])
    return tuple(r.results[0][f"o{i}"] for i in range(len(OUTS)))
```

```python
import math
from contextlib import ExitStack, contextmanager

import numpy as np

import concourse.bass as bass
from concourse import mybir

F32 = mybir.dt.float32
I32 = mybir.dt.int32
ALU = mybir.AluOpType
ACT = mybir.ActivationFunctionType
AX = mybir.AxisListType

P = 128
D = 1024
KT = D // P
SEQ = 512
NT = SEQ // P
NB = 8
PAST = 1024
PAGE = 128
NPG = PAST // PAGE
DH = 64
H = 8
HW = H * DH
NHP = H // 2
CH = 512
W0 = 8 * HW
W1 = 2864
HN = 16
G = 2
HPG = HN // G
CB = 32
NCB = PAST // CB
NPB = SEQ // CB
NSB = PAST // 64
EPS = 1e-6
NEG = -1e30
SCALE = DH ** -0.5
SQ, SK, SV, SG, RQ, RK, RV, RG = range(8)
SECTION = [(i + 4) % 8 for i in range(8)]

AUX = [("ident", P), ("gain_in0", KT), ("tri_neg", P), ("ones_neg", P), ("strict", P), ("strict_neg", P),
       ("causal_neg", P), ("swap", P), ("ret_decay", H * P), ("q_decay", H), ("k_decay", H), ("chunk_decay", NHP),
       ("cosine", (NT + 1) * DH), ("sine", (NT + 1) * DH), ("gamma", NHP), ("half_ones", 2),
       ("mean_ones", P), ("own_head", HW), ("to_row", NB * NB),
       ("gain_in1", KT), ("gain_ret", HW), ("gain_sq", DH), ("gain_sk", DH),
       ("gain_q", DH), ("gain_sel", DH), ("gain_win", DH), ("gain_cmp", 1), ("pe", CB),
       ("own_group", G), ("group_sum", NB * G), ("cmp_own", NB * NCB), ("spread", P),
       ("forced", NSB), ("block_no", NSB), ("cmp_neg", NT * NPB), ("cmp_one", NT * NPB)]
AT = {}
_n = 0
for _name, _w in AUX:
    AT[_name] = (_n, _n + _w)
    _n += _w
NAUX = _n


def constants():
    f = np.float32
    c = np.zeros((P, NAUX), f)

    def put(name, a):
        a = np.asarray(a, f)
        lo, hi = AT[name]
        c[:a.shape[0], lo:hi] = a.reshape(a.shape[0], -1)

    i = np.arange(P)
    row, col = i[:, None], i[None, :]
    put("ident", np.eye(P))
    put("tri_neg", -(row >= col).astype(f))
    put("ones_neg", -np.ones((P, P)))
    put("strict", row < col)
    put("strict_neg", np.where(row < col, 0, NEG))
    put("swap", (row + DH) % P == col)
    put("causal_neg", np.where(col <= row, 0, NEG))
    lg = np.log1p(-np.exp2(-5.0 - np.arange(H)))
    dec = np.exp(-lg[None, :] * (i[:, None] + 1)) * SCALE
    put("ret_decay", dec[:, :, None] * (row <= col)[:, None, :])
    put("q_decay", np.exp(lg[None, :] * (i[:, None] + 1)))
    put("k_decay", np.exp(lg[None, :] * (P - 1 - i[:, None])) * SCALE)
    head = 2 * np.arange(NHP)[None, :] + (i[:, None] // DH)
    put("chunk_decay", np.exp(lg[head] * P))
    put("gamma", np.exp(lg[head]))
    half = DH // 2
    inv = (10000.0 ** (-np.arange(half, dtype=f) / half)).astype(f)
    pos = np.concatenate([np.arange(SEQ), np.full(P, PAST)]).reshape(NT + 1, P).T.astype(f)
    ang = pos[:, :, None] * inv
    put("cosine", np.concatenate([np.cos(ang), np.cos(ang)], -1))
    put("sine", np.concatenate([-np.sin(ang), np.sin(ang)], -1))
    put("half_ones", (row // DH == np.arange(2)[None, :]))
    put("mean_ones", (row // DH == col // DH) / DH)
    put("own_head", (i[:, None] % 32 == np.arange(HW)[None, :] // DH))
    put("to_row", np.broadcast_to(np.eye(NB)[None], (P, NB, NB)))
    put("own_group", ((i[:, None] % HN) // HPG == np.arange(G)[None, :]))
    bg = np.arange(NB * G)
    put("group_sum", ((i[:, None] // HPG) == bg[None, :]))
    put("spread", (bg[:, None] == i[None, :] // HPG))
    put("cmp_own", np.where(i[:, None] // HN == np.arange(NB * NCB)[None, :] // NCB, 0, NEG))
    blk = np.arange(NSB)
    put("forced", np.broadcast_to(1000.0 * ((blk == 0) | (blk == NSB - 1)), (NB * G, NSB)))
    put("block_no", np.broadcast_to(blk + 1.0, (NB * G, NSB)))
    t = np.arange(SEQ).reshape(NT, P).T[:, :, None]
    ok = np.arange(NPB) * CB + CB - 1 <= t
    put("cmp_neg", np.where(ok, 0, NEG))
    put("cmp_one", ok)
    return c


class Steps:

    def __init__(self, eng, sem):
        self.eng, self.sem, self.n, self.base = eng, sem, 0, 0

    def done(self, ins):
        ins.then_inc(self.sem, 1)
        self.n += 1
        self.eng.wait_ge(self.sem, self.base + self.n)

    @contextmanager
    def loop(self, count, steps, first=0):
        start = self.n
        with self.eng.Fori(0, count) as i:
            self.base, self.n = i * steps + start, 0
            yield i + first
            assert self.n == steps, (self.n, steps)
        self.base, self.n = 0, start + count * steps


class Marks:

    def __init__(self, sem, names):
        self.sem, self.names, self.given = sem, names, 0

    def next(self, name):
        assert self.names[self.given] == name, name
        self.given += 1
        return self.sem, 1

    def at(self, name):
        return self.sem, self.names.index(name) + 1


def build(nc, ins, outs):
    with ExitStack() as ctx:
        def sb(name, shape, dt=F32):
            return ctx.enter_context(nc.sbuf_tensor(name, shape, dt))

        def sem(name):
            return ctx.enter_context(nc.semaphore(name))

        def dram(name, shape):
            return nc.dram_tensor(name, shape, F32, kind="Internal").ap()

        ps = ctx.enter_context(nc.psum_tensor("ps", [P, 8, CH], F32))

        z = sb("z", [P, NT + 1, W0])
        wring = sb("wring", [P, 2, KT, CH])
        xres = sb("xres", [P, NT + 1, D])
        aux = sb("consts", [P, NAUX])
        NX, NQ, NPAGES = KT * (SEQ + NB), NB * HW, 4 * HW
        arena = sb("arena", [P, NX + NQ + NPAGES])
        xnT = arena[:, 0:NX].rearrange("p (k n) -> p k n", k=KT)
        qbc = arena[:, NX:NX + NQ].rearrange("p (b c) -> p b c", b=NB)
        pages = arena[:, NX + NQ:].rearrange("p (s c) -> p s c", s=4)
        work = sb("work", [P, 3072])
        S_ret = sb("S_ret", [P, NHP, DH])
        kqT = sb("kqT", [P, 2 * NHP * NB])
        stats = sb("stats", [P, 96])
        table = sb("table", [1, NB * NPG], I32)

        def cst(name, rows=P):
            lo, hi = AT[name]
            return aux[0:rows, lo:hi]

        def flat(a):
            return a.rearrange("p a b -> p (a b)")

        xflat = flat(xres[:])

        d_sq = dram("d_sq", (NB, HW))
        d_rv = dram("d_rv", (NB, HW))
        d_ro = dram("d_ro", (2, NB, NHP, DH))

        s_first, s_aux, s_x, s_table = sem("first_loaded"), sem("aux_loaded"), sem("x_loaded"), sem("table_loaded")
        w_loaded = [sem("w_loaded0"), sem("w_loaded1")]
        page_loaded = [sem(f"page_loaded{i}") for i in range(4)]
        page_free = sem("page_free")
        act_step, dve_step, pool_step = sem("act_step"), sem("dve_step"), sem("pool_step")
        xn_ready, xt_summed, xnT_ready = sem("xn_ready"), sem("xt_summed"), sem("xnT_ready")
        mm_done, bank_free = sem("mm_done"), sem("bank_free")
        ssq_ready, rstd_ready = sem("ssq_ready"), sem("rstd_ready")
        sq_sent, sq_spread = sem("sq_sent"), sem("sq_spread")
        sections_ready = sem("sections_ready")
        ret_staged, ret_turned, ret_T, ret_att, ret_attm, ret_kd, ret_o, ret_kv, ret_S, ret_done = (
            sem("ret_" + x) for x in ("staged", "turned", "T", "att", "attm", "kd", "o", "kv", "S", "done"))
        gn_sum, gn_rstd = sem("gn_sum"), sem("gn_rstd")
        sb_staged, sb_turned, sb_T, sb_z, sb_ln, sb_sp, sb_la, sb_masked, sb_a, sb_o, sb_mixed = (
            sem("sb_" + x) for x in ("staged", "turned", "T", "z", "ln", "sp", "la", "masked", "a", "o", "mixed"))
        ds_scores, ds_ln, ds_sp, ds_la, ds_lasum, ds_a, ds_stage, ds_o, ds_om, ds_row, ds_mixed = (
            sem("ds_" + x) for x in ("scores", "ln", "sp", "la", "lasum", "a", "stage", "o", "om", "row", "mixed"))
        rs_in, rs_turned, rs_kqT, rs_S, rs_t, rs_sum, rs_row, rs_sent, rs_back, rs_done = (
            sem("rs_" + x) for x in ("in", "turned", "kqT", "S", "t", "sum", "row", "sent", "back", "done"))
        rv_sent = sem("rv_sent")
        zeroed, zeroed_stats, rstd_x = sem("zeroed"), sem("zeroed_stats"), sem("rstd_x")
        mix_turned, mix_T, xr_loaded = sem("mix_turned"), sem("mix_T"), sem("xr_loaded")
        stored = sem("stored")

        rows = [P] * NT + [NB]
        NCHUNK0 = W0 // CH
        NC1 = -(-W1 // CH)

        Q1, KC, VC, KS, VS, KW, VW, GATE, BG = 0, 1024, 1152, 1280, 1408, 1536, 1664, 1792, 2816
        P_OFF, PT_OFF = 2864, 3376
        N_CMP = NB * NCB + NPB
        kcT = arena[:, 0:CB * N_CMP].rearrange("p (l n) -> p l n", l=CB)
        ckT, rk1, cvT = work[:, 0:N_CMP], work[:, 272:544], work[:, 816:1088]
        cv_s = work[:, 1088:1344]
        cv_pair = work[:, 1344:1600]
        cvT_pair = work[:, 544:672]
        q_bh, kn_bh, QT = work[:, 1664:1728], work[:, 1728:1984], work[:, 1984:2112]
        o_cmp, q_dup = work[:, 2112:2240], work[:, 2240:2368]
        kn_bg = work[0:NB * G, 2368:2624]
        small = work[:, 2624:2880]
        pick = work[0:NB * G, 2880:2960]
        prod = work[:, 2976:3040]
        q_one, p_one = work[:, 3040:3040 + HN], work[:, 272:272 + 12 * HN]
        KZ = 2 * SEQ + NPB
        Kz = arena[:, 0:4 * KZ].rearrange("p (g u c) -> p g u c", g=G, u=2)
        q_tok, qTs = arena[:, 4160:4672], arena[:, 4672:5184]
        p_cmp = arena[:, 5184:5696].rearrange("p (t u n) -> p t u n", t=NT, u=2)
        p_cmpT = arena[:, 5696:6208]
        KTs = [arena[:, 6208:6720], arena[:, 6720:7232], work[:, 272:784]]
        PT1 = [z[:, NT, P_OFF + j * P:P_OFF + (j + 1) * P] for j in range(NPG)] + \
              [arena[:, 8000 + j * P:8000 + (j + 1) * P] for j in range(4)]
        PT1_sel, PT1_win = z[:, NT, P_OFF:P_OFF + NPG * P], arena[:, 8000:8000 + 4 * P]
        Pexp = arena[:, 5184:6720]
        p_imp = arena[:, 8768:9024]
        p_impT = arena[:, 9024:9280].rearrange("p (j c) -> p j c", j=2)
        oT1 = arena[:, 6976:7232].rearrange("p (w c) -> p w c", w=2)
        o3 = arena[:, 7232:7616]
        o3s = arena[:, 7232:8000].rearrange("p (b c) -> p b c", b=2)
        o3b = small[:, 64:192]
        o_row = arena[0:NB, 7616:8640]
        slot1 = pages[:, 1:4, :]
        wcmp = [wring[:, u].rearrange("p k c -> p (k c)").rearrange("p (l m) -> p l m", l=CB) for u in range(2)]
        d_q, d_kv, d_g, d_o = (dram("d_q", (NB, D)), dram("d_kv", (NB, G, 4, DH)), dram("d_g", (NB, 3 * HN)), dram("d_o", (NB, D)))
        k_ssq, k_rstd = sem("k_ssq"), sem("k_rstd")
        heads_ready = sem("heads_ready")
        wz, wcmp_loaded = sem("wz"), [sem("wcmp_k_loaded"), sem("wcmp_v_loaded")]
        cm_pages = [[z[:, t, P_OFF + q * 4 * P:P_OFF + (q + 1) * 4 * P] for q in range(2)] for t in range(4)]
        cm_loaded = [[sem(f"cm_loaded{t}{q}") for q in range(2)] for t in range(4)]
        cm_turned, cm_T, cmp_turned, cmp_T, cm_proj, cm_sq, cm_mean, cm_rstd, ckT_ready, cvT_ready = (
            sem("cm_" + x) for x in ("turned", "T", "p_turned", "p_T", "proj", "sq", "mean", "rstd", "ckT", "cvT"))
        cv_turned, cv_ready, kz_turned, kz_T, kz_swapped, kz_ready = (
            sem(x) for x in ("cv_turned", "cv_ready", "kz_turned", "kz_T", "kz_swapped", "kz_ready"))
        nq_staged, nq_turned, nq_T, nc_s, nc_max, nc_exp, nc_p, nc_turned, nc_T = (
            sem(x) for x in ("nq_staged", "nq_turned", "nq_T", "nc_s", "nc_max", "nc_exp", "nc_p", "nc_turned", "nc_T"))
        n_s, n_max, n_p, n_t, n_pt, n_av, n_o, n_mix = (sem("n_" + x) for x in ("s", "max", "p", "t", "pt", "av", "o", "mix"))
        r_sent, r_back = sem("r_sent"), sem("r_back")
        marks_dve = Marks(sem("sample_dve"), ["r_dup", "r_kn", "i_max", "i_p", "i_neg", "i_out", "sk_max", "sv_sum", "sv_done"])
        marks_pe = Marks(sem("sample_pe"), ["r_spread", "r_turned", "i_s", "i_sum", "i_o", "sk_back", "sk_pturned", "sv_back"])
        marks_act = Marks(sem("sample_act"), ["r_QT", "i_exp", "i_T", "sk_exp", "sk_PT"])
        sk_loaded = [sem(f"sk_loaded{q}") for q in range(3)]
        sk_turned, sk_T, sk_scored = (sem("sk_" + x) for x in ("turned", "T", "scored"))
        sv_loaded = [sem(f"sv_loaded{q}") for q in range(3)]
        sv_used, sv_staged, sv_T, sv_sent, sv_row = (sem("sv_" + x) for x in ("used", "staged", "T", "sent", "row"))

        def sec(t, s, r=None):
            return z[0:(r or rows[t]), t, s * HW:(s + 1) * HW]

        def quarters(a, e):
            return [(c // P * 32, c, min(c + P, e)) for c in range(a, e, P)]

        def heads(a):
            return a.rearrange("p (h d) -> p h d", d=DH)

        def bc(a, shape):
            return a.broadcast_to(shape)

        def page_group(eng, name, col, dst, sem_):
            src = ins[name].rearrange("n p g d -> n p (g d)")
            for m in range(4):
                page = eng.value_load(table[0:1, bass.ds(col + m, 1)], min_val=0, max_val=src.shape[0] - 1)
                eng.dma_start(dst[:, m * P:(m + 1) * P].rearrange("p (a c) -> p a c", a=1),
                              src[bass.ds(page, 1)].rearrange("n p c -> p n c")).then_inc(sem_, 16)

        qk_st = xflat[:, 256:256 + 1024]
        qBD = xflat[:, 1280:2304].rearrange("p (a b n) -> p a b n", a=NHP, b=2)
        kT_r = xflat[:, 2304:2816]
        attm = xflat[:, 2816:3840]
        kd = xflat[:, 3840:4352]
        o_tmp = xflat[:, 4352:4864]
        tmp = work[:, 0:512]
        tmp2 = work[:, 512:1024]
        zs = work[:, 1024:1536]
        spz = work[:, 1536:2048]
        tail = work[:, 2048:2560]
        lnz = work[:, 2560:3072]
        a_st = work[:, 1536:2048].rearrange("p (j c) -> p j c", c=32)
        om = arena[:, 0:NB * HW]
        A_rs, B_rs = arena[:, NX:NX + 2048], arena[:, NX + 2048:NX + NQ]

        def by_pair(a):
            return a.rearrange("p (b a e) -> p b a e", b=NB, a=NHP)

        with nc.Block() as block:

            @block.sync
            def _(sp):
                x_tiles = ins["x_prompt"].rearrange("b (t p) d -> p (b t) d", p=P)
                x_rows = ins["x_sample"].rearrange("b s d -> (b s) d")
                sp.dma_start(xres[:, 0:NT, :], x_tiles).then_inc(s_x, 16)
                sp.dma_start(xres[0:NB, NT, :], x_rows).then_inc(s_x, 16)
                first = AT["gain_in0"][1]
                sp.dma_start(aux[:, 0:first], ins["aux"][:, 0:first]).then_inc(s_first, 16)

                w_in0 = ins["w_in0"].rearrange("(k p) n -> p k n", p=P)
                for n in range(4):
                    if n >= 2:
                        sp.wait_ge(mm_done, 5 * (n - 1))
                    c = SECTION[n] * CH
                    sp.dma_start(wring[:, n % 2], w_in0[:, :, c:c + CH]).then_inc(w_loaded[n % 2], 16)
                    if n == 0:
                        sp.dma_start(aux[:, first:NAUX], ins["aux"][:, first:NAUX]).then_inc(s_aux, 16)
                with sp.Fori(0, 2) as i:
                    for u in range(2):
                        sp.wait_ge(mm_done, 10 * i + 5 * (3 + u))
                        sp.dma_start(wring[:, u], w_in0[:, :, bass.ds(i * 2 * CH + u * CH, CH)]).then_inc(w_loaded[u], 16)
                sp.wait_ge(bank_free, 5 + 5 * 7)
                sp.dma_start(d_rv, sec(NT, RV)).then_inc(rv_sent, 16)
                sp.wait_ge(rv_sent, 16)
                sp.wait_ge(ds_scores, 1)
                for u in range(2):
                    half = slice(u * DH, (u + 1) * DH)
                    sp.dma_start(by_pair(A_rs)[half], ins["state_ret"].rearrange("b (a u) d e -> u d b a e", u=2)[u]).then_inc(rs_in, 16)
                    for b in range(NB):
                        row = d_rv.rearrange("b (a u e) -> b u a e", u=2, e=DH)[b, u]
                        sp.dma_start(by_pair(B_rs)[half, b], row.partition_broadcast(DH)).then_inc(rs_in, 16)
                w_out0 = ins["w_out0"].rearrange("(k p) n -> p k n", p=P)
                for u in range(2):
                    sp.wait_ge(mm_done, 5 * (7 + u))
                    sp.dma_start(wring[:, u], w_out0[:, :, u * CH:(u + 1) * CH]).then_inc(w_loaded[u], 16)

                n_store = [0]

                def store(out, src):
                    sp.dma_start(out, src).then_inc(stored, 16)
                    n_store[0] += 16

                sp.wait_ge(sections_ready, 2)
                store(outs["o4"].rearrange("b (t p) h d -> p (b t) (h d)", p=P), z[:, 0:NT, SK * HW:(SK + 1) * HW])
                store(outs["o5"].rearrange("b (t p) h d -> p (b t) (h d)", p=P), z[:, 0:NT, SV * HW:(SV + 1) * HW])
                store(outs["o6"].rearrange("b s h d -> (b s) (h d)"), sec(NT, SK))
                store(outs["o7"].rearrange("b s h d -> (b s) (h d)"), sec(NT, SV))
                sp.wait_ge(ret_S, NT + 1)
                for u in range(2):
                    store(outs["o2"].rearrange("b (a u) d e -> u d (b a) e", u=2)[u], S_ret[u * DH:(u + 1) * DH])
                sp.wait_ge(rs_S, 1)
                for u in range(2):
                    store(outs["o3"].rearrange("b (a u) d e -> u d b a e", u=2)[u], by_pair(A_rs)[u * DH:(u + 1) * DH])
                sp.wait_ge(rs_row, 1)
                sp.dma_start(d_ro.rearrange("u b a e -> u (b a e)"), B_rs[0:2]).then_inc(rs_sent, 16)
                sp.wait_ge(rs_sent, 16)
                for u in range(2):
                    sp.dma_start(B_rs[0:NB, 0:HW].rearrange("b (a u e) -> b a u e", u=2, e=DH)[:, :, u], d_ro[u]).then_inc(rs_back, 16)
                sp.wait_ge(sb_mixed, H + 2)
                sp.dma_start(xres[:, 0:NT, :], x_tiles).then_inc(xr_loaded, 16)
                sp.dma_start(xres[0:NB, NT, :], x_rows).then_inc(xr_loaded, 16)
                for k, name in ((18, "cache_win_k"), (19, "cache_win_v")):
                    store(outs[f"o{k}"].rearrange("b s g d -> b (s g d)")[:, 0:511 * G * DH],
                          ins[name].rearrange("b s g d -> b (s g d)")[:, G * DH:512 * G * DH])
                w_in1 = ins["w_in1"].rearrange("(k p) n -> p k n", p=P)
                for c in range(NC1):
                    n, w = 10 + c, min(CH, W1 - c * CH)
                    sp.wait_ge(mm_done, 5 * (n - 1))
                    sp.dma_start(wring[:, n % 2, :, 0:w], w_in1[:, :, c * CH:c * CH + w]).then_inc(w_loaded[n % 2], 16)
                    if c == 1:
                        sp.wait_ge(mix_turned, 5)
                        sp.wait_ge(s_table, 16)
                    if 1 <= c <= 4:
                        for q in range(2):
                            page_group(sp, "cache_cmp_k", (c - 1) * NPG + 4 * q, cm_pages[c - 1][q], cm_loaded[c - 1][q])
                for t in range(4):
                    sp.wait_ge(cm_turned, 2 * t + 1)
                    page_group(sp, "cache_cmp_k", (4 + t) * NPG, cm_pages[t][0], cm_loaded[t][0])
                sp.wait_ge(heads_ready, 2)
                sp.dma_start(d_q, z[0:NB, NT, Q1:Q1 + D]).then_inc(r_sent, 16)
                sp.dma_start(d_g, z[0:NB, NT, BG:BG + 3 * HN]).then_inc(r_sent, 16)
                for g in range(G):
                    sp.dma_start(d_kv[:, g], z[0:NB, NT, KS:GATE].rearrange("b (k g e) -> b k g e", k=4, g=G)[:, :, g]).then_inc(r_sent, 16)
                sp.wait_ge(r_sent, 64)
                sp.dma_start(q_bh, d_q.rearrange("b (h e) -> (b h) e", e=DH)).then_inc(r_back, 16)
                sp.dma_start(stats[:, 0:3], d_g.rearrange("b (h x) -> (b h) x", x=3)).then_inc(r_back, 16)
                sp.dma_start(kn_bg, d_kv.rearrange("b g k e -> (b g) (k e)")).then_inc(r_back, 16)
                with sp.Fori(0, 2) as r:
                    for t in range(4):
                        sp.wait_ge(cm_turned, r * 8 + (8 + 2 * t + 1))
                        page_group(sp, "cache_cmp_v", r * 4 * NPG + t * NPG, cm_pages[t][0], cm_loaded[t][0])
                sp.wait_ge(heads_ready, 2)
                for k, col in ((8, KC), (9, VC), (10, KS), (11, VS), (12, KW), (13, VW)):
                    store(outs[f"o{k}"].rearrange("b (t p) g d -> p (b t) (g d)", p=P), z[:, 0:NT, col:col + P])
                for k, col in ((14, KC), (15, VC), (16, KS), (17, VS)):
                    store(outs[f"o{k}"].rearrange("b s g d -> (b s) (g d)"), z[0:NB, NT, col:col + P])
                for k, col in ((18, KW), (19, VW)):
                    store(outs[f"o{k}"].rearrange("b s g d -> b (s g d)")[:, 511 * G * DH:], z[0:NB, NT, col:col + P])
                w_out1 = ins["w_out1"].rearrange("(k p) n -> p k n", p=P)
                for u in range(2):
                    sp.wait_ge(cm_proj, u + 1)
                    sp.dma_start(wring[:, u], w_out1[:, :, u * CH:(u + 1) * CH]).then_inc(w_loaded[u], 16)
                for name, loaded, used in (("cache_sel_k", sk_loaded, sk_turned), ("cache_sel_v", sv_loaded, sv_used)):
                    with sp.Fori(0, NB) as b:
                        for q in range(2):
                            sp.wait_ge(used, b * 3 + (q + 1))
                            page_group(sp, name, b * NPG + 4 * q, slot1[:, q], loaded[q])
                sp.wait_ge(*marks_dve.at("sv_sum"))
                sp.dma_start(d_o.rearrange("b (h e) -> (b h) e", e=DH), q_bh).then_inc(sv_sent, 16)
                sp.wait_ge(sv_sent, 16)
                sp.dma_start(o_row, d_o).then_inc(sv_row, 16)
                for u in range(2):
                    cols = slice(u * CH, (u + 1) * CH)
                    for t in range(0, NT, 2):
                        sp.wait_ge(bank_free, 5 + 80 + 5 * u + t + 2)
                        store(outs["o0"].rearrange("b (t p) d -> p (b t) d", p=P)[:, t:t + 2, cols], xres[:, t:t + 2, cols])
                    sp.wait_ge(bank_free, 5 + 85 + 5 * u)
                    store(outs["o1"].rearrange("b s d -> (b s) d")[:, cols], xres[0:NB, NT, cols])
                sp.wait_ge(stored, n_store[0])

            @block.gpsimd
            def _(pool):
                pool.dma_start(table[:], ins["page_table"].rearrange("(o b) n -> o (b n)", o=1)).then_inc(s_table, 16)
                pool.wait_ge(s_table, 16)
                pool.wait_ge(s_aux, 16)
                pool.sem_inc(page_free, 4)

                def load_pages(cache, before):
                    src = ins[cache].rearrange("n p h d -> n p (h d)")
                    with pool.Fori(0, NB * NPG // 4) as r:
                        for u in range(4):
                            pool.wait_ge(page_free, r * 4 + (before + u + 1))
                            page = pool.value_load(table[0:1, bass.ds(r * 4 + u, 1)], min_val=0, max_val=src.shape[0] - 1)
                            pool.dma_start(pages[:, u:u + 1, :], src[bass.ds(page, 1)].rearrange("n p c -> p n c")
                                           ).then_inc(page_loaded[u], 16)

                load_pages("cache_sb_k", 0)
                with pool.Fori(0, NT) as t:
                    pool.wait_ge(ret_staged, t + 1)
                    nc.gpsimd.tensor_tensor(heads(kd), heads(qk_st[:, HW:2 * HW]),
                                            bc(cst("k_decay").unsqueeze(2), [P, H, DH]), ALU.mult).then_inc(ret_kd, 1)
                    pool.wait_ge(ret_kv, t + 1)
                load_pages("cache_sb_v", NB * NPG)
                for v, wname in enumerate(("w_cmp_k", "w_cmp_v")):
                    pool.wait_ge(mm_done, 5 * (10 + NC1 - 1 + v))
                    nc.gpsimd.memset(wring[:, v], 0.0).then_inc(wz, 1)
                    pool.wait_ge(wz, v + 1)
                    for g in range(G):
                        pool.dma_start(wcmp[v][g * DH:(g + 1) * DH, :, g * DH:(g + 1) * DH],
                                       ins[wname].rearrange("l d e -> d l e")).then_inc(wcmp_loaded[v], 16)
                st = Steps(pool, pool_step)
                pool.wait_ge(cm_proj, 2)
                st.done(nc.gpsimd.memset(Kz[0:DH, :, 1, :], 0.0))
                nc.gpsimd.memset(Kz[DH:P, :, 0, :], 0.0).then_inc(kz_ready, 1)
                pool.sem_inc(n_mix, 2)
                with st.loop(HN // 2, 2 * NT) as i:
                    for t in range(NT):
                        pool.wait_ge(n_o, i * 4 + (t + 3))
                        st.done(nc.gpsimd.tensor_tensor(o3b, o3s[:, t % 2, 0:P], o3s[:, t % 2, P:2 * P], ALU.add))
                        st.done(nc.gpsimd.tensor_tensor(o3b, o3b, o3s[:, t % 2, 2 * P:3 * P], ALU.add))
                        gate = z[:, t:t + 1, bass.ds(i * P + GATE, P)]
                        nc.gpsimd.tensor_tensor(gate, gate, o3b.rearrange("p (a c) -> p a c", a=1), ALU.mult).then_inc(n_mix, 1)
                        pool.wait_ge(n_mix, i * 4 + (t + 3))
            kT_s = xflat[:, 1024:1536]

            def q_s(h2):
                return xflat[:, 1536 + h2 * 512:2048 + h2 * 512]

            def sp_s(h2, s):
                off = 2560 + h2 * 1280 + [0, 512, 896, 1152][s]
                return xflat[:, off:off + (NT - s) * P]

            def a_s(h2, s):
                off = RQ * HW + h2 * HW
                return z[:, s, off:off + (NT - s) * P]

            def xk(w):
                return arena[:, 4672 + w * 512:5184 + w * 512]

            tmp3 = work[:, 2048:2560]

            def nmax(u):
                return small[:, 16 + u % 8:17 + u % 8]

            def dens(u):
                t, h2, br = units[u]
                c = 32 + 6 * (t % 2) + 2 + 2 * br + h2
                return small[:, c:c + 1]

            MASK_PE = 8
            KEY_STEPS = {3: (0, 0), 5: (0, 1), 6: (0, 2), 8: (0, 3), 10: (1, 0), 11: (1, 1), 12: (1, 2), 13: (1, 3)}
            WINDOW_STEPS = {1: 0, 9: 1}
            VALUE_STEPS = {5: 0, 13: 1}

            units = [(t, h2, br) for t in range(NT) for h2 in range(2) for br in range(2)]
            blocks = [(h2, s) for h2 in range(2) for s in (3, 2, 1, 0)]
            NBK = len(blocks)

            @block.tensor
            def _(pe):
                ident = cst("ident")

                def turn(source, done_sem, ready_sem, free_sem, before, samples_ready=()):
                    for t in range(NT + 1):
                        n, r = before + t, rows[t]
                        pe.wait_ge(ready_sem, n + 1) if ready_sem is not None else None
                        if t >= 2:
                            pe.wait_ge(free_sem, n - 1)
                        if t == NT:
                            for sem_, value in samples_ready:
                                pe.wait_ge(sem_, value)
                        for k in range(KT):
                            b = 4 + 2 * (t % 2) + k // 4
                            mm = pe.transpose(ps[:, b, (k % 4) * P:(k % 4) * P + r], source(t, k), ident[0:r, 0:r])
                        mm.then_inc(done_sem, 1)

                def project(n, slot, turned, before, width=CH):
                    for t in range(NT):
                        pe.wait_ge(turned, before + t + 1)
                        pe.wait_ge(bank_free, n * 5 + (t + 1))
                        for k in range(KT):
                            mm = pe.matmul(ps[:, t, 0:width], xnT[:, k, t * P:(t + 1) * P], wring[:, slot, k, 0:width],
                                           start=(k == 0), stop=(k == KT - 1))
                        mm.then_inc(mm_done, 1)
                    pe.wait_ge(turned, before + NT + 1)
                    pe.wait_ge(bank_free, n * 5 + (NT + 1))
                    for k in range(KT):
                        for row, a, e in quarters(0, width):
                            mm = pe.matmul(ps[row:row + NB, NT, 0:e - a], xnT[:, k, SEQ:SEQ + NB], wring[:, slot, k, a:e],
                                           start=(k == 0), stop=(k == KT - 1))
                    mm.then_inc(mm_done, 1)

                pe.wait_ge(s_first, 16)
                turn(lambda t, k: work[0:rows[t], (t % 2) * D + k * P:(t % 2) * D + (k + 1) * P],
                     xt_summed, xn_ready, xnT_ready, 0)
                with pe.Fori(0, NCHUNK0 // 2) as i:
                    for u in range(2):
                        pe.wait_ge(w_loaded[u], i * 16 + 16)
                        project(i * 2 + u, u, xnT_ready, 0)

                pe.wait_ge(sections_ready, 4)
                for j in range(2 * NHP):
                    src = z[0:NB, NT, RQ * HW + j * P:RQ * HW + (j + 1) * P]
                    mm = pe.transpose(ps[:, 6, j * NB:(j + 1) * NB], src, ident[0:NB, 0:NB])
                mm.then_inc(rs_turned, 1)
                pe.wait_ge(ds_sp, 1)
                pe.matmul(ps[:, 7, :], cst("tri_neg"), spz, start=True, stop=False)
                pe.matmul(ps[:, 7, :], cst("ones_neg"), tail, start=False, stop=True).then_inc(ds_la, 1)

                pe.wait_ge(bank_free, 5 + 5 * NCHUNK0)
                pe.wait_ge(zeroed, 1)

                def ret_turn(t):
                    pe.wait_ge(ret_staged, t + 1)
                    for j in range(2 * NHP):
                        mm = pe.transpose(ps[:, j // 4, (j % 4) * P:(j % 4 + 1) * P], qk_st[:, j * P:(j + 1) * P], ident)
                    mm.then_inc(ret_turned, 1)

                def ret_chunk(t, last=False):
                    v_t = z[:, bass.ds(t, 1), RV * HW:(RV + 1) * HW].rearrange("p a c -> p (a c)")
                    pe.wait_ge(ret_T, t * 3 + 3)
                    for a in range(NHP):
                        mm = pe.matmul(ps[:, 2 + a // 2, (a % 2) * 256:(a % 2) * 256 + 256], kT_r[:, a * P:(a + 1) * P],
                                       qBD[:, a].rearrange("p b n -> p (b n)"), start=True, stop=True)
                    mm.then_inc(ret_att, 1)
                    if not last:
                        ret_turn(t + 1)
                    pe.wait_ge(ret_S, t + 1)
                    pe.wait_ge(ret_attm, t * 2 + 2)
                    for h in range(H):
                        o = ps[:, 4, h * DH:(h + 1) * DH]
                        pe.matmul(o, qBD[:, h // 2, h % 2, :], S_ret[:, h // 2, :], start=True, stop=False)
                        mm = pe.matmul(o, attm[:, h * P:(h + 1) * P], v_t[:, h * DH:(h + 1) * DH], start=False, stop=True)
                    mm.then_inc(ret_o, 1)
                    pe.wait_ge(ret_kd, t + 1)
                    for a in range(NHP):
                        mm = pe.matmul(ps[:, 5, a * P:(a + 1) * P], kd[:, a * P:(a + 1) * P], v_t[:, a * P:(a + 1) * P],
                                       start=True, stop=True)
                    mm.then_inc(ret_kv, 1)

                ret_turn(0)
                ret_chunk(0)
                with pe.Fori(1, NT - 1) as t:
                    ret_chunk(t)
                ret_chunk(NT - 1, last=True)

                pe.wait_ge(rs_t, 1)
                for j in range(4):
                    mm = pe.matmul(ps[32 * j:32 * j + 2, 6, :], cst("half_ones"), B_rs[:, j * 512:(j + 1) * 512], start=True, stop=True)
                mm.then_inc(rs_sum, 1)
                pe.wait_ge(rs_row, 1)
                pe.wait_ge(ds_lasum, 1)
                pe.wait_ge(ret_done, NT)

                pe.wait_ge(zeroed, 2)
                with pe.Fori(0, NHP) as i:
                    pe.wait_ge(sb_staged, i + 1)
                    for w in range(2):
                        for t in range(NT):
                            mm = pe.transpose(ps[:, w, t * P:(t + 1) * P], xflat[:, (2 * t + w) * P:(2 * t + w + 1) * P], ident)
                    mm.then_inc(sb_turned, 1)
                    pe.wait_ge(sb_T, i * 3 + 3)

                    def scores(j):
                        h2, s = blocks[j]
                        pe.wait_ge(sb_sp, i * NBK + (j + 1))
                        pe.matmul(ps[:, 2 + j % 2, 0:(NT - s) * P], kT_s[:, s * P:(s + 1) * P], q_s(h2)[:, s * P:SEQ],
                                  start=True, stop=True).then_inc(sb_z, 1)

                    def values(h2):
                        pe.wait_ge(sb_a, i * NBK + (4 * h2 + 6))
                        pe.wait_ge(sb_mixed, i * 2 + (h2 + 1))
                        for t in range(NT):
                            for s in range(t + 1):
                                mm = pe.matmul(ps[:, 6, (NT * h2 + t) * DH:(NT * h2 + t + 1) * DH], a_s(h2, s)[:, (t - s) * P:(t - s + 1) * P],
                                               z[:, s, bass.ds(i * P + (SV * HW + h2 * DH), DH)], start=(s == 0), stop=(s == t))
                        mm.then_inc(sb_o, 1)

                    def sample_page(j):
                        if j % NPG == 0:
                            pe.wait_ge(ds_stage, i + 1)
                            pe.wait_ge(ds_om, i * 2 + (j // NPG + 1))
                        pe.wait_ge(page_loaded[j % 4], i * 64 + 16 * (NB * NPG // 4 + j // 4 + 1))
                        row = j % 4 * 32
                        pe.matmul(ps[row:row + 32, 7, :], a_st[:, j, :], pages[:, j % 4, :],
                                  start=(j % NPG < 4), stop=(j % NPG >= 4)).then_inc(page_free, 1)

                    scores(0)
                    scores(1)
                    for j, (h2, s) in enumerate(blocks):
                        N = (NT - s) * P
                        bank = 4 + j % 2
                        pe.wait_ge(sb_sp, i * NBK + (j + 3))
                        pe.wait_ge(sb_a, i * NBK + (j + 1))
                        pe.matmul(ps[:, bank, 0:N], cst("tri_neg"), sp_s(h2, s), start=True, stop=False)
                        for j2 in range(s + 1, NT):
                            pe.matmul(ps[:, bank, (j2 - s) * P:N], cst("ones_neg"), sp_s(h2, j2), start=False, stop=False)
                        pe.matmul(ps[:, bank, 0:N], kT_s[:, s * P:(s + 1) * P], q_s(h2)[:, s * P:SEQ],
                                  start=False, stop=True).then_inc(sb_la, 1)
                        if j + 2 < NBK:
                            scores(j + 2)
                        if j == 4:
                            values(0)
                        sample_page(2 * j)
                        sample_page(2 * j + 1)
                    values(1)
                pe.wait_ge(ds_om, NB + 1)
                for b in range(NB):
                    mm = pe.matmul(ps[0:NB, 1, :], cst("to_row")[:, b * NB:(b + 1) * NB], om[:, b * HW:(b + 1) * HW],
                                   start=(b == 0), stop=(b == NB - 1))
                mm.then_inc(ds_row, 1)
                pe.wait_ge(sb_mixed, H + 2)
                turn(lambda t, k: z[0:rows[t], t, ((RG if k < 4 else SG) * HW + (k % 4) * P):((RG if k < 4 else SG) * HW + (k % 4 + 1) * P)],
                     mix_turned, None, mix_T, 0, [(ds_mixed, 1), (rs_done, 1)])
                for u in range(2):
                    pe.wait_ge(w_loaded[u], 16 * 5)
                    project(NCHUNK0 + u, u, mix_T, 0)

                turn(lambda t, k: work[0:rows[t], (t % 2) * D + k * P:(t % 2) * D + (k + 1) * P],
                     xt_summed, xn_ready, xnT_ready, 5)
                with pe.Fori(0, 2) as i:
                    for u in range(2):
                        pe.wait_ge(w_loaded[u], i * 16 + 16 * 6)
                        project(i * 2 + (10 + u), u, xnT_ready, 5)
                for u in range(2):
                    pe.wait_ge(w_loaded[u], 16 * 8)
                    project(14 + u, u, xnT_ready, 5, (CH, W1 - 5 * CH)[u])

                for w in range(2):
                    with pe.Fori(0, 2) as r:
                        for t in range(4):
                            for q in range(2):
                                pe.wait_ge(cm_loaded[t][q], r * 64 + 64 * (2 * w + 1))
                                pe.wait_ge(cm_T, r * 8 + (16 * w + 2 * t + q + 1))
                                for m in range(4):
                                    mm = pe.transpose(ps[:, 5 + q, m * P:(m + 1) * P], cm_pages[t][q][:, m * P:(m + 1) * P], ident)
                                mm.then_inc(cm_turned, 1)
                    if w == 0:
                        pe.wait_ge(bank_free, 5 + 80)
                    else:
                        pe.wait_ge(cmp_T, 1)
                    for t in range(NT):
                        col = (KC, VC)[w]
                        mm = pe.transpose(ps[:, 4, t * P:(t + 1) * P], z[:, t, col:col + P], ident)
                    mm.then_inc(cmp_turned, 1)
                    pe.wait_ge(cm_T, 2 + 16 * (w + 1))
                    pe.wait_ge(cmp_T, w + 1)
                    pe.wait_ge(wcmp_loaded[w], 32)
                    for l in range(CB):
                        mm = pe.matmul(ps[:, 7 if w == 0 else 3, 0:N_CMP], wcmp[w][:, l, :], kcT[:, l, :], start=(l == 0), stop=(l == CB - 1))
                    mm.then_inc(cm_proj, 1)
                    if w == 0:
                        pe.wait_ge(cm_sq, 1)
                        pe.matmul(ps[:, 2, 0:N_CMP], cst("mean_ones"), rk1, start=True, stop=True).then_inc(cm_mean, 1)
                    if w == 0:
                        pe.wait_ge(r_back, 48)
                        pe.matmul(ps[:, 0, 0:4 * DH], cst("spread", NB * G), kn_bg, start=True, stop=True).then_inc(*marks_pe.next("r_spread"))
                        pe.wait_ge(*marks_dve.at("r_dup"))
                        pe.transpose(ps[:, 1, 0:P], q_dup, ident).then_inc(*marks_pe.next("r_turned"))
                        pe.wait_ge(*marks_act.at("r_QT"))
                        pe.wait_ge(ckT_ready, 1)
                        pe.matmul(ps[:, 2, 0:NB * NCB], QT, ckT[:, 0:NB * NCB], start=True, stop=True).then_inc(*marks_pe.next("i_s"))
                        pe.wait_ge(*marks_dve.at("i_p"))
                        for j in range(2):
                            pe.transpose(ps[:, 3, j * P:(j + 1) * P], p_imp[:, j * P:(j + 1) * P], ident)
                        pe.matmul(ps[0:NB * G, 0, 0:NB * NCB], cst("group_sum"), p_imp, start=True, stop=True).then_inc(*marks_pe.next("i_sum"))
                        pe.wait_ge(*marks_act.at("i_T"))
                pe.wait_ge(cvT_ready, 2)
                for j in range(2):
                    pe.transpose(ps[:, 4, j * P:(j + 1) * P], cvT[:, j * P:(j + 1) * P], ident)
                pe.transpose(ps[:, 4, 2 * P:3 * P], cvT_pair, ident).then_inc(cv_turned, 1)
                pe.wait_ge(cv_ready, 1)
                for j in range(2):
                    mm = pe.matmul(ps[:, 3, 0:P], p_impT[:, j], cv_s[:, j * P:(j + 1) * P], start=(j == 0), stop=(j == 1))
                mm.then_inc(*marks_pe.next("i_o"))

                pe.wait_ge(heads_ready, 2)
                pe.wait_ge(ckT_ready, 1)
                for w in range(2):
                    for t in range(NT):
                        col = (KS, KW)[w]
                        mm = pe.transpose(ps[:, w, t * P:(t + 1) * P], z[:, t, col:col + P], ident)
                mm.then_inc(kz_turned, 1)
                pe.wait_ge(kz_T, 2)
                for w in range(2):
                    pe.matmul(ps[:, 5 + w, :], cst("swap"), xk(w), start=True, stop=True)
                pe.matmul(ps[:, 7, 0:NPB], cst("swap"), ckT[:, NB * NCB:N_CMP], start=True, stop=True).then_inc(kz_swapped, 1)

                pe.wait_ge(kz_ready, 3)
                pe.wait_ge(cv_ready, 1)
                def turn_q():
                    for t in range(NT):
                        mm = pe.transpose(ps[:, 3, t * P:(t + 1) * P], q_tok[:, t * P:(t + 1) * P], ident)
                    mm.then_inc(nq_turned, 1)

                pe.wait_ge(nq_staged, 1)
                turn_q()
                for g in range(G):
                    if g == 1:
                        pe.wait_ge(sk_T, 1 + 4 * NB)
                        pe.wait_ge(n_p, 4 + 64)
                        pe.wait_ge(*marks_dve.at("i_neg"))
                        for w in range(2):
                            pe.matmul(ps[:, w, :], cst("spread", NB * G),
                                      bc(pick[:, 64 + 8 * w:72 + 8 * w].unsqueeze(2), [NB * G, 8, DH]), start=True, stop=False)
                            for n in range(4):
                                pe.matmul(ps[:, w, n * P:(n + 1) * P], PT1[4 * w + n], ident, start=False, stop=(n == 3))
                        for n in range(4):
                            mm = pe.matmul(ps[:, 2, n * P:(n + 1) * P], PT1[8 + n], ident, start=True, stop=(n > 0))
                            if n == 0:
                                pe.matmul(ps[:, 2, 0:1], cst("spread", NB * G), cst("strict_neg", NB * G)[:, 0:1], start=False, stop=True)
                        mm.then_inc(*marks_pe.next("sk_back"))
                        pe.sem_inc(sv_used, 3)
                        pe.wait_ge(*marks_act.at("sk_exp"))
                        for n in range(12):
                            mm = pe.transpose(ps[:, n // 4, (n % 4) * P:(n % 4 + 1) * P], Pexp[:, n * P:(n + 1) * P], ident)
                        mm.then_inc(*marks_pe.next("sk_pturned"))
                        pe.wait_ge(*marks_act.at("sk_PT"))
                    with pe.Fori(0, HPG // 2) as j:
                        i = j + g * (HPG // 2)

                        def sample_keys(b2, q):
                            pe.wait_ge(nc_T, i + 1)
                            pe.wait_ge(sk_T, i * 8 + (4 * b2 + q + 1))
                            if q < 3:
                                pe.wait_ge(sk_loaded[q], (i * 128 + 64 * (b2 + 1)) if q < 2 else (i * 32 + 16 * (b2 + 1)))
                                for m in range(4):
                                    mm = pe.transpose(ps[:, 3, m * P:(m + 1) * P], slot1[:, q, m * P:(m + 1) * P], ident)
                                mm.then_inc(sk_turned, 1)
                            else:
                                for n in range(12):
                                    mm = pe.matmul(ps[:, 3, n * HN:(n + 1) * HN], KTs[n // 4][:, (n % 4) * P:(n % 4 + 1) * P],
                                                   q_one, start=True, stop=True)
                                mm.then_inc(sk_scored, 1)

                        def sample_values(b2):
                            pe.wait_ge(nc_T, i + 1)
                            pe.wait_ge(sv_T, j * 2 + (b2 + 1))
                            pe.wait_ge(sv_staged, j * 2 + (b2 + 1))
                            for q in range(3):
                                pe.wait_ge(sv_loaded[q], (j * 128 + 64 * (b2 + 1)) if q < 2 else (j * 32 + 16 * (b2 + 1)))
                                for m in range(4):
                                    n = 4 * q + m
                                    mm = pe.matmul(ps[:, 3, (q // 2) * HN:(q // 2 + 1) * HN], slot1[:, q, m * P:(m + 1) * P],
                                                   p_one[:, n * HN:(n + 1) * HN], start=(n in (0, 8)), stop=(n in (7, 11)))
                                mm.then_inc(sv_used, 1)

                        def s1(u):
                            t, h2, br = units[u]
                            N = (t + 1) * P
                            pe.wait_ge(n_p, i * 16 + (u + 2 if u > 2 else 4))
                            mm = pe.matmul(ps[:, u % 3, 0:N], qTs[:, t * P:(t + 1) * P], Kz[:, g, h2, br * SEQ:br * SEQ + N],
                                      start=True, stop=u >= MASK_PE)
                            if u < MASK_PE:
                                mm = pe.matmul(ps[:, u % 3, t * P:N], ident, cst("causal_neg"), start=False, stop=True)
                            mm.then_inc(n_s, 1)

                        def turn_p(u):
                            t, h2, br = units[u]
                            pe.wait_ge(n_p, i * 16 + (u + 5))
                            pe.wait_ge(n_pt, i * 16 + (u + 1))
                            for s in range(t + 1):
                                mm = pe.transpose(ps[:, 4 + br, s * P:(s + 1) * P], z[:, u % 4, P_OFF + s * P:P_OFF + (s + 1) * P], ident)
                            mm.then_inc(n_t, 1)

                        def turn_c():
                            pe.wait_ge(nc_p, i + 1)
                            for t in range(NT):
                                mm = pe.transpose(ps[:, 3, t * P:(t + 1) * P], p_cmp[:, t].rearrange("p u n -> p (u n)"), ident)
                            mm.then_inc(nc_turned, 1)

                        def av(u):
                            t, h2, br = units[u]
                            pe.wait_ge(n_pt, i * 16 + (u + 3))
                            if u % 4 == 0:
                                pe.wait_ge(n_o, i * 4 + (t + 1))
                            if u % 4 == 3:
                                pe.wait_ge(nc_T, i + 1)
                                pe.matmul(ps[:, 6 + t % 2, 0:P], p_cmpT[:, t * P:(t + 1) * P],
                                          cv_pair[:, g * P:(g + 1) * P], start=True, stop=True)
                            for s in range(t + 1):
                                col = (VS, VW)[br]
                                mm = pe.matmul(ps[:, 6 + t % 2, P + br * P + h2 * DH:P + br * P + (h2 + 1) * DH],
                                               z[:, u % 4, PT_OFF + s * P:PT_OFF + (s + 1) * P],
                                               z[:, s, g * DH + col:(g + 1) * DH + col], start=(s == 0), stop=(s == t))
                            mm.then_inc(n_av, 1)

                        pe.wait_ge(nq_T, i + 1)
                        s1(0)
                        for t in range(NT):
                            for h2 in range(2):
                                c = (2 * t + h2) * NPB
                                mm = pe.matmul(ps[:, 3, c:c + NPB], qTs[:, t * P:(t + 1) * P],
                                               Kz[:, g, h2, 2 * SEQ:KZ], start=True, stop=True)
                        mm.then_inc(nc_s, 1)
                        s1(1)
                        s1(2)
                        for u in range(16):
                            if u + 3 < 16:
                                s1(u + 3)
                            turn_p(u)
                            if u == 2:
                                turn_c()
                            if u:
                                av(u - 1)
                            if g == 0 and u in KEY_STEPS:
                                sample_keys(*KEY_STEPS[u])
                            if g == 1 and u in VALUE_STEPS:
                                sample_values(VALUE_STEPS[u])
                            if u == 14:
                                pe.wait_ge(nc_T, i + 1)
                                pe.wait_ge(nq_staged, i + 2)
                                pe.wait_ge(*((sk_T, i * 8 + 9) if g == 0 else (sv_T, j * 2 + 3)))
                                turn_q()
                        av(15)

                pe.wait_ge(sv_T, 1 + NB)
                for w in range(2):
                    mm = pe.transpose(ps[:, 2, w * P:(w + 1) * P], oT1[:, w], ident)
                mm.then_inc(*marks_pe.next("sv_back"))

                pe.wait_ge(n_mix, 2 + 4 * (HN // 2))
                turn(lambda t, k: z[0:rows[t], t, GATE + k * P:GATE + (k + 1) * P], mix_turned, None, mix_T, 5,
                     [marks_dve.at("sv_done")])
                for u in range(2):
                    pe.wait_ge(w_loaded[u], 16 * 9)
                    project(16 + u, u, mix_T, 5)

            @block.scalar
            def _(act):
                st = Steps(act, act_step)

                def rsqrt(a, n, sem_, value):
                    st.done(nc.scalar.activation(a, a, ACT.Ln, bias=EPS, scale=1.0 / n))
                    nc.scalar.activation(a, a, ACT.Exp, scale=-0.5).then_inc(sem_, 1)
                    act.wait_ge(sem_, value)

                def norm_x(layer):
                    for t in range(NT + 1):
                        r = rows[t]
                        if layer == 1:
                            act.wait_ge(bank_free, 5 + 45 + t + 1)
                        st.done(nc.scalar.activation(work[0:r, 2 * D:3 * D], xres[0:r, t, :], ACT.Square,
                                                     accum_out=stats[0:r, 80 + t:81 + t]))
                    rsqrt(stats[:, 80:85], D, rstd_x, layer + 1)
                    for t in range(NT + 1):
                        r, n = rows[t], 5 * layer + t
                        if t >= 2:
                            act.wait_ge(xt_summed, n - 1)
                        nc.scalar.activation(work[0:r, (t % 2) * D:(t % 2 + 1) * D], xres[0:r, t, :], ACT.Copy,
                                             scale=stats[0:r, 80 + t:81 + t]).then_inc(xn_ready, 1)

                LOG_EXP = "natural_log_exp_and_others"
                nc.scalar.preload_act_table_set(LOG_EXP)
                act.wait_ge(s_x, 32)
                act.wait_ge(zeroed_stats, 1)
                norm_x(0)
                act.sem_inc(bank_free, 5)
                for n in range(NCHUNK0):
                    if n == 0:
                        act.wait_ge(xn_ready, 5)
                        act.wait_ge(xnT_ready, 5)
                    for t in range(NT + 1):
                        act.wait_ge(mm_done, 5 * n + t + 1)
                        for row, a, e in (quarters(0, CH) if t == NT else [(0, 0, CH)]):
                            ins_ = nc.scalar.activation(sec(t, n)[:, a:e], ps[row:row + rows[t], t, 0:e - a],
                                                        ACT.Silu if n in (SG, RG) else ACT.Copy)
                        ins_.then_inc(bank_free, 1)
                    if n in (SQ, SK):
                        act.wait_ge(ssq_ready, n + 1)
                        rsqrt(stats[:, 0:40], DH, rstd_ready, n + 1)
                        if n == SQ:
                            act.wait_ge(sections_ready, 1)
                            act.dma_start(d_sq, sec(NT, SQ)).then_inc(sq_sent, 16)
                            act.wait_ge(sq_sent, 16)
                            act.dma_start(arena[:, NX:NX + NQ], d_sq.rearrange("(o b) c -> o (b c)", o=1)[0].partition_broadcast(P)).then_inc(sq_spread, 16)

                def softplus_tail(src, dst, sem_):
                    st.done(nc.scalar.activation(dst, src, ACT.Abs))
                    st.done(nc.scalar.activation(dst, dst, ACT.Exp, scale=-1.0))
                    nc.scalar.activation(dst, dst, ACT.Ln, bias=1.0).then_inc(sem_, 1)

                nc.scalar.preload_act_table_set(LOG_EXP)
                act.wait_ge(ds_scores, 1)
                softplus_tail(zs, lnz, ds_ln)

                act.wait_ge(sections_ready, 4)
                act.wait_ge(bank_free, 5 + 5 * NCHUNK0)

                def ret_stage(t):
                    nc.scalar.activation(qk_st.rearrange("p (a c) -> p a c", a=1), z[:, bass.ds(t, 1), RQ * HW:(RK + 1) * HW],
                                         ACT.Copy).then_inc(ret_staged, 1)

                def ret_copies(t):
                    act.wait_ge(ret_turned, t + 1)
                    for u in range(2):
                        half = slice(u * DH, (u + 1) * DH)
                        nc.scalar.activation(qBD[half, :, u, :], ps[half, 0, :].rearrange("p (a n) -> p a n", a=NHP), ACT.Copy).then_inc(ret_T, 1)
                    nc.scalar.activation(kT_r, ps[:, 1, :], ACT.Copy).then_inc(ret_T, 1)

                def ret_norm(t):
                    act.wait_ge(gn_sum, t + 1)
                    st.done(nc.scalar.activation(stats[:, 40:48], stats[:, 40:48], ACT.Ln, bias=EPS, scale=1.0 / DH))
                    nc.scalar.activation(stats[:, 40:48], stats[:, 40:48], ACT.Exp, scale=-0.5).then_inc(gn_rstd, 1)

                ret_stage(0)
                ret_copies(0)
                act.wait_ge(ret_kd, 1)
                ret_stage(1)
                with st.loop(NT - 2, 1, first=1) as t:
                    act.wait_ge(ret_o, t)
                    ret_copies(t)
                    act.wait_ge(ret_kd, t + 1)
                    ret_stage(t + 1)
                    ret_norm(t - 1)
                act.wait_ge(ret_o, NT - 1)
                ret_copies(NT - 1)
                ret_norm(NT - 2)
                ret_norm(NT - 1)
                act.wait_ge(rs_sum, 1)
                for j in range(4):
                    ins_ = nc.scalar.activation(B_rs[0:2, j * 512:(j + 1) * 512], ps[32 * j:32 * j + 2, 6, :], ACT.Copy)
                ins_.then_inc(rs_row, 1)
                act.wait_ge(ds_lasum, 1)
                nc.scalar.activation(zs, zs, ACT.Exp).then_inc(ds_a, 1)

                act.wait_ge(ds_a, 1)
                act.wait_ge(zeroed, 2)
                act.sem_inc(sb_a, 2)
                with st.loop(NHP, 2 * NBK) as i:
                    act.wait_ge(page_free, i * 2 * NPG + (4 + NB * NPG))
                    nc.scalar.activation(a_st[:, :, 0:H], zs[:, bass.ds(i * 2 * NPG * H, 2 * NPG * H)].rearrange("p (j h) -> p j h", h=H),
                                         ACT.Copy).then_inc(ds_stage, 1)
                    nc.scalar.activation(xflat[:, 0:1024].rearrange("p (t w c) -> p t w c", t=NT, w=2),
                                         z[:, 0:NT, 0:2 * HW].rearrange("p t (w c) -> p t w c", w=2)[:, :, :, bass.ds(i * P, P)],
                                         ACT.Copy).then_inc(sb_staged, 1)
                    act.wait_ge(sb_turned, i + 1)
                    for u in range(2):
                        half = slice(u * DH, (u + 1) * DH)
                        nc.scalar.activation(q_s(u)[half], ps[half, 0, :], ACT.Copy, scale=SCALE).then_inc(sb_T, 1)
                    nc.scalar.activation(kT_s, ps[:, 1, :], ACT.Copy).then_inc(sb_T, 1)

                    def tail_of(j):
                        h2, s = blocks[j]
                        act.wait_ge(sb_z, i * NBK + (j + 1))
                        act.wait_ge(sb_sp, i * NBK + (j + 1))
                        softplus_tail(ps[:, 2 + j % 2, 0:(NT - s) * P], (tmp, tmp2)[j % 2][:, 0:(NT - s) * P], sb_ln)

                    tail_of(0)
                    for j, (h2, s) in enumerate(blocks):
                        if j + 1 < NBK:
                            tail_of(j + 1)
                        act.wait_ge(sb_masked, i * NBK + (j + 1))
                        act.wait_ge(sb_mixed, i * 2 + (h2 + 1))
                        nc.scalar.activation(a_s(h2, s), ps[:, 4 + j % 2, 0:(NT - s) * P], ACT.Exp).then_inc(sb_a, 1)

                act.wait_ge(gn_sum, NT + 1)
                rsqrt(stats[0:NB, 40:48], DH, gn_rstd, NT + 1)
                act.wait_ge(w_loaded[0], 16 * 5)
                for t in range(NT + 1):
                    act.wait_ge(mix_turned, t + 1)
                    b, r = 4 + 2 * (t % 2), rows[t]
                    nc.scalar.activation(xnT[:, :, t * P:t * P + r],
                                         ps[:, b:b + 2, :].rearrange("p b (k n) -> p (b k) n", k=4)[:, :, 0:r], ACT.Copy).then_inc(mix_T, 1)

                nc.scalar.preload_act_table_set(LOG_EXP)
                norm_x(1)
                for c in range(NC1):
                    n = 10 + c
                    w = min(CH, W1 - c * CH)
                    lo, hi = min(max(GATE - c * CH, 0), w), min(max(BG - c * CH, 0), w)
                    parts = [(0, lo, ACT.Copy), (lo, hi, ACT.Silu), (hi, w, ACT.Sigmoid)]
                    parts = [x for x in parts if x[1] > x[0]]
                    for k, (a, e, f) in enumerate(parts):
                        for t in range(NT + 1):
                            act.wait_ge(mm_done, 5 * n + t + 1)
                            if t < NT:
                                ins_ = nc.scalar.activation(z[:, t, c * CH + a:c * CH + e], ps[:, t, a:e], f)
                            else:
                                for row, a2, e2 in quarters(a, e):
                                    ins_ = nc.scalar.activation(z[0:NB, NT, c * CH + a2:c * CH + e2], ps[row:row + NB, NT, 0:e2 - a2], f)
                            if k == len(parts) - 1:
                                ins_.then_inc(bank_free, 1)
                    if c in (1, 3):
                        act.wait_ge(k_ssq, (c + 1) // 2)
                        rsqrt(stats[:, 0:80], DH, k_rstd, (c + 1) // 2)
                nc.scalar.preload_act_table_set(LOG_EXP)
                act.wait_ge(s_table, 16)
                for t in range(4):
                    act.wait_ge(cm_turned, 2 * t + 2)
                    page_group(act, "cache_cmp_k", (4 + t) * NPG + 4, cm_pages[t][1], cm_loaded[t][1])
                for t in range(4):
                    act.wait_ge(cm_turned, 8 + 2 * t + 2)
                    page_group(act, "cache_cmp_v", t * NPG + 4, cm_pages[t][1], cm_loaded[t][1])
                act.wait_ge(cm_mean, 1)
                st.done(nc.scalar.activation(rk1, ps[:, 2, 0:N_CMP], ACT.Ln, bias=EPS))
                nc.scalar.activation(rk1, rk1, ACT.Exp, scale=-0.5).then_inc(cm_rstd, 1)
                act.wait_ge(*marks_pe.at("r_turned"))
                nc.scalar.activation(QT, ps[:, 1, 0:P], ACT.Copy).then_inc(*marks_act.next("r_QT"))
                act.wait_ge(*marks_dve.at("i_max"))
                nc.scalar.activation(p_imp, p_imp, ACT.Exp, bias=stats[:, 4:5], accum_out=stats[:, 5:6]).then_inc(*marks_act.next("i_exp"))
                act.wait_ge(*marks_pe.at("i_sum"))
                nc.scalar.activation(p_impT, ps[:, 3, 0:2 * P].rearrange("p (j c) -> p j c", j=2), ACT.Copy).then_inc(*marks_act.next("i_T"))
                for t in range(4):
                    act.wait_ge(cm_turned, 16 + 2 * t + 2)
                    page_group(act, "cache_cmp_v", (4 + t) * NPG + 4, cm_pages[t][1], cm_loaded[t][1])
                act.wait_ge(cm_proj, 2)
                nc.scalar.activation(cvT[:, 0:N_CMP], ps[:, 3, 0:N_CMP], ACT.Copy).then_inc(cvT_ready, 1)
                act.wait_ge(kz_turned, 1)
                for w in range(2):
                    nc.scalar.activation(xk(w), ps[:, w, :], ACT.Copy).then_inc(kz_T, 1)

                for u in range(2):
                    half = slice(u * DH, (u + 1) * DH)
                    ins_ = nc.scalar.activation(Kz[half, u, u, 0:2 * SEQ].rearrange("p (w n) -> p w n", w=2), ps[half, 0:2, :], ACT.Copy)
                ins_.then_inc(kz_ready, 1)
                act.wait_ge(kz_ready, 3)
                act.sem_inc(n_p, 4)
                act.sem_inc(n_pt, 2)
                nc.scalar.activation(q_tok.rearrange("p (t c) -> p t c", t=NT), z[:, 0:NT, 0:P], ACT.Copy).then_inc(nq_staged, 1)
                act.wait_ge(nq_turned, 1)
                nc.scalar.activation(qTs, ps[:, 3, :], ACT.Copy, scale=SCALE).then_inc(nq_T, 1)
                for g in range(G):
                    if g == 1:
                        act.wait_ge(*marks_dve.at("sk_max"))
                        st.done(nc.scalar.activation(Pexp[:, 0:1024], ps[:, 0:2, :].rearrange("p a c -> p (a c)"), ACT.Exp,
                                                     bias=stats[:, 8:9], accum_out=stats[:, 12:13]))
                        st.done(nc.scalar.activation(Pexp[:, 1024:1536], ps[:, 2, :], ACT.Exp, bias=stats[:, 9:10], accum_out=stats[:, 13:14]))
                        nc.scalar.activation(stats[:, 14:16], stats[:, 6:8], ACT.Exp).then_inc(*marks_act.next("sk_exp"))
                        act.wait_ge(*marks_pe.at("sk_pturned"))
                        nc.scalar.activation(PT1_sel, ps[:, 0:2, :].rearrange("p a c -> p (a c)"), ACT.Copy)
                        nc.scalar.activation(PT1_win, ps[:, 2, :], ACT.Copy).then_inc(*marks_act.next("sk_PT"))
                    with act.Fori(0, HPG // 2) as j:
                        i = j + g * (HPG // 2)

                        def exp(u):
                            t, h2, br = units[u]
                            N = (t + 1) * P
                            act.wait_ge(n_max, i * 16 + (u + 1))
                            act.wait_ge(n_t, i * 16 + (u + 1))
                            if u % 4 == 0:
                                act.wait_ge(n_o, i * 4 + (t + 1))
                            nc.scalar.activation(z[:, u % 4, P_OFF:P_OFF + N], ps[:, u % 3, 0:N], ACT.Exp, bias=nmax(u),
                                                 accum_out=dens(u)).then_inc(n_p, 1)

                        def load_window(b2):
                            win, loaded, used = (("cache_win_k", sk_loaded, sk_turned), ("cache_win_v", sv_loaded, sv_used))[g]
                            act.wait_ge(used, j * 6 + (3 * b2 + 3))
                            act.dma_start(slot1[:, 2].rearrange("p (t c) -> p t c", t=4),
                                          ins[win][bass.ds(j * 2 + b2, 1)].rearrange("b (t p) g d -> p (b t) (g d)", p=P)
                                          ).then_inc(loaded[2], 16)

                        exp(0)
                        exp(1)
                        for u in range(16):
                            t, h2, br = units[u]
                            N = (t + 1) * P
                            if u + 2 < 16:
                                exp(u + 2)
                            if u in WINDOW_STEPS:
                                load_window(WINDOW_STEPS[u])
                            if u == 0:
                                act.wait_ge(nc_max, i + 1)
                                nc.scalar.activation(p_cmp[:, :, :, 0:NPB], p_cmp[:, :, :, 0:NPB], ACT.Exp).then_inc(nc_exp, 1)
                            act.wait_ge(n_t, i * 16 + (u + 5))
                            act.wait_ge(n_av, i * 16 + (u + 1))
                            nc.scalar.activation(z[:, u % 4, PT_OFF:PT_OFF + N], ps[:, 4 + br, 0:N], ACT.Copy).then_inc(n_pt, 1)
                            if u == 2:
                                act.wait_ge(nc_turned, i + 1)
                                nc.scalar.activation(p_cmpT, ps[:, 3, :], ACT.Copy).then_inc(nc_T, 1)
                            if u == 8:
                                nc.scalar.activation(q_tok.rearrange("p (t c) -> p t c", t=NT), z[:, 0:NT, bass.ds(i * P + P, P)],
                                                     ACT.Copy).then_inc(nq_staged, 1)
                            if u == 14:
                                act.wait_ge(nq_turned, i + 2)
                                nc.scalar.activation(qTs, ps[:, 3, :], ACT.Copy, scale=SCALE).then_inc(nq_T, 1)

                for t in range(NT + 1):
                    act.wait_ge(mix_turned, 5 + t + 1)
                    b, r = 4 + 2 * (t % 2), rows[t]
                    nc.scalar.activation(xnT[:, :, t * P:t * P + r],
                                         ps[:, b:b + 2, :].rearrange("p b (k n) -> p (b k) n", k=4)[:, :, 0:r], ACT.Copy).then_inc(mix_T, 1)

            @block.vector
            def _(dve):
                st = Steps(dve, dve_step)
                TT, TS, STT, RED = (nc.vector.tensor_tensor, nc.vector.tensor_scalar,
                                    nc.vector.scalar_tensor_tensor, nc.vector.tensor_reduce)
                nc.vector.memset(stats[:], 1.0).then_inc(zeroed_stats, 1)
                dve.wait_ge(zeroed_stats, 1)
                dve.wait_ge(s_first, 16)

                def turned_x(layer):
                    gain = cst(f"gain_in{layer}")
                    for t in range(NT + 1):
                        r, n = rows[t], 5 * layer + t
                        dve.wait_ge(xt_summed, n + 1)
                        b = 4 + 2 * (t % 2)
                        TT(xnT[:, :, t * P:t * P + r], ps[:, b:b + 2, :].rearrange("p b (k n) -> p (b k) n", k=4)[:, :, 0:r],
                           bc(gain.unsqueeze(2), [P, KT, r]), ALU.mult).then_inc(xnT_ready, 1)

                turned_x(0)
                st.done(nc.vector.memset(S_ret[:], 0.0))
                dve.sem_inc(ret_S, 1)
                dve.wait_ge(xn_ready, 5)
                st.done(nc.vector.memset(qBD[0:DH, :, 1, :], 0.0))
                nc.vector.memset(qBD[DH:P, :, 0, :], 0.0).then_inc(zeroed, 1)
                dve.wait_ge(xt_summed, 5)

                def head_norm(n, gain):
                    dve.wait_ge(bank_free, 5 + 5 * (n + 1))
                    for t in range(NT + 1):
                        r = rows[t]
                        st.done(TT(tmp[0:r], sec(t, n), sec(t, n), ALU.mult))
                        red = RED(stats[0:r, 8 * t:8 * t + 8], heads(tmp[0:r]), AX.X, ALU.add)
                        if t < NT:
                            st.done(red)
                        else:
                            red.then_inc(ssq_ready, 1)
                    dve.wait_ge(rstd_ready, n + 1)
                    for t in reversed(range(NT + 1)):
                        r = rows[t]
                        st.done(TT(heads(sec(t, n)), heads(sec(t, n)), bc(stats[0:r, 8 * t:8 * t + 8].unsqueeze(2), [r, H, DH]), ALU.mult))
                        mul = TT(heads(sec(t, n)), heads(sec(t, n)), bc(cst(gain, r).unsqueeze(1), [r, H, DH]), ALU.mult)
                        if t:
                            st.done(mul)
                        else:
                            mul.then_inc(sections_ready, 1)
                            dve.wait_ge(sections_ready, n + 1)

                dve.wait_ge(s_aux, 16)
                head_norm(SQ, "gain_sq")
                head_norm(SK, "gain_sk")

                dve.wait_ge(sq_spread, 16)
                with st.loop(NB * NPG // 4, 4) as r:
                    for u in range(4):
                        dve.wait_ge(page_loaded[u], r * 16 + 16)
                        TT(tmp.rearrange("p (a c) -> p a c", a=1), pages[:, u:u + 1, :], qbc[:, bass.ds(r // 2, 1), :], ALU.mult).then_inc(page_free, 1)
                        dve.wait_ge(page_free, r * 4 + (4 + u + 1))
                        st.done(RED(zs[:, bass.ds(r * 4 * H + u * H, H)], heads(tmp), AX.X, ALU.add))
                TS(zs, zs, SCALE, None, ALU.mult).then_inc(ds_scores, 1)
                dve.wait_ge(ds_scores, 1)

                def rotate(n, value):
                    dve.wait_ge(bank_free, 5 + 5 * (n + 1))
                    hf = DH // 2
                    for t in range(NT + 1):
                        r = rows[t]
                        x = heads(sec(t, n))
                        cos = bc(cst("cosine", r)[:, t * DH:(t + 1) * DH].unsqueeze(1), [r, H, DH])
                        sin = cst("sine", r)[:, t * DH:(t + 1) * DH]
                        st.done(TT(heads(tmp[0:r]), x, cos, ALU.mult))
                        st.done(TT(heads(tmp2[0:r])[:, :, 0:hf], x[:, :, hf:DH], bc(sin[:, 0:hf].unsqueeze(1), [r, H, hf]), ALU.mult))
                        st.done(TT(heads(tmp2[0:r])[:, :, hf:DH], x[:, :, 0:hf], bc(sin[:, hf:DH].unsqueeze(1), [r, H, hf]), ALU.mult))
                        add = TT(sec(t, n), tmp[0:r], tmp2[0:r], ALU.add)
                        if t < NT:
                            st.done(add)
                        else:
                            add.then_inc(sections_ready, 1)
                            dve.wait_ge(sections_ready, value)

                rotate(RQ, 3)
                rotate(RK, 4)
                dve.wait_ge(ds_ln, 1)
                st.done(STT(spz, zs, 0.0, lnz, ALU.max, ALU.add))
                pg = lambda a, j: a.rearrange("p (b j h) -> p b j h", b=NB, j=NPG)[:, :, j, :]
                st.done(nc.vector.memset(pg(tail, NPG - 1), 0.0))
                for j in reversed(range(NPG - 1)):
                    add = TT(pg(tail, j), pg(tail, j + 1), pg(spz, j + 1), ALU.add)
                    if j:
                        st.done(add)
                    else:
                        add.then_inc(ds_sp, 1)

                def group_norm(o, r, gate, n, sem_, wait=None):
                    mean, var = stats[0:r, 48:56], stats[0:r, 40:48]
                    st.done(RED(mean, heads(o), AX.X, ALU.add))
                    st.done(TS(mean, mean, 1.0 / DH, None, ALU.mult))
                    st.done(TT(heads(o), heads(o), bc(mean.unsqueeze(2), [r, H, DH]), ALU.subtract))
                    st.done(TT(tmp[0:r], o, o, ALU.mult))
                    RED(var, heads(tmp[0:r]), AX.X, ALU.add).then_inc(gn_sum, 1)
                    dve.wait_ge(gn_rstd, n)
                    st.done(TT(heads(o), heads(o), bc(var.unsqueeze(2), [r, H, DH]), ALU.mult))
                    st.done(TT(o, o, cst("gain_ret", r), ALU.mult))
                    TT(gate, gate, o.rearrange("p (a c) -> p a c", a=1), ALU.mult).then_inc(sem_, 1)

                dve.wait_ge(rs_turned, 1)
                st.done(nc.vector.tensor_copy(kqT[:], ps[:, 6, 0:2 * NHP * NB]))
                kq = kqT[:].rearrange("p (w a b) -> p w b a", w=2, b=NB)
                dve.wait_ge(rs_in, 16 * 18)
                st.done(TT(by_pair(B_rs), by_pair(B_rs), bc(kq[:, 1].unsqueeze(3), [P, NB, NHP, DH]), ALU.mult))
                st.done(TT(by_pair(A_rs), by_pair(A_rs), bc(cst("gamma").unsqueeze(1).unsqueeze(3), [P, NB, NHP, DH]), ALU.mult))
                STT(A_rs, B_rs, SCALE, A_rs, ALU.mult, ALU.add).then_inc(rs_S, 1)
                dve.wait_ge(rs_S, 1)
                TT(by_pair(B_rs), by_pair(A_rs), bc(kq[:, 0].unsqueeze(3), [P, NB, NHP, DH]), ALU.mult).then_inc(rs_t, 1)
                dve.wait_ge(ds_la, 1)
                TT(zs, zs, ps[:, 7, :], ALU.add).then_inc(ds_lasum, 1)

                dve.wait_ge(bank_free, 5 + 5 * NCHUNK0)

                def ret_weights(t):
                    dve.wait_ge(ret_att, t + 1)
                    for j in range(2):
                        TT(attm[:, j * 512:(j + 1) * 512], ps[:, 2 + j, :], cst("ret_decay")[:, j * 512:(j + 1) * 512], ALU.mult).then_inc(ret_attm, 1)

                def ret_out(t):
                    dve.wait_ge(ret_o, t + 1)
                    st.done(TT(heads(o_tmp), heads(ps[:, 4, :]), bc(cst("q_decay").unsqueeze(2), [P, H, DH]), ALU.mult))
                    st.done(TT(S_ret[:], S_ret[:], bc(cst("chunk_decay").unsqueeze(2), [P, NHP, DH]), ALU.mult))
                    dve.wait_ge(ret_kv, t + 1)
                    kv = ps[:, 5, :].rearrange("p (a c) -> p a c", a=NHP)
                    st.done(TT(S_ret[0:DH], S_ret[0:DH], kv[0:DH, :, 0:DH], ALU.add))
                    TT(S_ret[DH:P], S_ret[DH:P], kv[DH:P, :, DH:P], ALU.add).then_inc(ret_S, 1)
                    dve.wait_ge(ret_S, t + 2)

                def ret_norm(t):
                    group_norm(o_tmp, P, z[:, bass.ds(t, 1), RG * HW:(RG + 1) * HW], t + 1, ret_done)
                    dve.wait_ge(ret_done, t + 1)

                ret_weights(0)
                ret_out(0)
                with st.loop(NT - 2, 9, first=1) as t:
                    ret_weights(t)
                    ret_norm(t - 1)
                    ret_out(t)
                ret_weights(NT - 1)
                ret_norm(NT - 2)
                ret_out(NT - 1)
                ret_norm(NT - 1)

                st.done(nc.vector.memset(a_st, 0.0))
                st.done(nc.vector.memset(q_s(0)[DH:P], 0.0))
                nc.vector.memset(q_s(1)[0:DH], 0.0).then_inc(zeroed, 1)
                dve.sem_inc(sb_sp, 2)
                dve.sem_inc(sb_mixed, 2)
                dve.sem_inc(ds_om, 1)
                with st.loop(NHP, NBK) as i:
                    def softplus(j):
                        h2, s = blocks[j]
                        N = (NT - s) * P
                        dve.wait_ge(sb_ln, i * NBK + (j + 1))
                        st.done(STT(sp_s(h2, s), ps[:, 2 + j % 2, 0:N], 0.0, (tmp, tmp2)[j % 2][:, 0:N], ALU.max, ALU.add))
                        TT(sp_s(h2, s)[:, 0:P], sp_s(h2, s)[:, 0:P], cst("strict"), ALU.mult).then_inc(sb_sp, 1)

                    def mix(h2):
                        dve.wait_ge(sb_o, i * 2 + (h2 + 1))
                        gate = z[:, 0:NT, bass.ds(i * P + (SG * HW + h2 * DH), DH)]
                        TT(gate, gate, ps[:, 6, h2 * NT * DH:(h2 + 1) * NT * DH].rearrange("p (t d) -> p t d", d=DH), ALU.mult).then_inc(sb_mixed, 1)

                    def own_columns(b2):
                        dve.wait_ge(page_free, i * 2 * NPG + (4 + NB * NPG + NPG * (b2 + 1)))
                        TT(om[:, bass.ds(i * 2 * HW + b2 * HW, HW)], ps[:, 7, :], cst("own_head"), ALU.mult).then_inc(ds_om, 1)

                    softplus(0)
                    for j, (h2, s) in enumerate(blocks):
                        if j + 1 < NBK:
                            softplus(j + 1)
                        if j == 4:
                            own_columns(0)
                        dve.wait_ge(sb_la, i * NBK + (j + 1))
                        TT(ps[:, 4 + j % 2, 0:P], ps[:, 4 + j % 2, 0:P], cst("strict_neg"), ALU.add).then_inc(sb_masked, 1)
                        if j == 5:
                            mix(0)
                    mix(1)
                    own_columns(1)

                dve.wait_ge(rs_back, 32)
                group_norm(B_rs[0:NB, 0:HW], NB, sec(NT, RG).rearrange("p (a c) -> p a c", a=1), NT + 1, rs_done)
                dve.wait_ge(ds_row, 1)
                TT(sec(NT, SG), sec(NT, SG), ps[0:NB, 1, :], ALU.mult).then_inc(ds_mixed, 1)

                def add_residual(n, u):
                    for t in range(NT + 1):
                        dve.wait_ge(mm_done, 5 * n + t + 1)
                        for row, a, e in (quarters(0, CH) if t == NT else [(0, 0, CH)]):
                            x = xres[0:rows[t], t, u * CH + a:u * CH + e]
                            add = TT(x, x, ps[row:row + rows[t], t, 0:e - a], ALU.add)
                        add.then_inc(bank_free, 1)

                dve.wait_ge(xr_loaded, 32)
                for u in range(2):
                    add_residual(NCHUNK0 + u, u)


                turned_x(1)

                def squares(a, t, col, n):
                    r = rows[t]
                    x = z[0:r, t, a:a + n * DH]
                    st.done(TT(tmp3[0:r, 0:n * DH], x, x, ALU.mult))
                    return RED(stats[0:r, col:col + n], heads(tmp3[0:r, 0:n * DH]), AX.X, ALU.add)

                def scaled(a, t, col, n, gain):
                    r = rows[t]
                    x = heads(z[0:r, t, a:a + n * DH])
                    st.done(TT(x, x, bc(stats[0:r, col:col + n].unsqueeze(2), [r, n, DH]), ALU.mult))
                    return TT(x, x, bc(cst(gain, r).unsqueeze(1), [r, n, DH]), ALU.mult)

                st.done(nc.vector.memset(stats[:], 1.0))
                for c in range(2):
                    dve.wait_ge(bank_free, 5 + 5 * (11 + c))
                    for t in range(NT + 1):
                        red = squares(c * CH, t, 16 * t + 8 * c, 8)
                        if c == 1 and t == NT:
                            red.then_inc(k_ssq, 1)
                        else:
                            st.done(red)
                dve.wait_ge(k_rstd, 1)
                for t in range(NT + 1):
                    mul = scaled(Q1, t, 16 * t, HN, "gain_q")
                    mul.then_inc(heads_ready, 1) if t == NT else st.done(mul)
                dve.wait_ge(heads_ready, 1)
                dve.wait_ge(bank_free, 5 + 5 * 14)
                for t in range(NT + 1):
                    st.done(squares(KS, t, 16 * t, 2))
                    red = squares(KW, t, 16 * t + 2, 2)
                    red.then_inc(k_ssq, 1) if t == NT else st.done(red)
                dve.wait_ge(k_rstd, 2)
                for t in range(NT + 1):
                    st.done(scaled(KS, t, 16 * t, 2, "gain_sel"))
                    mul = scaled(KW, t, 16 * t + 2, 2, "gain_win")
                    st.done(mul)
                dve.wait_ge(bank_free, 5 + 80)
                dve.sem_inc(heads_ready, 1)

                dve.sem_inc(cm_T, 2)
                for w in range(2):
                    if w == 1:
                        dve.wait_ge(cm_proj, 1)
                    with dve.Fori(0, NB) as b:
                        for q in range(2):
                            dve.wait_ge(cm_turned, b * 2 + (16 * w + q + 1))
                            TT(kcT[:, :, bass.ds(b * NCB + q * NPB, NPB)].rearrange("p l n -> p n l"),
                               ps[:, 5 + q, :].rearrange("p (n l) -> p n l", l=CB),
                               bc(cst("pe").unsqueeze(1), [P, NPB, CB]), ALU.add).then_inc(cm_T, 1)
                    dve.wait_ge(cmp_turned, w + 1)
                    TT(kcT[:, :, NB * NCB:N_CMP].rearrange("p l n -> p n l"), ps[:, 4, :].rearrange("p (n l) -> p n l", l=CB),
                       bc(cst("pe").unsqueeze(1), [P, NPB, CB]), ALU.add).then_inc(cmp_T, 1)
                    if w == 0:
                        dve.wait_ge(cm_proj, 1)
                        st.done(nc.vector.tensor_copy(ckT, ps[:, 7, 0:N_CMP]))
                        TT(rk1, ckT, ckT, ALU.mult).then_inc(cm_sq, 1)
                        dve.wait_ge(cm_rstd, 1)
                        STT(ckT, ckT, cst("gain_cmp"), rk1, ALU.mult, ALU.mult).then_inc(ckT_ready, 1)
                        dve.wait_ge(r_back, 48)
                        dve.wait_ge(*marks_pe.at("r_spread"))
                        st.done(nc.vector.tensor_copy(kn_bh, ps[:, 0, 0:4 * DH]))
                        st.done(TS(q_bh, q_bh, SCALE, None, ALU.mult))
                        for g in range(G):
                            ts = TS(q_dup[:, g * DH:(g + 1) * DH], q_bh, cst("own_group")[:, g:g + 1], None, ALU.mult)
                            st.done(ts) if g == 0 else ts.then_inc(*marks_dve.next("r_dup"))
                        for v in range(2):
                            st.done(TT(prod, q_bh, kn_bh[:, 2 * v * DH:(2 * v + 1) * DH], ALU.mult))
                            red = RED(stats[:, 6 + v:7 + v], prod, AX.X, ALU.add)
                            st.done(red) if v == 0 else red.then_inc(*marks_dve.next("r_kn"))
                        dve.wait_ge(*marks_pe.at("i_s"))
                        st.done(TT(p_imp, ps[:, 2, 0:NB * NCB], cst("cmp_own"), ALU.add))
                        RED(stats[:, 4:5], p_imp, AX.X, ALU.max, negate=True).then_inc(*marks_dve.next("i_max"))
                        dve.wait_ge(*marks_act.at("i_exp"))
                        st.done(nc.vector.reciprocal(stats[:, 5:6], stats[:, 5:6]))
                        TS(p_imp, p_imp, stats[:, 5:6], None, ALU.mult).then_inc(*marks_dve.next("i_p"))
                        dve.wait_ge(*marks_pe.at("i_sum"))
                        imp, least, hit, last, neg = pick[:, 0:16], pick[:, 16:17], pick[:, 32:48], pick[:, 17:18], pick[:, 64:80]
                        st.done(RED(imp, ps[0:NB * G, 0, 0:NB * NCB].rearrange("p (b k r) -> p k b r", b=NB, r=2), AX.XY, ALU.add))
                        st.done(TT(imp, imp, cst("forced", NB * G), ALU.add))
                        st.done(RED(least, imp, AX.X, ALU.min))
                        st.done(TS(hit, imp, least, None, ALU.is_equal))
                        st.done(TT(hit, hit, cst("block_no", NB * G), ALU.mult))
                        st.done(RED(last, hit, AX.X, ALU.max))
                        TS(neg, cst("block_no", NB * G), last, NEG, ALU.is_equal, ALU.mult).then_inc(*marks_dve.next("i_neg"))
                dve.wait_ge(cvT_ready, 1)
                pair = cvT_pair.rearrange("p (u n) -> p u n", u=2)
                st.done(nc.vector.memset(cvT_pair, 0.0))
                nc.vector.tensor_copy(pair[:, :, 0:NPB], bc(cvT[:, NB * NCB:N_CMP].unsqueeze(1), [P, 2, NPB])).then_inc(cvT_ready, 1)
                st.done(nc.vector.memset(cv_pair, 0.0))
                dve.wait_ge(cv_turned, 1)
                st.done(nc.vector.tensor_copy(cv_s, ps[:, 4, 0:2 * P]))
                for u in range(2):
                    half = slice(u * DH, (u + 1) * DH)
                    cp = nc.vector.tensor_copy(cv_pair[half].rearrange("p (g u e) -> p g u e", g=G, u=2)[:, :, u, :],
                                               ps[half, 4, 2 * P:3 * P].rearrange("p (g e) -> p g e", g=G))
                    st.done(cp) if u == 0 else cp.then_inc(cv_ready, 1)

                dve.wait_ge(*marks_pe.at("i_o"))
                nc.vector.tensor_copy(o_cmp, ps[:, 3, 0:P]).then_inc(*marks_dve.next("i_out"))
                dve.wait_ge(*marks_dve.at("i_out"))
                dve.sem_inc(sk_turned, 3)

                dve.wait_ge(cm_proj, 2)
                dve.wait_ge(kz_swapped, 1)
                for u in range(2):
                    half = slice(u * DH, (u + 1) * DH)
                    for w in range(2):
                        st.done(nc.vector.tensor_copy(Kz[half, 1 - u, u, w * SEQ:(w + 1) * SEQ], ps[half, 5 + w, :]))
                    st.done(nc.vector.tensor_copy(Kz[half, u, u, 2 * SEQ:KZ], ckT[half, NB * NCB:N_CMP]))
                    cp = nc.vector.tensor_copy(Kz[half, 1 - u, u, 2 * SEQ:KZ], ps[half, 7, 0:NPB])
                    st.done(cp)
                st.done(nc.vector.memset(small[:, 32:44], 1.0))
                nc.vector.memset(arena[:, 5184:5696], 0.0).then_inc(kz_ready, 1)
                dve.wait_ge(kz_ready, 3)

                dve.sem_inc(n_o, 2)
                dve.sem_inc(n_t, 4)
                dve.sem_inc(n_av, 4)
                dve.sem_inc(sk_T, 1)
                dve.sem_inc(sv_T, 1)
                dve.sem_inc(sk_scored, 1)
                for g in range(G):
                    if g == 1:
                        sel, win = ps[:, 0:2, :].rearrange("p a c -> p (a c)"), ps[:, 2, :]
                        dve.wait_ge(*marks_pe.at("sk_back"))
                        st.done(RED(stats[:, 8:9], sel, AX.X, ALU.max))
                        st.done(RED(stats[:, 9:10], win, AX.X, ALU.max))
                        st.done(TT(stats[:, 8:10], stats[:, 8:10], stats[:, 6:8], ALU.max))
                        st.done(TS(stats[:, 8:10], stats[:, 8:10], -1.0, None, ALU.mult))
                        TT(stats[:, 6:8], stats[:, 6:8], stats[:, 8:10], ALU.add).then_inc(*marks_dve.next("sk_max"))
                        dve.wait_ge(*marks_act.at("sk_exp"))
                        st.done(TT(stats[:, 12:14], stats[:, 12:14], stats[:, 14:16], ALU.add))
                        st.done(nc.vector.reciprocal(stats[:, 12:14], stats[:, 12:14]))
                        st.done(TT(stats[:, 1:3], stats[:, 1:3], stats[:, 12:14], ALU.mult))
                        dve.wait_ge(*marks_pe.at("sk_pturned"))
                        st.done(nc.vector.memset(arena[:, 5184:5696], 0.0))
                    with st.loop(HPG // 2, 5 + (16 - MASK_PE) + 4 * 2) as j:
                        i = j + g * (HPG // 2)


                        def sample_keys(b2, q):
                            if q < 3:
                                dve.wait_ge(sk_turned, i * 6 + (3 * b2 + q + 4))
                                dve.wait_ge(sk_scored, i * 2 + (b2 + 1))
                                cp = nc.vector.tensor_copy(KTs[q], ps[:, 3, :])
                                if q == 0:
                                    cp = nc.vector.tensor_copy(q_one, QT[:, bass.ds(i * 2 * HN + b2 * HN, HN)])
                                cp.then_inc(sk_T, 1)
                            else:
                                dve.wait_ge(sk_scored, i * 2 + (b2 + 2))
                                for w, (dst, n) in enumerate(((PT1_sel, 8), (PT1_win, 4))):
                                    cp = nc.vector.tensor_copy(dst.rearrange("p (n c) -> p n c", n=n)[:, :, bass.ds(i * 2 * HN + b2 * HN, HN)],
                                                               ps[:, 3, w * P:w * P + n * HN].rearrange("p (n c) -> p n c", n=n))
                                cp.then_inc(sk_T, 1)

                        def sample_weights(b2):
                            for dst, src, n in ((p_one[:, 0:P], PT1_sel, 8), (p_one[:, P:12 * HN], PT1_win, 4)):
                                cp = nc.vector.tensor_copy(dst.rearrange("p (n c) -> p n c", n=n),
                                                           src.rearrange("p (n c) -> p n c", n=n)[:, :, bass.ds(j * 2 * HN + b2 * HN, HN)])
                            cp.then_inc(sv_staged, 1)

                        def sample_values(b2):
                            dve.wait_ge(sv_used, j * 6 + (3 * b2 + 6))
                            nc.vector.tensor_copy(oT1[:, :, bass.ds(j * 2 * HN + b2 * HN, HN)],
                                                  ps[:, 3, 0:2 * HN].rearrange("p (w c) -> p w c", w=2)).then_inc(sv_T, 1)

                        pc = p_cmp[:, :, :, 0:NPB]
                        cs = small[:, 0:8].rearrange("p (t u) -> p t u", t=NT)

                        def cmp_max():
                            dve.wait_ge(nc_s, i + 1)
                            st.done(TT(pc, ps[:, 3, 0:P].rearrange("p (t u n) -> p t u n", t=NT, u=2),
                                       bc(cst("cmp_neg").rearrange("p (t n) -> p t n", t=NT).unsqueeze(2), [P, NT, 2, NPB]), ALU.add))
                            st.done(RED(cs, pc, AX.X, ALU.max))
                            TT(pc, pc, bc(cs.unsqueeze(3), [P, NT, 2, NPB]), ALU.subtract).then_inc(nc_max, 1)

                        def cmp_weights():
                            dve.wait_ge(nc_exp, i + 1)
                            st.done(RED(cs, pc, AX.X, ALU.add))
                            st.done(nc.vector.reciprocal(cs, cs))
                            st.done(TT(pc, pc, bc(cs.unsqueeze(3), [P, NT, 2, NPB]), ALU.mult))
                            TT(pc, pc, bc(cst("cmp_one").rearrange("p (t n) -> p t n", t=NT).unsqueeze(2), [P, NT, 2, NPB]), ALU.mult).then_inc(nc_p, 1)

                        def row_max(u):
                            t, h2, br = units[u]
                            dve.wait_ge(n_s, i * 16 + (u + 1))
                            if u >= MASK_PE:
                                st.done(TT(ps[:, u % 3, t * P:(t + 1) * P], ps[:, u % 3, t * P:(t + 1) * P], cst("causal_neg"), ALU.add))
                            RED(nmax(u), ps[:, u % 3, 0:(t + 1) * P], AX.X, ALU.max, negate=True).then_inc(n_max, 1)

                        def combine(t):
                            dve.wait_ge(n_av, i * 16 + (4 * t + 8))
                            dve.wait_ge(n_mix, i * 4 + (t + 1))
                            d, c = small[:, 32 + 6 * (t % 2):38 + 6 * (t % 2)], small[:, 48:54]
                            gates = z[:, t, bass.ds(i * 6 + BG, 6)].rearrange("p (u x) -> p x u", x=3)
                            st.done(nc.vector.reciprocal(c, d))
                            st.done(TT(c.rearrange("p (x u) -> p x u", u=2), c.rearrange("p (x u) -> p x u", u=2), gates, ALU.mult))
                            TT(o3s[:, t % 2].rearrange("p (x d) -> p x d", x=6), ps[:, 6 + t % 2, 0:3 * P].rearrange("p (x d) -> p x d", x=6),
                               bc(c.unsqueeze(2), [P, 6, DH]), ALU.mult).then_inc(n_o, 1)
                            dve.wait_ge(n_o, i * 4 + (t + 3))

                        row_max(0)
                        row_max(1)
                        row_max(2)
                        cmp_max()
                        for u in range(16):
                            if g == 0 and u - 1 in KEY_STEPS:
                                sample_keys(*KEY_STEPS[u - 1])
                            if g == 1 and u + 2 in VALUE_STEPS:
                                sample_weights(VALUE_STEPS[u + 2])
                            if g == 1 and u - 1 in VALUE_STEPS:
                                sample_values(VALUE_STEPS[u - 1])
                            if u + 3 < 16:
                                row_max(u + 3)
                            if u == 1:
                                cmp_weights()
                            if u % 4 == 1 and u > 4:
                                combine(u // 4 - 1)
                        combine(3)

                dve.wait_ge(n_mix, 2 + 4 * (HN // 2))
                own = bc(cst("own_group").unsqueeze(2), [P, G, DH])
                st.done(TT(o3[:, 0:P].rearrange("p (g e) -> p g e", g=G), o_cmp.rearrange("p (g e) -> p g e", g=G), own, ALU.mult))
                dve.wait_ge(*marks_pe.at("sv_back"))
                for w in range(2):
                    st.done(TT(o3[:, (w + 1) * P:(w + 2) * P].rearrange("p (g e) -> p g e", g=G),
                               ps[:, 2, w * P:(w + 1) * P].rearrange("p (g e) -> p g e", g=G), own, ALU.mult))
                r3 = small[:, 0:3 * DH].rearrange("p (x e) -> p x e", x=3)
                st.done(RED(r3, o3.rearrange("p (x g e) -> p x e g", x=3, g=G), AX.X, ALU.add))
                for w in range(2):
                    st.done(STT(r3[:, w + 1, :], kn_bh[:, (2 * w + 1) * DH:(2 * w + 2) * DH], stats[:, 14 + w:15 + w], r3[:, w + 1, :], ALU.mult, ALU.add))
                st.done(TS(q_bh, r3[:, 0, :], stats[:, 0:1], None, ALU.mult))
                for w in range(2):
                    add = STT(q_bh, r3[:, w + 1, :], stats[:, w + 1:w + 2], q_bh, ALU.mult, ALU.add)
                    st.done(add) if w == 0 else add.then_inc(*marks_dve.next("sv_sum"))
                dve.wait_ge(sv_row, 16)
                gate = z[0:NB, NT, GATE:BG]
                TT(gate, gate, o_row, ALU.mult).then_inc(*marks_dve.next("sv_done"))
                for u in range(2):
                    add_residual(16 + u, u)


SHAPES = {
    "x_prompt": (1, SEQ, D), "x_sample": (NB, 1, D), "state_ret": (NB, H, DH, DH),
    "cache_sb_k": (80, PAGE, H, DH), "cache_sb_v": (80, PAGE, H, DH), "page_table": (NB, NPG),
    "w_in0": (D, W0), "w_out0": (D, D), "w_in1": (D, W1), "w_out1": (D, D),
}
DIRECT = ["x_prompt", "x_sample", "state_ret", "cache_sb_k", "cache_sb_v", "cache_cmp_k", "cache_cmp_v",
          "cache_sel_k", "cache_sel_v", "cache_win_k", "cache_win_v", "page_table", "w_in0", "w_out0",
          "w_in1", "w_cmp_k", "w_cmp_v", "w_out1"]
KV = (1, SEQ, G, DH)
KVS = (NB, 1, G, DH)
WB = (NB, 512, G, DH)
OUTS = [(1, SEQ, D), (NB, 1, D), (1, H, DH, DH), (NB, H, DH, DH), (1, SEQ, H, DH), (1, SEQ, H, DH),
        (NB, 1, H, DH), (NB, 1, H, DH), KV, KV, KV, KV, KV, KV, KVS, KVS, KVS, KVS, WB, WB]


def parameters(aux, inputs):
    def put(name, a):
        lo, hi = AT[name]
        aux[:, lo:hi] = a

    for layer in (0, 1):
        put(f"gain_in{layer}", inputs[f"norm{layer}_g"].reshape(KT, P).T)
    put("gain_ret", inputs["ret_gn_g"].reshape(1, HW))
    for name, key in (("gain_sq", "sb_qn_g"), ("gain_sk", "sb_kn_g"), ("gain_q", "nsa_qn_g"),
                      ("gain_sel", "sel_kn_g"), ("gain_win", "win_kn_g")):
        put(name, inputs[key].reshape(1, DH))
    put("gain_cmp", np.concatenate([inputs["cmp_kn_g"]] * G).reshape(P, 1))
    put("pe", np.concatenate([inputs["cmp_pe"].T] * G))
    return aux


def kernel(**inputs):
    import concourse.bacc as bacc
    from concourse.bass_utils import run_bass_kernel_spmd

    inputs = {k: np.asarray(v) for k, v in inputs.items()}
    arrays = {name: np.ascontiguousarray(inputs[name]) for name in DIRECT}
    arrays["aux"] = parameters(constants(), inputs)
    nc = bacc.Bacc("TRN2", target_bir_lowering=False, num_devices=1)
    ins = {k: nc.dram_tensor(k, a.shape, mybir.dt.from_np(a.dtype), kind="ExternalInput").ap() for k, a in arrays.items()}
    outs = {f"o{i}": nc.dram_tensor(f"o{i}", s, F32, kind="ExternalOutput").ap() for i, s in enumerate(OUTS)}
    build(nc, ins, outs)
    r = run_bass_kernel_spmd(nc, [arrays], core_ids=[0])
    return tuple(r.results[0][f"o{i}"] for i in range(len(OUTS)))
```
